# Optimizing a Trainium2 kernel written in Bass

```python
import math
import jax, jax.numpy as jnp
from jax import lax
import numpy as np

D_MODEL = 2048
BATCH = 1
SEQ = 256
DEPTH = 1

CHUNK = 128
A_GROUPS = 8
A_WIDTH = 1024
A_GROUP_DIM = A_WIDTH // A_GROUPS
B_HEADS = 8
B_HEAD_DIM = 128
B_WIDTH = B_HEADS * B_HEAD_DIM
Q_BLOCK = 128
N_EXPERTS = 32
TOP_K = 4
D_EXPERT = 512
SWIGLU_LIMIT = 7.0
SWIGLU_ALPHA = 1.702
DEEPNORM_ALPHA = (2.0 * DEPTH) ** 0.25
DEEPNORM_BETA = (8.0 * DEPTH) ** -0.25
LN_EPS = 1e-5
NEG_INF = -1e30
IN_SPLITS = (A_WIDTH, 2 * A_WIDTH, 2 * A_WIDTH + B_WIDTH, 2 * A_WIDTH + 2 * B_WIDTH,
             2 * A_WIDTH + 3 * B_WIDTH, 2 * A_WIDTH + 3 * B_WIDTH + B_HEADS,
             2 * A_WIDTH + 3 * B_WIDTH + B_HEADS + D_MODEL)
IN_COLS = 2 * A_WIDTH + 3 * B_WIDTH + B_HEADS + 2 * D_MODEL

kernel_name = "hybrid_sgu_fox_moe_deepnorm_adaln"

def layer_norm(x, g, b):
    xf = x.astype(jnp.float32)
    mu = jnp.mean(xf, axis=-1, keepdims=True)
    var = jnp.mean(jnp.square(xf - mu), axis=-1, keepdims=True)
    return ((xf - mu) * lax.rsqrt(var + LN_EPS) * g + b).astype(x.dtype)

def chunked_sgu(u, v, ln_g, w_s, b_s):
    bsz, seq, _ = v.shape
    n_chunks = seq // CHUNK
    vf = v.astype(jnp.float32).reshape(bsz, n_chunks, CHUNK, A_GROUPS, A_GROUP_DIM)
    mu = jnp.mean(vf, axis=-1, keepdims=True)
    var = jnp.mean(jnp.square(vf - mu), axis=-1, keepdims=True)
    vn = (vf - mu) * lax.rsqrt(var + LN_EPS) * ln_g
    causal = jnp.tril(jnp.ones((CHUNK, CHUNK), dtype=bool))
    w = jnp.where(causal, w_s.astype(jnp.float32), 0.0)
    mixed = jnp.einsum('gts,bnsgc->bntgc', w, vn) + b_s.astype(jnp.float32).T[None, None, :, :, None]
    return u * mixed.reshape(bsz, seq, A_WIDTH).astype(u.dtype)

def forgetting_attention(q, k, v, f_logit, b_f):
    bsz, seq, _ = q.shape
    n_blocks = seq // Q_BLOCK
    qf = q.astype(jnp.float32).reshape(bsz, seq, B_HEADS, B_HEAD_DIM)
    kf = k.astype(jnp.float32).reshape(bsz, seq, B_HEADS, B_HEAD_DIM)
    vf = v.astype(jnp.float32).reshape(bsz, seq, B_HEADS, B_HEAD_DIM)
    log_f = jax.nn.log_sigmoid(f_logit.astype(jnp.float32) + b_f.astype(jnp.float32))
    cum = jnp.transpose(jnp.cumsum(log_f, axis=1), (0, 2, 1))
    q_blocks = qf.reshape(bsz, n_blocks, Q_BLOCK, B_HEADS, B_HEAD_DIM).transpose(1, 0, 2, 3, 4)
    cq_blocks = cum.reshape(bsz, B_HEADS, n_blocks, Q_BLOCK).transpose(2, 0, 1, 3)
    q_pos = jnp.arange(seq, dtype=jnp.int32).reshape(n_blocks, Q_BLOCK)
    k_pos = jnp.arange(seq, dtype=jnp.int32)
    scale = B_HEAD_DIM ** -0.5

    def one_block(args):
        q_i, cq_i, pos_i = args
        s = jnp.einsum('bqhd,bkhd->bhqk', q_i, kf) * scale
        s = s + cq_i[..., None] - cum[:, :, None, :]
        s = jnp.where(pos_i[:, None] >= k_pos[None, :], s, NEG_INF)
        p = jax.nn.softmax(s, axis=-1)
        return jnp.einsum('bhqk,bkhd->bqhd', p, vf)

    o = lax.map(one_block, (q_blocks, cq_blocks, q_pos))
    return o.transpose(1, 0, 2, 3, 4).reshape(bsz, seq, B_WIDTH).astype(q.dtype)

def hybrid_mixer(h, w_in, b_f, sgu_ln_g, spatial_w, spatial_b, w_proj_a, w_proj_b, w_o):
    z = h @ w_in
    u_a, v_a, q_b, k_b, v_b, f_b, g_a, g_b = jnp.split(z, IN_SPLITS, axis=-1)
    y_a = chunked_sgu(jax.nn.gelu(u_a), jax.nn.gelu(v_a), sgu_ln_g, spatial_w, spatial_b)
    y_b = forgetting_attention(q_b, k_b, v_b, f_b, b_f)
    merged = jax.nn.sigmoid(g_a) * (y_a @ w_proj_a) + jax.nn.sigmoid(g_b) * (y_b @ w_proj_b)
    return merged @ w_o

def moe_ffn(h, router_w, router_b, w_gate, b_gate, w_up, b_up, w_down, b_down):
    logits = (h @ router_w + router_b).astype(jnp.float32)
    top_v, top_i = lax.top_k(logits, TOP_K)
    top_w = jax.nn.softmax(top_v, axis=-1)
    combine = jnp.sum(jax.nn.one_hot(top_i, N_EXPERTS, dtype=jnp.float32) * top_w[..., None], axis=-2)
    out = jnp.zeros(h.shape, jnp.float32)
    for e in range(N_EXPERTS):
        g = jnp.minimum(h @ w_gate[e] + b_gate[e], SWIGLU_LIMIT)
        u = jnp.clip(h @ w_up[e] + b_up[e], -SWIGLU_LIMIT, SWIGLU_LIMIT)
        act = g * jax.nn.sigmoid(SWIGLU_ALPHA * g) * (u + 1.0)
        out = out + combine[..., e:e + 1] * (act @ w_down[e] + b_down[e]).astype(jnp.float32)
    return out.astype(h.dtype)

def setup_inputs(seed: int = 0) -> dict:
    key = jax.random.key(seed)
    ks = jax.random.split(key, 24)
    L, D, E, F = DEPTH, D_MODEL, N_EXPERTS, D_EXPERT

    def nrm(k, shape, scale):
        return jax.random.normal(k, shape, jnp.float32) * scale

    tril = jnp.tril(jnp.ones((CHUNK, CHUNK), jnp.float32))
    return {
        "x": nrm(ks[0], (BATCH, SEQ, D), 1.0),
        "c": nrm(ks[1], (BATCH, D), 1.0),
        "w_ada": nrm(ks[2], (L, D, 6 * D), 0.1 * D ** -0.5),
        "b_ada": nrm(ks[3], (L, 6 * D), 0.02),
        "w_in": nrm(ks[4], (L, D, IN_COLS), D ** -0.5),
        "b_f": 2.0 + nrm(ks[5], (L, B_HEADS), 0.5),
        "sgu_ln_g": 1.0 + nrm(ks[6], (L, A_GROUPS, A_GROUP_DIM), 0.02),
        "spatial_w": tril * nrm(ks[7], (L, A_GROUPS, CHUNK, CHUNK), CHUNK ** -0.5),
        "spatial_b": 1.0 + nrm(ks[8], (L, A_GROUPS, CHUNK), 0.02),
        "w_proj_a": nrm(ks[9], (L, A_WIDTH, D), A_WIDTH ** -0.5),
        "w_proj_b": nrm(ks[10], (L, B_WIDTH, D), B_WIDTH ** -0.5),
        "w_o": nrm(ks[11], (L, D, D), DEEPNORM_BETA * D ** -0.5),
        "ln1_g": 1.0 + nrm(ks[12], (L, D), 0.02),
        "ln1_b": nrm(ks[13], (L, D), 0.02),
        "router_w": nrm(ks[14], (L, D, E), D ** -0.5),
        "router_b": nrm(ks[15], (L, E), 0.01),
        "w_gate": nrm(ks[16], (L, E, D, F), D ** -0.5),
        "b_gate": nrm(ks[17], (L, E, F), 0.02),
        "w_up": nrm(ks[18], (L, E, D, F), D ** -0.5),
        "b_up": nrm(ks[19], (L, E, F), 0.02),
        "w_down": nrm(ks[20], (L, E, F, D), DEEPNORM_BETA * F ** -0.5),
        "b_down": nrm(ks[21], (L, E, D), 0.02),
        "ln2_g": 1.0 + nrm(ks[22], (L, D), 0.02),
        "ln2_b": nrm(ks[23], (L, D), 0.02),
    }

def reference(x, c, w_ada, b_ada, w_in, b_f, sgu_ln_g, spatial_w, spatial_b, w_proj_a, w_proj_b,
              w_o, ln1_g, ln1_b, router_w, router_b, w_gate, b_gate, w_up, b_up, w_down, b_down,
              ln2_g, ln2_b):
    cond = jax.nn.silu(c)
    for l in range(DEPTH):
        mod = (cond @ w_ada[l] + b_ada[l])[:, None, :]
        sh1, sc1, g1, sh2, sc2, g2 = jnp.split(mod, 6, axis=-1)
        h = x * (1.0 + sc1) + sh1
        mix = hybrid_mixer(h, w_in[l], b_f[l], sgu_ln_g[l], spatial_w[l], spatial_b[l],
                           w_proj_a[l], w_proj_b[l], w_o[l])
        x = layer_norm(DEEPNORM_ALPHA * x + (1.0 + g1) * mix, ln1_g[l], ln1_b[l])
        h = x * (1.0 + sc2) + sh2
        ffn = moe_ffn(h, router_w[l], router_b[l], w_gate[l], b_gate[l], w_up[l], b_up[l],
                      w_down[l], b_down[l])
        x = layer_norm(DEEPNORM_ALPHA * x + (1.0 + g2) * ffn, ln2_g[l], ln2_b[l])
    return x


_drawn_inputs = setup_inputs


def setup_inputs(seed=0):
    import zlib

    import numpy as np

    out = dict(_drawn_inputs(seed))
    spreads = {}
    factors = {'sgu_ln_g': 5.105,
     'spatial_b': 7.315,
     'router_b': 2.717,
     'b_gate': 8.0,
     'b_up': 8.0,
     'b_down': 6.401,
     'ln2_g': 2.831,
     'ln2_b': 2.879}
    for name, (base, spread) in spreads.items():
        noise = np.random.default_rng([zlib.crc32(name.encode()), seed]).standard_normal(out[name].shape)
        drawn = base * np.exp(spread * noise) if base else spread * noise
        out[name] = __import__('jax').numpy.asarray(drawn.astype(out[name].dtype))
    for name, factor in factors.items():
        out[name] = (out[name] * factor).astype(out[name].dtype)
    return out
```

```python
from contextlib import ExitStack

import concourse.bass as bass
from concourse import mybir

F32 = mybir.dt.float32
F32R = mybir.dt.float32r
I32 = mybir.dt.int32
U32 = mybir.dt.uint32
ALU = mybir.AluOpType
ACT = mybir.ActivationFunctionType
AX = mybir.AxisListType

P = 128
D = 2048
SEQ = 256
TB = SEQ // P
KD = D // P
AW = 1024
HEADS = 8
E = 32
TOPK = 4
FE = 512
FC = FE // P
ALPHA = 2.0 ** 0.25
EPS = 1e-5
LIMIT = 7.0
SWI = 1.702
NEG = -1e30
SCALE = P ** -0.5
COLS = 512
SLOTS = 64
MAX_PASS = SEQ // SLOTS
GA = 10
GG = 8
F_COL = GA * COLS
RAW_SLOTS = 6
SPLIT_SLOTS = 3
UNITS = 12
KPU = 4
PAIRS = E // 2
KB = 1024
U_, V_, Q_, K_, VB_ = 0, AW, 2 * AW, 3 * AW, 4 * AW
NADA1 = 2 * KD
NPROJ = D // COLS


def layer(nc, A, mod_dram, out):
    ctx = ExitStack()
    with ctx:
        def sem(name):
            return ctx.enter_context(nc.semaphore(name))

        room = 207 * KB + 512
        ctx.enter_context(nc.sbuf_tensor("arena", [P, room // 4], F32))
        base = nc.sbuf_base - room
        cursor = [0]

        def place(name, shape, dt=F32, at=None):
            size = 4
            for n in shape[1:]:
                size *= n
            size = (size + 31) // 32 * 32
            if at is None:
                at = cursor[0]
                cursor[0] += size
            assert at + size <= room, (name, at + size, room)
            return nc.alloc_sbuf_tensor_at(name, shape, dt, offset=base + at)

        raw = [place(f"raw{s}", [P, KPU, COLS]) for s in range(RAW_SLOTS)]
        x = place("x", [P, TB, D])
        ident = place("ident", [P, P])
        ones = place("ones", [P, P])
        tri_incl = place("tri_incl", [P, P])
        tri_excl = place("tri_excl", [P, P])
        twin = place("twin", [P, SLOTS])
        slot_i = place("slot_i", [P, P], I32)
        slot_id = place("slot_id", [P, P])
        expert_i = place("expert_i", [P, E], I32)
        expert_id = place("expert_id", [P, E])
        bgu = place("bgu", [P, E, 2 * FC])
        posm = place("posm", [P, TB, E + 1])
        comb = place("comb", [P, TB, E])
        st = place("st", [P, 16, 6])
        mv = place("mv", [P, 16, 2])
        rstd = place("rstd", [P, 16])
        npass_i = place("npass_i", [1, 1], I32)
        npass_f = place("npass_f", [1, 8])
        rb_row = place("rb_row", [1, E])
        phase = cursor[0]

        hT = place("hT", [P, KD, SEQ])
        zA = place("zA", [P, TB, F_COL])
        zG = place("zG", [P, TB, GG * COLS])
        acc = place("acc", [P, 4, D])
        tmp = place("tmp", [P, 2, 1536])
        condT = place("condT", [P, KD])
        bada2 = place("bada2", [64, P])
        modrow = place("modrow", [64, P])
        modcol = place("modcol", [P, 64])
        mod1 = place("mod1", [P, 2 * KD])
        badaT = place("badaT", [P, 2 * KD])
        bsT = place("bsT", [P, HEADS])
        wf = place("wf", [P, KD, HEADS])
        bf_row = place("bf_row", [1, HEADS])
        lf = place("lf", [P, TB * HEADS])
        lt = place("lt", [P, TB * HEADS])
        cum = place("cum", [P, TB * HEADS])
        mx = place("mx", [P, 2, 8])
        sums = place("sums", [P, 8])
        cT = place("cT", [P, 2, KD])
        o_hT = phase
        o_zA = o_hT + 16 * KB
        o_zG = o_zA + 40 * KB
        o_acc = o_zG + 32 * KB
        o_tmp = o_acc + 32 * KB
        o_end = o_tmp + 12 * KB
        acc1 = place("acc1", [P, 2, D], at=o_zG)
        mask3 = place("mask3", [P, 3, P])
        cumT = place("cumT", [HEADS, SEQ])
        probs = tmp[:, 1, :].rearrange("p (h c) -> p h c", h=4)
        probsT = tmp[:, 0, :].rearrange("p (h c) -> p h c", h=4)
        wsT = tmp[:, 0, 0:HEADS * P].rearrange("p (g t) -> p g t", g=HEADS)
        lng = tmp[:, 1, 0:AW]
        ws_raw = place("ws_raw", [P, HEADS, P], at=o_acc)
        c_rows = place("c_rows", [KD, P], at=o_acc + 4 * KB)
        bada_rows = place("bada_rows", [2 * KD, P], at=o_acc + 5 * KB)
        bs_rows = place("bs_rows", [HEADS, P], at=o_acc + 6 * KB)
        bg_rows = place("bg_rows", [P, P], at=o_acc + 7 * KB)
        bu_rows = place("bu_rows", [P, P], at=o_acc + 8 * KB)

        g1_row, ln1g, ln1b, sc2_row, sh2_row = [
            place(f"row_{n}", [P, D], at=o_zA + i * 8 * KB) for i, n in enumerate(["g1", "ln1g", "ln1b", "sc2", "sh2"])]
        h2 = place("h2", [P, TB, D], at=o_acc)
        h2T = place("h2T", [P, KD, SEQ], at=o_zG + 16 * KB)
        rw = place("rw", [P, KD, E], at=o_tmp)
        bdown = place("bdown", [E, D], at=o_tmp + 4 * KB)
        logit = place("logit", [P, TB, E], at=o_tmp + 2 * KB)
        mask = place("mask", [P, TB, E], at=o_tmp + 2 * KB + 256)
        onehot = place("onehot", [P, 1, E], at=o_tmp + 2 * KB + 512)
        top = place("top", [P, TB, 8], at=o_tmp + 2 * KB + 768)
        topi = place("topi", [P, TB, 8], U32, at=o_tmp + 2 * KB + 832)
        topf = place("topf", [P, TB, 8], at=o_tmp + 2 * KB + 896)
        topw = place("topw", [P, TB, 8], at=o_tmp + 2 * KB + 960)
        tops = place("tops", [P, 4], at=o_tmp + 2 * KB + 640)
        combT = place("combT", [E, SEQ], at=o_tmp + 3 * KB)
        h2hi = place("h2hi", [P, TB, D], F32R, at=o_hT)
        h2lo = place("h2lo", [P, TB, D], F32R, at=o_acc + 16 * KB)
        out_acc = place("out_acc", [P, TB, D], at=o_zA)
        hi = [place(f"hi{s}", [P, KPU, COLS], F32R, at=o_zA + (16 + 8 * s) * KB) for s in range(SPLIT_SLOTS)]
        lo = [place(f"lo{s}", [P, KPU, COLS], F32R, at=o_zG + 8 * s * KB) for s in range(2)]
        lo.append(place("lo2", [P, KPU, COLS], F32R, at=o_zG + 24 * KB))
        hsel = place("hsel", [P, KD, P], F32R, at=o_zG + 16 * KB)
        y = [place(f"y{m}", [P, D], at=o_acc + 8 * m * KB) for m in range(2)]
        act = place("act", [P, 3, FC * SLOTS], at=o_tmp)
        actR = place("actR", [P, FC, 2, SLOTS], F32R, at=o_tmp + 3 * KB)
        gu_sb = place("gu_sb", [P, 2, FE], at=o_tmp + 5 * KB)
        sel = place("sel", [P, TB, SLOTS], F32R, at=o_tmp + 9 * KB)
        selw = place("selw", [P, TB, P], at=o_tmp + 9 * KB + 512)
        selwT = [place(f"selwT{m}", [P, SEQ], at=o_tmp + 10 * KB + 512 + m * KB) for m in range(2)]
        g2_row, ln2g, ln2b = [place(f"row_{n}", [P, D], at=o_zA + (16 + 8 * i) * KB) for i, n in enumerate(["g2", "ln2g", "ln2b"])]

        bank = ctx.enter_context(nc.psum_tensor("bank", [P, 8, COLS], F32))

        c_loaded = sem("c_loaded")
        x_loaded = sem("x_loaded")
        rows_loaded = sem("rows_loaded")
        landed = [sem(f"landed{s}") for s in range(RAW_SLOTS)]
        consts_made = sem("consts_made")
        acc1_zeroed = sem("acc1_zeroed")
        acc_zeroed = sem("acc_zeroed")
        ws_masked = sem("ws_masked")
        row_lng = sem("row_lng")
        wf_loaded = sem("wf_loaded")
        v_stat = sem("v_stat")
        v_agg = sem("v_agg")
        scored = sem("scored")
        scored_max = sem("scored_max")
        gated = sem("gated")
        ffn_done = sem("ffn_done")
        experts_begun = sem("experts_begun")
        cT_done = sem("cT_done")
        sig_c = sem("sig_c")
        cond_done = sem("cond_done")
        rowsT_done = sem("rowsT_done")
        rowsT_copied = sem("rowsT_copied")
        xT_done = sem("xT_done")
        xT_copied = sem("xT_copied")
        ada1_done = sem("ada1_done")
        ada2_done = sem("ada2_done")
        ada1_cols = sem("ada1_cols")
        mod1_done = sem("mod1_done")
        h_done = sem("h_done")
        main_used = sem("main_used")
        z_copied = sem("z_copied")
        dve_step = sem("dve_step")
        act_step = sem("act_step")
        pool_step = sem("pool_step")
        v_var = sem("v_var")
        v_std = sem("v_std")
        vn_done = sem("vn_done")
        f_done = sem("f_done")
        lt_done = sem("lt_done")
        lf_done = sem("lf_done")
        qkT_done = sem("qkT_done")
        qkT_copied = sem("qkT_copied")
        sgu_done = sem("sgu_done")
        ya_done = sem("ya_done")
        cum_done = sem("cum_done")
        cum_copied = sem("cum_copied")
        scores_done = sem("scores_done")
        max_done = sem("max_done")
        exp_done = sem("exp_done")
        probs_done = sem("probs_done")
        pT_done = sem("pT_done")
        pT_copied = sem("pT_copied")
        oT_done = sem("oT_done")
        oT_copied = sem("oT_copied")
        yaT_done = sem("yaT_done")
        yaT_copied = sem("yaT_copied")
        cols2_done = sem("cols2_done")
        cols2_copied = sem("cols2_copied")
        modT_done = sem("modT_done")
        modrow_done = sem("modrow_done")
        mod_stored = sem("mod_stored")
        merged_done = sem("merged_done")
        mT_done = sem("mT_done")
        mT_copied = sem("mT_copied")
        row_in = {n: sem(f"in_{n}") for n in ("g1", "ln1g", "ln1b", "sc2", "sh2", "rw", "rb", "bdown", "g2", "ln2g", "ln2b")}
        res_done = sem("res_done")
        var1 = sem("var1")
        std1 = sem("std1")
        x1_done = sem("x1_done")
        h2_done = sem("h2_done")
        h2T_done = sem("h2T_done")
        h2T_copied = sem("h2T_copied")
        h2hi_done = sem("h2hi_done")
        h2lo_done = sem("h2lo_done")
        logit_done = sem("logit_done")
        top_done = sem("top_done")
        topw_done = sem("topw_done")
        mask_done = sem("mask_done")
        pos_done = sem("pos_done")
        npass_done = sem("npass_done")
        comb_done = sem("comb_done")
        combT_done = sem("combT_done")
        combT_copied = sem("combT_copied")
        bias_done = sem("bias_done")
        bias_copied = sem("bias_copied")
        hi_ready = sem("hi_ready")
        lo_ready = sem("lo_ready")
        unit_used = sem("unit_used")
        sel_ready = sem("sel_ready")
        selw_ready = sem("selw_ready")
        gathered = sem("gathered")
        hsel_ready = sem("hsel_ready")
        gu_copied = sem("gu_copied")
        tsum_done = sem("tsum_done")
        gate_ready = sem("gate_ready")
        sig_ready = sem("sig_ready")
        swiglu_step = sem("swiglu_step")
        act_ready = sem("act_ready")
        y_filled = sem("y_filled")
        selwT_done = sem("selwT_done")
        selwT_filled = sem("selwT_filled")
        scattered = sem("scattered")
        scatter_added = sem("scatter_added")
        pos_moved = sem("pos_moved")
        var2 = sem("var2")
        std2 = sem("std2")
        out_ready = sem("out_ready")
        out_stored = sem("out_stored")

        n_rows = 7

        def ada_unit(k, j):
            return A["w_ada"][0, bass.ts(k, P), j * D:(j + 1) * D]

        def win_unit(g, u, gates=False):
            col = g * COLS + (HEADS if gates else 0)
            return A["w_in"][0, u * COLS:(u + 1) * COLS, bass.ds(col, COLS)].rearrange("(k p) f -> p k f", p=P)

        def square_unit(w, n, u):
            return w[0, u * COLS:(u + 1) * COLS, n * COLS:(n + 1) * COLS].rearrange("(k p) f -> p k f", p=P)

        def expert_unit(e, u):
            if u < 2 * FC:
                w = A["w_gate"] if u % 2 == 0 else A["w_up"]
                r = (u // 2) * KPU * P
                return w[0, e, r:r + KPU * P, :].rearrange("(k p) f -> p k f", p=P)
            c = u - 2 * FC
            return A["w_down"][0, e, c * P:(c + 1) * P, :].rearrange("p (n f) -> p n f", n=KPU)

        def flat(slot):
            return slot[:, :, :].rearrange("p k f -> p (k f)")

        MAIN_FILLS = NADA1 // RAW_SLOTS
        ADA_FILLS = NADA1 // RAW_SLOTS + 1
        EXP_FILLS = [ADA_FILLS + 2 * KD] * 2 + [MAIN_FILLS + GA + GG + 2 * NPROJ] * 4
        GM = GA + GG

        block = ctx.enter_context(nc.Block())

        @block.sync
        def _(sp):
            def ada1_load(i, m):
                sp.dma_start(flat(raw[m]), ada_unit(3 * i + m // 2, m % 2)).then_inc(landed[m], 16)

            for m in range(RAW_SLOTS):
                ada1_load(0, m)
            with sp.Fori(1, NADA1 // RAW_SLOTS) as i:
                for m in range(RAW_SLOTS):
                    sp.wait_ge(ada1_done, i * RAW_SLOTS + m - 5)
                    ada1_load(i, m)
            for m in range(2):
                sp.wait_ge(ada1_done, NADA1 - 2 + m - 5)
                ada1_load(NADA1 // RAW_SLOTS, m)

            def mixer_loads(g, gates, ada):
                first = isinstance(g, int) and g == 0
                for u in range(4):
                    if first:
                        sp.wait_ge(ada1_done, NADA1 - RAW_SLOTS + u + 1)
                    else:
                        sp.wait_ge(main_used, 4 * g + u - 3)
                    sp.dma_start(raw[2 + u][:, :, :], win_unit(g, u, gates)).then_inc(landed[2 + u], 16)
                    if ada:
                        j = u
                        if first and j < 2:
                            sp.wait_ge(ada1_done, NADA1 - 1 + j)
                        else:
                            sp.wait_ge(ada2_done, 4 * g + j - 1)
                        sp.dma_start(flat(raw[j % 2]), ada_unit(g, 2 + j)).then_inc(landed[j % 2], 16)

            mixer_loads(0, False, True)
            with sp.Fori(1, GA) as g:
                mixer_loads(g, False, True)
            for g in range(GA, GM):
                mixer_loads(g, True, g < KD)
            for n in range(NPROJ):
                for u in range(4):
                    sp.wait_ge(main_used, 4 * (GM + n) + u - 3)
                    w = A["w_proj_a"] if u < 2 else A["w_proj_b"]
                    sp.dma_start(raw[2 + u][:, :, :], square_unit(w, n, u % 2)).then_inc(landed[2 + u], 16)
            for n in range(NPROJ):
                for u in range(4):
                    sp.wait_ge(main_used, 4 * (GM + NPROJ + n) + u - 3)
                    sp.dma_start(raw[2 + u][:, :, :], square_unit(A["w_o"], n, u)).then_inc(landed[2 + u], 16)

            def expert_load(e, u):
                s = u % RAW_SLOTS
                sp.dma_start(raw[s][:, :, :], expert_unit(e, u)).then_inc(landed[s], 16)

            sp.wait_ge(ada2_done, 4 * KD)
            for u in range(RAW_SLOTS):
                if u >= 2:
                    sp.wait_ge(main_used, 4 * (GM + 2 * NPROJ) - 4 + u - 1)
                expert_load(0, u)
            sp.wait_ge(npass_done, 1)
            npass = sp.value_load(npass_i[0:1, 0:1], min_val=1, max_val=MAX_PASS)
            with sp.Fori(0, npass) as ps:
                with sp.Fori(0, E) as e:
                    U0 = sp.snap((ps * E + e) * UNITS)
                    e_next = sp.snap(sp.to_reg((e + 1) & (E - 1)), min_val=0, max_val=E - 1)
                    for u in list(range(RAW_SLOTS, UNITS)) + list(range(RAW_SLOTS)):
                        ahead = UNITS if u < RAW_SLOTS else 0
                        sp.wait_ge(lo_ready, U0 + (ahead + u - RAW_SLOTS + 1))
                        if u == 2 * FC:
                            sp.sem_inc(experts_begun, 1)
                        expert_load(e_next if ahead else e, u)
            fills = [sp.snap(sp.to_reg(npass * (16 * E * UNITS // RAW_SLOTS) + 16 * (EXP_FILLS[s] + 1)), min_val=1, max_val=1 << 16) for s in range(RAW_SLOTS)]
            for s in range(RAW_SLOTS):
                sp.wait_ge(landed[s], fills[s])
            sp.wait_ge(ffn_done, 1)
            for name, dst, src in [("g2", g2_row, mod_dram[3 * KD:4 * KD, :].rearrange("k c -> (k c)")),
                                   ("ln2g", ln2g, A["ln2_g"][0, :]), ("ln2b", ln2b, A["ln2_b"][0, :])]:
                sp.dma_start(dst[:, :], src.partition_broadcast(P)).then_inc(row_in[name], 16)
            for tb in range(TB):
                sp.wait_ge(out_ready, tb + 1)
                sp.dma_start(out[0, tb * P:(tb + 1) * P, :], out_acc[:, tb, :]).then_inc(out_stored, 16)
            sp.wait_ge(out_stored, 16 * TB)

        @block.gpsimd
        def _(pool):
            steps = [0]

            def chain(ins):
                steps[0] += 1
                ins.then_inc(pool_step, 1)
                pool.wait_ge(pool_step, steps[0])

            def keep(t, op, base, partition, pattern, fill=0.0):
                return pool.affine_select(out=t, in_=t, compare_op=op, fill=fill, base=base, pattern=pattern,
                                          channel_multiplier=partition)

            pool.memset(acc1[:, :, :], 0.0).then_inc(acc1_zeroed, 1)
            chain(pool.memset(ident[:, :], 0.0))
            keep(ident[:, :], ALU.not_equal, 0, 1, [[-1, P]], 1.0).then_inc(consts_made, 1)
            pool.memset(ones[:, :], 1.0).then_inc(consts_made, 1)
            chain(pool.memset(tri_incl[:, :], 1.0))
            keep(tri_incl[:, :], ALU.is_ge, 0, -1, [[1, P]]).then_inc(consts_made, 1)
            chain(pool.memset(tri_excl[:, :], 1.0))
            keep(tri_excl[:, :], ALU.is_gt, 0, -1, [[1, P]]).then_inc(consts_made, 1)
            chain(pool.memset(twin[:, :], 0.0))
            chain(keep(twin[:, :], ALU.not_equal, 0, 1, [[-1, SLOTS]], 1.0))
            keep(twin[:, :], ALU.not_equal, -SLOTS, 1, [[-1, SLOTS]], 1.0).then_inc(consts_made, 1)
            chain(pool.iota(slot_i[:, :], pattern=[[0, 2], [1, SLOTS]], base=0, channel_multiplier=0))
            pool.tensor_copy(slot_id[:, :], slot_i[:, :]).then_inc(consts_made, 1)
            chain(pool.iota(expert_i[:, :], pattern=[[1, E]], base=0, channel_multiplier=0))
            pool.tensor_copy(expert_id[:, :], expert_i[:, :]).then_inc(consts_made, 1)
            chain(pool.memset(mask3[:, :, :], 0.0))
            for b in (0, 2):
                keep(mask3[:, b, :], ALU.is_ge, 0, 1, [[-1, P]], NEG).then_inc(consts_made, 1)

            pool.wait_ge(rowsT_done, 1)
            for j in range(4):
                pool.memset(acc[:, j, :], 0.0).then_inc(acc_zeroed, 1)
            pool.wait_ge(rowsT_copied, 3)
            for g in range(HEADS):
                keep(wsT[:, g, :], ALU.is_ge, 0, -1, [[1, P]]).then_inc(ws_masked, 1)

            pool.wait_ge(modrow_done, 1)
            pool.dma_start(mod_dram[:, :], modrow[:, :]).then_inc(mod_stored, 16)
            pool.wait_ge(mod_stored, 16)
            pool.wait_ge(main_used, 4 * (GM + NPROJ))
            for name, dst, src in [("g1", g1_row, mod_dram[0:KD, :].rearrange("k c -> (k c)")),
                                   ("ln1g", ln1g, A["ln1_g"][0, :]), ("ln1b", ln1b, A["ln1_b"][0, :]),
                                   ("sc2", sc2_row, mod_dram[2 * KD:3 * KD, :].rearrange("k c -> (k c)")),
                                   ("sh2", sh2_row, mod_dram[KD:2 * KD, :].rearrange("k c -> (k c)"))]:
                pool.dma_start(dst[:, :], src.partition_broadcast(P)).then_inc(row_in[name], 16)
            pool.dma_start(rw[:, :, :], A["router_w"][0].rearrange("(k p) e -> p k e", p=P)).then_inc(row_in["rw"], 16)
            pool.dma_start(rb_row[:, :], A["router_b"][0:1, :]).then_inc(row_in["rb"], 16)
            pool.dma_start(bdown[:, :], A["b_down"][0]).then_inc(row_in["bdown"], 16)

            pool.wait_ge(h2lo_done, TB)
            for m in range(2):
                for half in range(2):
                    pool.memset(y[m][:, half * 1024:(half + 1) * 1024], 0.0).then_inc(y_filled, 1)
            pool.wait_ge(bias_done, 8)
            for m in range(2):
                pool.memset(selwT[m][:, :], 0.0).then_inc(selwT_filled, 1)

        @block.tensor
        def _(pe):
            def T(dst, src, rows=P):
                return pe.transpose(dst, src, ident[0:rows, 0:rows])

            pe.wait_ge(consts_made, 1)
            pe.wait_ge(c_loaded, 16)
            T(bank[:, 0, 0:KD], c_rows[:, :], KD).then_inc(cT_done, 1)
            pe.wait_ge(rows_loaded, 16 * n_rows)
            T(bank[:, 1, 0:2 * KD], bada_rows[:, :], 2 * KD)
            T(bank[:, 1, 32:32 + HEADS], bs_rows[:, :], HEADS)
            T(bank[:, 1, P:2 * P], bg_rows[:, :])
            T(bank[:, 1, 2 * P:3 * P], bu_rows[:, :])
            for g in range(HEADS):
                last = T(bank[:, 2 + g // 4, (g % 4) * P:(g % 4 + 1) * P], ws_raw[:, g, :])
            last.then_inc(rowsT_done, 1)
            pe.wait_ge(x_loaded, 16)
            for b in range(8):
                if b == 4:
                    pe.wait_ge(sig_c, 1)
                    pe.wait_ge(rowsT_copied, 3)
                for i in range(4):
                    k, tb = 2 * b + i // 2, i % 2
                    last = T(bank[:, (4 + b) % 8, i * P:(i + 1) * P], x[:, tb, k * P:(k + 1) * P])
                last.then_inc(xT_done, 1)

            pe.wait_ge(consts_made, 2)
            pe.wait_ge(xT_copied, 8)
            pe.wait_ge(ada1_done, NADA1)
            for j in range(2):
                for k in range(KD):
                    last = pe.matmul(bank[:, 0, j * KD + k:j * KD + k + 1], acc1[:, j, k * P:(k + 1) * P], ones[:, 0:1],
                                     start=True, stop=True)
            last.then_inc(ada1_cols, 1)

            def main_unit(G, u):
                pe.wait_ge(landed[2 + u], (G + MAIN_FILLS + 1) * 16)

            def group(G, lhsT, banks):
                for u in range(4):
                    main_unit(G, u)
                    if isinstance(G, int) and G == 0:
                        pe.wait_ge(h_done, 4 * (u + 1))
                    for tb in range(TB):
                        for kk in range(KPU):
                            last = pe.matmul(bank[:, banks[tb], :], lhsT[:, u * KPU + kk, tb * P:(tb + 1) * P],
                                             raw[2 + u][:, kk, :], start=(u == 0 and kk == 0),
                                             stop=(u == 3 and kk == KPU - 1))
                    last.then_inc(main_used, 1)

            def win_group(G, parity):
                if not (isinstance(G, int) and G < 2):
                    pe.wait_ge(z_copied, G * 2 - 2)
                group(G, hT, [2 * parity, 2 * parity + 1])

            pe.wait_ge(mod1_done, 1)
            for G in range(2):
                win_group(G, G)
            with pe.Fori(1, GA // 2) as i:
                for parity in range(2):
                    win_group(i * 2 + parity, parity)

            pe.wait_ge(wf_loaded, 16)
            for tb in range(TB):
                for k in range(KD):
                    pe.matmul(bank[:, 4, tb * HEADS:(tb + 1) * HEADS], hT[:, k, tb * P:(tb + 1) * P], wf[:, k, :],
                              start=(k == 0), stop=False)
                last = pe.matmul(bank[:, 4, tb * HEADS:(tb + 1) * HEADS], ones[0:1, :], bf_row[:, :], start=False, stop=True)
            last.then_inc(f_done, 1)

            def qkT(half):
                for h in range(4 * half, 4 * half + 4):
                    b = 4 + h % 4
                    if h == 0:
                        pe.wait_ge(z_copied, 2 * GA)
                        pe.wait_ge(lt_done, 1)
                        pe.wait_ge(lf_done, 1)
                    if h >= 4:
                        pe.wait_ge(qkT_copied, 2 * (h - 4) + 2)
                    for i, off in enumerate((Q_, Q_, K_, K_)):
                        last = T(bank[:, b, i * P:(i + 1) * P], zA[:, i % 2, off + h * P:off + (h + 1) * P])
                    last.then_inc(qkT_done, 1)

            def sgu():
                pe.wait_ge(vn_done, 2 * TB)
                pe.wait_ge(ws_masked, HEADS)
                pe.wait_ge(qkT_copied, 2 * HEADS)
                for g in range(HEADS):
                    pe.matmul(bank[:, 4 + g // 2, (g % 2) * SEQ:(g % 2 + 1) * SEQ], wsT[:, g, :],
                              zA[:, 0:TB, V_ + g * P:V_ + (g + 1) * P], start=True, stop=True).then_inc(sgu_done, 1)

            def cumulate():
                pe.wait_ge(ya_done, HEADS)
                pe.wait_ge(lf_done, 2)
                l0, l1 = lf[:, 0:HEADS], lf[:, HEADS:2 * HEADS]
                pe.matmul(bank[:, 4, 0:HEADS], tri_incl[:, :], l0, start=True, stop=True)
                pe.matmul(bank[:, 4, HEADS:2 * HEADS], ones[:, :], l0, start=True, stop=False)
                pe.matmul(bank[:, 4, HEADS:2 * HEADS], tri_incl[:, :], l1, start=False, stop=True)
                pe.matmul(bank[0:HEADS, 5, 0:P], l0, tri_incl[:, :], start=True, stop=True)
                pe.matmul(bank[0:HEADS, 5, P:SEQ], l0, ones[:, :], start=True, stop=False)
                pe.matmul(bank[0:HEADS, 5, P:SEQ], l1, tri_incl[:, :], start=False, stop=True).then_inc(cum_done, 1)

            def scores(half):
                pe.wait_ge(cum_copied, 2)
                if half:
                    pe.wait_ge(oT_copied, 4)
                for hh in range(4):
                    h = 4 * half + hh
                    for tb in range(TB):
                        o = bank[:, 4 + hh, tb * P:tb * P + (tb + 1) * P]
                        pe.matmul(o, zA[:, tb, Q_ + h * P:Q_ + (h + 1) * P], zA[:, 0:tb + 1, K_ + h * P:K_ + (h + 1) * P],
                                  start=True, stop=False)
                        last = pe.matmul(o, ident[0:HEADS, h:h + 1].to_broadcast([HEADS, P]), cumT[:, 0:(tb + 1) * P],
                                         start=False, stop=True)
                    last.then_inc(scores_done, 1)

            def probsT_of(half):
                for hh in range(4):
                    pe.wait_ge(probs_done, 4 * half + hh + 1)
                    for b in range(3):
                        last = T(bank[:, 4 + hh, b * P:(b + 1) * P], probs[:, hh, b * P:(b + 1) * P])
                    last.then_inc(pT_done, 1)

            def oT(half):
                for hh in range(4):
                    h = 4 * half + hh
                    pe.wait_ge(pT_copied, h + 1)
                    pe.matmul(bank[:, 4 + hh, 0:SEQ], zA[:, 0, VB_ + h * P:VB_ + (h + 1) * P], probsT[:, hh, 0:SEQ],
                              start=True, stop=False)
                    pe.matmul(bank[:, 4 + hh, P:SEQ], zA[:, 1, VB_ + h * P:VB_ + (h + 1) * P], probsT[:, hh, SEQ:3 * P],
                              start=False, stop=True).then_inc(oT_done, 1)

            def yaT():
                pe.wait_ge(z_copied, 2 * GM)
                for b in range(4):
                    for i in range(4):
                        tb, c = i // 2, 2 * b + i % 2
                        last = T(bank[:, b, i * P:(i + 1) * P], zA[:, tb, U_ + c * P:U_ + (c + 1) * P])
                    last.then_inc(yaT_done, 1)

            after = {10: [lambda: qkT(0)], 11: [lambda: qkT(1)], 12: [sgu], 13: [cumulate], 14: [lambda: scores(0)],
                     15: [lambda: probsT_of(0)], 16: [lambda: oT(0), lambda: scores(1)],
                     17: [lambda: probsT_of(1), yaT, lambda: oT(1)]}
            for G in range(GA, GM):
                win_group(G, G % 2)
                for stage in after[G]:
                    stage()

            pe.wait_ge(oT_copied, 8)
            pe.wait_ge(ada2_done, 4 * KD)
            for j in range(4):
                for k in range(KD):
                    last = pe.matmul(bank[:, 7, j * KD + k:j * KD + k + 1], acc[:, j, k * P:(k + 1) * P], ones[:, 0:1],
                                     start=True, stop=True)
            last.then_inc(cols2_done, 1)

            def project(n):
                s = 4 * (n % 2)
                if n == 0:
                    pe.wait_ge(yaT_copied, 4)
                if n == 1:
                    pe.wait_ge(modrow_done, 1)
                if n >= 2:
                    pe.wait_ge(mT_copied, 2 * (n - 1))
                for u in range(4):
                    main_unit(GM + n, u)
                    off = V_ if u < 2 else Q_
                    for tb in range(TB):
                        for kk in range(KPU):
                            c = (u % 2) * KPU + kk
                            last = pe.matmul(bank[:, s + 2 * (u // 2) + tb, :], zA[:, tb, off + c * P:off + (c + 1) * P],
                                             raw[2 + u][:, kk, :], start=(c == 0), stop=(c == 7))
                    last.then_inc(main_used, 1)

            def mergedT(n):
                s = 4 * (n % 2)
                pe.wait_ge(merged_done, 2 * (n + 1))
                for b in range(2):
                    for i in range(4):
                        k, tb = 2 * b + i // 2, i % 2
                        last = T(bank[:, s + b, i * P:(i + 1) * P], zG[:, tb, n * COLS + k * P:n * COLS + (k + 1) * P])
                    last.then_inc(mT_done, 1)

            for n in range(NPROJ):
                project(n)
                if n == 0:
                    pe.wait_ge(cols2_copied, 1)
                    T(bank[0:4 * KD, 6, 0:P], modcol[:, :]).then_inc(modT_done, 1)
                if n:
                    mergedT(n - 1)
            mergedT(NPROJ - 1)

            for n in range(NPROJ):
                if n == 0:
                    pe.wait_ge(mT_copied, 2 * NPROJ)
                if n >= 2:
                    pe.wait_ge(res_done, 2 * (n - 1))
                group(GM + NPROJ + n, hT, [2 * (n % 2), 2 * (n % 2) + 1])

            for b in range(8):
                if b == 0:
                    pe.wait_ge(res_done, 2 * NPROJ)
                pe.wait_ge(h2_done, 2)
                for i in range(4):
                    k, tb = 2 * b + i // 2, i % 2
                    last = T(bank[:, b, i * P:(i + 1) * P], h2[:, tb, k * P:(k + 1) * P])
                last.then_inc(h2T_done, 1)
            pe.wait_ge(h2T_copied, 8)
            pe.wait_ge(row_in["rw"], 16)
            pe.wait_ge(row_in["rb"], 16)
            for tb in range(TB):
                for k in range(KD):
                    pe.matmul(bank[:, 0, tb * E:(tb + 1) * E], h2T[:, k, tb * P:(tb + 1) * P], rw[:, k, :],
                              start=(k == 0), stop=False)
                last = pe.matmul(bank[:, 0, tb * E:(tb + 1) * E], ones[0:1, :], rb_row[:, :], start=False, stop=True)
            last.then_inc(logit_done, 1)
            pe.wait_ge(mask_done, 2)
            pe.matmul(bank[:, 1, 0:E], tri_excl[:, :], mask[:, 0, :], start=True, stop=True)
            pe.matmul(bank[:, 1, E:2 * E], ones[:, :], mask[:, 0, :], start=True, stop=False)
            pe.matmul(bank[:, 1, E:2 * E], tri_excl[:, :], mask[:, 1, :], start=False, stop=True)
            pe.matmul(bank[:, 1, 2 * E:3 * E], ones[:, :], mask[:, 0, :], start=True, stop=False)
            pe.matmul(bank[:, 1, 2 * E:3 * E], ones[:, :], mask[:, 1, :], start=False, stop=True).then_inc(pos_done, 1)
            pe.wait_ge(comb_done, 2)
            for tb in range(TB):
                last = T(bank[0:E, 2, tb * P:(tb + 1) * P], comb[:, tb, :])
            last.then_inc(combT_done, 1)

            def gather(X, first=False):
                pe.wait_ge(sel_ready, X + 1)
                if not first:
                    pe.wait_ge(y_filled, X * 4)
                for c in range(KD):
                    for part, src in ((0, h2hi), (1, h2lo)):
                        o = bank[:, 2 + c // 4, (c % 4) * P + part * SLOTS:(c % 4) * P + (part + 1) * SLOTS]
                        for tb in range(TB):
                            last = pe.matmul(o, src[:, tb, c * P:(c + 1) * P], sel[:, tb, :], start=(tb == 0), stop=(tb == 1))
                    if c % 4 == 3:
                        last.then_inc(gathered, 1)

            def scatter(X, j0, wait_bank):
                pe.wait_ge(y_filled, X * 4 + 4)
                pe.wait_ge(selwT_filled, X + 2)
                for i in range(8):
                    tb, n = i // 4, i % 4
                    if i >= 2:
                        pe.wait_ge(scatter_added, j0 + (i - 1))
                    o = bank[:, 7 if i % 2 == 0 else 0, :]
                    pe.matmul(o, selwT[0][:, tb * P:(tb + 1) * P], y[0][:, n * COLS:(n + 1) * COLS], start=True, stop=False)
                    pe.matmul(o, selwT[1][:, tb * P:(tb + 1) * P], y[1][:, n * COLS:(n + 1) * COLS],
                              start=False, stop=True).then_inc(scattered, 1)

            pe.wait_ge(combT_copied, 1)
            pe.wait_ge(row_in["bdown"], 16)
            for i in range(8):
                tb, n = i // 4, i % 4
                if i >= 2:
                    pe.wait_ge(bias_copied, i - 1)
                pe.matmul(bank[:, 7 if i % 2 == 0 else 0, :], combT[:, tb * P:(tb + 1) * P],
                          bdown[:, n * COLS:(n + 1) * COLS], start=True, stop=True).then_inc(bias_done, 1)
            pe.wait_ge(h2lo_done, TB)
            gather(0, first=True)
            pe.wait_ge(bias_copied, 8)
            pe.wait_ge(npass_done, 1)
            npass = pe.value_load(npass_i[0:1, 0:1], min_val=1, max_val=MAX_PASS)
            with pe.Fori(0, npass) as ps:
                with pe.Fori(0, PAIRS) as q:
                    pair = ps * PAIRS + q
                    for m in range(2):
                        X = pair * 2 + m
                        U0 = pair * (2 * UNITS) + m * UNITS
                        for u in range(2 * FC):
                            pe.wait_ge(hsel_ready, X * 4 + (u // 2 + 1))
                            pe.wait_ge(lo_ready, U0 + (u + 1))
                            for kk in range(KPU):
                                for part in (hi, lo):
                                    last = pe.matmul(bank[:, u % 2, :], hsel[:, (u // 2) * KPU + kk, :], part[u % SPLIT_SLOTS][:, kk, :],
                                                     start=(u < 2 and kk == 0 and part is hi),
                                                     stop=(u >= 6 and kk == KPU - 1 and part is lo))
                            last.then_inc(unit_used, 1)
                        gather(X + 1)
                        pe.wait_ge(gu_copied, X * 2 + 2)
                        for c in range(2 * FC):
                            last = pe.matmul(bank[:, 6, c * SLOTS:(c + 1) * SLOTS], gu_sb[:, c // FC, (c % FC) * P:(c % FC + 1) * P],
                                             twin[:, :], start=True, stop=True)
                        last.then_inc(tsum_done, 1)
                        if m == 0:
                            scatter(X, pair * 8, True)
                            pe.wait_ge(scatter_added, pair * 8 + 8)
                        else:
                            pe.wait_ge(selwT_filled, X + 2)
                        pe.wait_ge(selw_ready, X + 1)
                        for tb in range(TB):
                            last = T(bank[:, 7, tb * P:(tb + 1) * P], selw[:, tb, :])
                        last.then_inc(selwT_done, 1)
                        pe.wait_ge(act_ready, X + 1)
                        pe.wait_ge(hsel_ready, X * 4 + 8)
                        for c in range(FC):
                            u = 2 * FC + c
                            pe.wait_ge(lo_ready, U0 + (u + 1))
                            for n in range(4):
                                for part in (hi, lo):
                                    last = pe.matmul(bank[:, 2 + n, :], actR[:, c, :, :].rearrange("p a s -> p (a s)"),
                                                     part[u % SPLIT_SLOTS][:, n, :], start=(c == 0 and part is hi),
                                                     stop=(c == FC - 1 and part is lo))
                            last.then_inc(unit_used, 1)
            scatter(npass * E, npass * (4 * E), False)

        @block.scalar
        def _(act_):
            def copy(dst, src, **k):
                return act_.activation(dst, src, ACT.Copy, **k)

            act_.dma_start(c_rows[:, :], A["c"][0, :].rearrange("(k p) -> k p", p=P)).then_inc(c_loaded, 16)
            for dst, src in ((bada_rows[:, :], A["b_ada"][0, 0:2 * D].rearrange("(k p) -> k p", p=P)),
                             (bs_rows[:, :], A["spatial_b"][0]),
                             (bg_rows[:, :], A["b_gate"][0].rearrange("e (c p) -> (e c) p", p=P)),
                             (bu_rows[:, :], A["b_up"][0].rearrange("e (c p) -> (e c) p", p=P)),
                             (ws_raw[:, :, :], A["spatial_w"][0].rearrange("g t s -> t g s")),
                             (bf_row[:, :], A["b_f"][0:1, :]),
                             (bada2[:, :], A["b_ada"][0, 2 * D:6 * D].rearrange("(k p) -> k p", p=P))):
                act_.dma_start(dst, src).then_inc(rows_loaded, 16)
            act_.dma_start(x[:, :, :], A["x"][0].rearrange("(t p) d -> p t d", p=P)).then_inc(x_loaded, 16)
            act_.dma_start(lng, A["sgu_ln_g"][0].rearrange("g c -> (g c)").partition_broadcast(P)).then_inc(row_lng, 16)
            act_.dma_start(wf[:, :, :], A["w_in"][0, :, F_COL:F_COL + HEADS].rearrange("(k p) f -> p k f", p=P)).then_inc(wf_loaded, 16)

            act_.wait_ge(cT_done, 1)
            copy(cT[:, 0, :], bank[:, 0, 0:KD]).then_inc(sig_c, 1)
            act_.activation(cT[:, 1, :], bank[:, 0, 0:KD], ACT.Sigmoid).then_inc(sig_c, 1)
            act_.wait_ge(rowsT_done, 1)
            copy(wsT[:, 0:4, :], bank[:, 2, :]).then_inc(rowsT_copied, 1)
            copy(wsT[:, 4:8, :], bank[:, 3, :]).then_inc(rowsT_copied, 1)
            copy(badaT[:, :], bank[:, 1, 0:2 * KD])
            copy(bsT[:, :], bank[:, 1, 32:32 + HEADS])
            copy(bgu[:, :, 0:FC], bank[:, 1, P:2 * P].rearrange("p (e c) -> p e c", e=E))
            copy(bgu[:, :, FC:2 * FC], bank[:, 1, 2 * P:3 * P].rearrange("p (e c) -> p e c", e=E)).then_inc(rowsT_copied, 1)
            for b in range(8):
                act_.wait_ge(xT_done, b + 1)
                copy(hT[:, 2 * b:2 * b + 2, :], bank[:, (4 + b) % 8, :]).then_inc(xT_copied, 1)

            def z_out(G, parity, dst, func):
                act_.wait_ge(main_used, G * 4 + 4)
                for tb in range(TB):
                    act_.activation(dst(tb), bank[:, 2 * parity + tb, :], func).then_inc(z_copied, 1)

            def zA_cols(G):
                return lambda tb: zA[:, tb, bass.ds(G * COLS, COLS)]

            with act_.Fori(0, 2) as i:
                for parity in range(2):
                    G = i * 2 + parity
                    z_out(G, parity, zA_cols(G), ACT.Gelu_apprx_tanh)
            for G in range(4, 6):
                z_out(G, G % 2, zA_cols(G), ACT.Copy)
            act_.wait_ge(v_var, 1)
            act_.activation(rstd[:, :], mv[:, :, 1], ACT.Sqrt).then_inc(v_std, 1)
            with act_.Fori(3, 5) as i:
                for parity in range(2):
                    G = i * 2 + parity
                    z_out(G, parity, zA_cols(G), ACT.Copy)

            act_.wait_ge(f_done, 1)
            act_.activation(lt[:, :], bank[:, 4, 0:2 * HEADS], ACT.Abs).then_inc(act_step, 1)
            act_.wait_ge(act_step, 1)
            act_.activation(lt[:, :], lt[:, :], ACT.Exp, scale=-1.0).then_inc(act_step, 1)
            act_.wait_ge(act_step, 2)
            act_.activation(lt[:, :], lt[:, :], ACT.Ln, bias=1.0).then_inc(lt_done, 1)

            def gate_out(G):
                z_out(G, G % 2, lambda tb: zG[:, tb, (G - GA) * COLS:(G - GA + 1) * COLS], ACT.Sigmoid)

            def qkT_out(half):
                for h in range(4 * half, 4 * half + 4):
                    act_.wait_ge(qkT_done, h + 1)
                    copy(zA[:, 0:TB, Q_ + h * P:Q_ + (h + 1) * P], bank[:, 4 + h % 4, 0:SEQ].rearrange("p (t c) -> p t c", t=TB),
                         scale=SCALE).then_inc(qkT_copied, 1)
                    copy(zA[:, 0:TB, K_ + h * P:K_ + (h + 1) * P], bank[:, 4 + h % 4, SEQ:2 * SEQ].rearrange("p (t c) -> p t c", t=TB)
                         ).then_inc(qkT_copied, 1)

            def cum_out():
                act_.wait_ge(cum_done, 1)
                copy(cum[:, :], bank[:, 4, 0:2 * HEADS]).then_inc(cum_copied, 1)
                copy(cumT[:, :], bank[0:HEADS, 5, 0:SEQ], scale=-1.0).then_inc(cum_copied, 1)

            def exps(half):
                act_.wait_ge(max_done, half + 1)
                for hh in range(4):
                    act_.activation(probs[:, hh, 0:P], probs[:, hh, 0:P], ACT.Exp, bias=mx[:, 1, 2 * hh:2 * hh + 1],
                                    accum_out=sums[:, 2 * hh:2 * hh + 1]).then_inc(exp_done, 1)
                    act_.activation(probs[:, hh, P:3 * P], probs[:, hh, P:3 * P], ACT.Exp, bias=mx[:, 1, 2 * hh + 1:2 * hh + 2],
                                    accum_out=sums[:, 2 * hh + 1:2 * hh + 2]).then_inc(exp_done, 1)

            def pT_out(half):
                for hh in range(4):
                    act_.wait_ge(pT_done, 4 * half + hh + 1)
                    copy(probsT[:, hh, :], bank[:, 4 + hh, 0:3 * P]).then_inc(pT_copied, 1)

            def oT_out(half):
                for h in range(4 * half, 4 * half + 4):
                    act_.wait_ge(oT_done, h + 1)
                    copy(zA[:, 0:TB, Q_ + h * P:Q_ + (h + 1) * P],
                         bank[:, 4 + h % 4, 0:SEQ].rearrange("p (t c) -> p t c", t=TB)).then_inc(oT_copied, 1)

            def yaT_out():
                for b in range(4):
                    act_.wait_ge(yaT_done, b + 1)
                    copy(zA[:, 0:TB, V_ + 2 * b * P:V_ + 2 * (b + 1) * P],
                         bank[:, b, :].rearrange("p (t c) -> p t c", t=TB)).then_inc(yaT_copied, 1)

            gate_out(10)
            qkT_out(0)
            gate_out(11)
            qkT_out(1)
            gate_out(12)
            gate_out(13)
            cum_out()
            gate_out(14)
            exps(0)
            gate_out(15)
            pT_out(0)
            gate_out(16)
            oT_out(0)
            exps(1)
            gate_out(17)
            pT_out(1)
            yaT_out()
            oT_out(1)
            act_.wait_ge(cols2_done, 1)
            copy(modcol[:, :], bank[:, 7, 0:4 * KD]).then_inc(cols2_copied, 1)
            for n in range(NPROJ):
                for b in range(2):
                    act_.wait_ge(mT_done, 2 * n + b + 1)
                    copy(hT[:, 4 * n + 2 * b:4 * n + 2 * b + 2, :], bank[:, 4 * (n % 2) + b, :]).then_inc(mT_copied, 1)
            for tb in range(TB):
                act_.wait_ge(var1, tb + 1)
                act_.activation(rstd[:, tb:tb + 1], mv[:, tb, 1:2], ACT.Sqrt).then_inc(std1, 1)
            for b in range(8):
                act_.wait_ge(h2T_done, b + 1)
                copy(h2T[:, 2 * b:2 * b + 2, :], bank[:, b, :]).then_inc(h2T_copied, 1)
            act_.wait_ge(mT_done, 2 * NPROJ)
            act_.wait_ge(main_used, 4 * (GM + 2 * NPROJ))
            for tb in range(TB):
                copy(h2hi[:, tb, :], h2[:, tb, :]).then_inc(h2hi_done, 1)
            for tb in range(TB):
                act_.wait_ge(top_done, tb + 1)
                act_.activation(topw[:, tb, 0:TOPK], top[:, tb, 0:TOPK], ACT.Exp, bias=tops[:, tb:tb + 1],
                                accum_out=tops[:, 2 + tb:3 + tb]).then_inc(topw_done, 1)
            act_.wait_ge(combT_done, 1)
            copy(combT[:, :], bank[0:E, 2, 0:SEQ]).then_inc(combT_copied, 1)

            def split(U, u, e_free=True):
                if e_free:
                    act_.wait_ge(unit_used, U - (SPLIT_SLOTS - 1))
                copy(hi[u % SPLIT_SLOTS][:, :, :], raw[u % RAW_SLOTS][:, :, :]).then_inc(hi_ready, 1)

            def hsel_out(X):
                for b in range(4):
                    act_.wait_ge(gathered, X * 4 + (b + 1))
                    copy(hsel[:, 4 * b:4 * b + 4, :], bank[:, 2 + b, :]).then_inc(hsel_ready, 1)

            act_.wait_ge(h2_done, 2)
            for u in range(SPLIT_SLOTS):
                act_.wait_ge(landed[u], 16 * (EXP_FILLS[u] + 1))
                split(u, u, False)
            hsel_out(0)
            act_.wait_ge(npass_done, 1)
            npass = act_.value_load(npass_i[0:1, 0:1], min_val=1, max_val=MAX_PASS)
            with act_.Fori(0, npass) as ps:
                with act_.Fori(0, PAIRS) as q:
                    pair = ps * PAIRS + q
                    for m in range(2):
                        X = pair * 2 + m
                        U0 = pair * (2 * UNITS) + m * UNITS

                        def unit(u):
                            s = u % RAW_SLOTS
                            act_.wait_ge(landed[s], (pair * 4 + (2 * m + u // RAW_SLOTS + EXP_FILLS[s] + 1)) * 16)
                            split(U0 + u, u)

                        for u in range(3, 10):
                            unit(u)
                        act_.wait_ge(unit_used, U0 + 2 * FC)
                        for i in range(2):
                            copy(gu_sb[:, i, :], bank[:, i, :]).then_inc(gu_copied, 1)
                        hsel_out(X + 1)
                        unit(10)
                        act_.wait_ge(gate_ready, X + 1)
                        act_.activation(act[:, 2, :], act[:, 0, :], ACT.Sigmoid, scale=SWI).then_inc(sig_ready, 1)
                        act_.wait_ge(selwT_done, X + 1)
                        copy(selwT[m][:, :], bank[:, 7, 0:SEQ]).then_inc(selwT_filled, 1)
                        for u in range(11, 15):
                            unit(u)
                        act_.wait_ge(unit_used, U0 + UNITS)
                        for n in range(4):
                            copy(y[m][:, n * COLS:(n + 1) * COLS], bank[:, 2 + n, :]).then_inc(y_filled, 1)
            for tb in range(TB):
                act_.wait_ge(var2, tb + 1)
                act_.activation(rstd[:, tb:tb + 1], mv[:, tb, 1:2], ACT.Sqrt).then_inc(std2, 1)

        @block.vector
        def _(dve):
            steps = [0]

            def chain(ins):
                steps[0] += 1
                ins.then_inc(dve_step, 1)
                dve.wait_ge(dve_step, steps[0])

            dve.wait_ge(sig_c, 2)
            chain(dve.tensor_tensor(condT[:, :], cT[:, 0, :], cT[:, 1, :], ALU.mult))
            dve.wait_ge(acc1_zeroed, 1)

            def add_unit(dst, slot, k, done):
                return dve.scalar_tensor_tensor(out=dst, in0=flat(slot), scalar=condT[:, k], in1=dst,
                                                op0=ALU.mult, op1=ALU.add).then_inc(done, 1)

            def ada1(i, m):
                n = i * RAW_SLOTS + m
                if not (isinstance(n, int) and n < 2):
                    dve.wait_ge(ada1_done, n - 1)
                dve.wait_ge(landed[m], (i + 1) * 16)
                add_unit(acc1[:, m % 2, :], raw[m], bass.ds(i * 3 + m // 2, 1), ada1_done)

            for m in range(RAW_SLOTS):
                ada1(0, m)
            with dve.Fori(1, NADA1 // RAW_SLOTS) as i:
                for m in range(RAW_SLOTS):
                    ada1(i, m)
            for m in range(2):
                ada1(NADA1 // RAW_SLOTS, m)
            dve.wait_ge(ada1_cols, 1)
            dve.wait_ge(rowsT_copied, 3)
            dve.tensor_tensor(mod1[:, 0:KD], bank[:, 0, 0:KD], badaT[:, 0:KD], ALU.add).then_inc(mod1_done, 1)
            dve.scalar_tensor_tensor(out=mod1[:, KD:2 * KD], in0=bank[:, 0, KD:2 * KD], scalar=1.0, in1=badaT[:, KD:2 * KD],
                                     op0=ALU.add, op1=ALU.add).then_inc(mod1_done, 1)
            dve.wait_ge(mod1_done, 2)
            dve.wait_ge(xT_copied, 8)
            for k in range(KD):
                dve.tensor_scalar(hT[:, k, :], hT[:, k, :], mod1[:, KD + k:KD + k + 1], mod1[:, k:k + 1],
                                  ALU.mult, ALU.add).then_inc(h_done, 1)

            def ada2(k):
                for j in range(4):
                    if not (isinstance(k, int) and k == 0):
                        dve.wait_ge(ada2_done, k * 4 + j - 3)
                    dve.wait_ge(landed[j % 2], (k * 2 + j // 2 + ADA_FILLS + 1) * 16)
                    add_unit(acc[:, j, :], raw[j % 2], bass.ds(k, 1), ada2_done)

            dve.wait_ge(acc_zeroed, 4)
            ada2(0)
            with dve.Fori(1, 5) as k:
                ada2(k)

            dve.wait_ge(z_copied, 8)
            for tb in range(TB):
                for g in range(HEADS):
                    dve.bn_stats(st[:, tb * HEADS + g, :], zA[:, tb, V_ + g * P:V_ + (g + 1) * P]).then_inc(v_stat, 1)
            for i in range(TB * HEADS):
                dve.wait_ge(v_stat, i + 1)
                dve.bn_aggr(mv[:, i, :], st[:, i, :]).then_inc(v_agg, 1)
            dve.wait_ge(v_agg, TB * HEADS)
            dve.tensor_scalar(mv[:, :, 1], mv[:, :, 1], EPS, None, ALU.add).then_inc(v_var, 1)
            with dve.Fori(5, 8) as k:
                ada2(k)
            dve.wait_ge(v_std, 1)
            chain(dve.reciprocal(rstd[:, :], rstd[:, :]))
            for tb in range(TB):
                for g in range(HEADS):
                    v = zA[:, tb, V_ + g * P:V_ + (g + 1) * P]
                    i = tb * HEADS + g
                    ins = dve.tensor_scalar(v, v, mv[:, i, 0:1], rstd[:, i:i + 1], ALU.subtract, ALU.mult)
                ins.then_inc(vn_done, 1)
            for tb in range(TB):
                if tb == 0:
                    dve.wait_ge(row_lng, 16)
                dve.wait_ge(vn_done, TB)
                v = zA[:, tb, V_:V_ + AW]
                dve.tensor_tensor(v, v, lng, ALU.mult).then_inc(vn_done, 1)
            with dve.Fori(8, 10) as k:
                ada2(k)

            dve.wait_ge(lt_done, 1)
            chain(dve.tensor_scalar(lf[:, :], bank[:, 4, 0:2 * HEADS], 0.0, None, ALU.min))
            dve.tensor_tensor(lf[:, :], lf[:, :], lt[:, :], ALU.subtract).then_inc(lf_done, 2)

            def gate_u():
                for g in range(HEADS):
                    dve.wait_ge(sgu_done, g + 1 if g % 2 else g + 2)
                    u = zA[:, 0:TB, U_ + g * P:U_ + (g + 1) * P]
                    dve.scalar_tensor_tensor(out=u, in0=bank[:, 4 + g // 2, (g % 2) * SEQ:(g % 2 + 1) * SEQ].rearrange("p (t c) -> p t c", t=TB),
                                             scalar=bsT[:, g:g + 1], in1=u, op0=ALU.add, op1=ALU.mult).then_inc(ya_done, 1)

            def maxima(half):
                if half:
                    dve.wait_ge(pT_done, 4)
                for hh in range(4):
                    h = 4 * half + hh
                    dve.wait_ge(scores_done, h + 1)
                    dve.scalar_tensor_tensor(out=probs[:, hh, 0:P], in0=bank[:, 4 + hh, 0:P], scalar=cum[:, h:h + 1],
                                             in1=mask3[:, 0, :], op0=ALU.add, op1=ALU.add).then_inc(scored, 1)
                    dve.scalar_tensor_tensor(out=probs[:, hh, P:3 * P], in0=bank[:, 4 + hh, P:3 * P], scalar=cum[:, HEADS + h:HEADS + h + 1],
                                             in1=mask3[:, 1:3, :].rearrange("p b c -> p (b c)"), op0=ALU.add, op1=ALU.add).then_inc(scored, 1)
                for hh in range(4):
                    dve.wait_ge(scored, 8 * half + 2 * hh + 2)
                    dve.tensor_reduce(mx[:, 0, 2 * hh:2 * hh + 1], probs[:, hh, 0:P], AX.X, ALU.max).then_inc(scored_max, 1)
                    dve.tensor_reduce(mx[:, 0, 2 * hh + 1:2 * hh + 2], probs[:, hh, P:3 * P], AX.X, ALU.max).then_inc(scored_max, 1)
                dve.wait_ge(scored_max, 8 * half + 8)
                dve.tensor_scalar(mx[:, 1, :], mx[:, 0, :], -1.0, None, ALU.mult).then_inc(max_done, 1)

            def normalise(half):
                dve.wait_ge(exp_done, 8 * (half + 1))
                chain(dve.reciprocal(sums[:, :], sums[:, :]))
                for hh in range(4):
                    dve.tensor_scalar(probs[:, hh, 0:P], probs[:, hh, 0:P], sums[:, 2 * hh:2 * hh + 1], None, ALU.mult)
                    dve.tensor_scalar(probs[:, hh, P:3 * P], probs[:, hh, P:3 * P], sums[:, 2 * hh + 1:2 * hh + 2], None,
                                      ALU.mult).then_inc(probs_done, 1)

            ada2(10)
            ada2(11)
            ada2(12)
            gate_u()
            ada2(13)
            ada2(14)
            dve.wait_ge(cum_copied, 2)
            maxima(0)
            ada2(15)
            normalise(0)
            maxima(1)
            normalise(1)

            dve.wait_ge(modT_done, 1)
            dve.tensor_tensor(modrow[:, :], bank[0:4 * KD, 6, 0:P], bada2[:, :], ALU.add).then_inc(modrow_done, 1)

            for n in range(NPROJ):
                dve.wait_ge(main_used, 4 * (GM + n + 1))
                for tb in range(TB):
                    ga = zG[:, tb, n * COLS:(n + 1) * COLS]
                    gb = zG[:, tb, D + n * COLS:D + (n + 1) * COLS]
                    dve.tensor_tensor(ga, bank[:, 4 * (n % 2) + tb, :], ga, ALU.mult).then_inc(gated, 1)
                    dve.tensor_tensor(gb, bank[:, 4 * (n % 2) + 2 + tb, :], gb, ALU.mult).then_inc(gated, 1)
                for tb in range(TB):
                    ga = zG[:, tb, n * COLS:(n + 1) * COLS]
                    gb = zG[:, tb, D + n * COLS:D + (n + 1) * COLS]
                    dve.wait_ge(gated, 4 * n + 2 * tb + 2)
                    dve.tensor_tensor(ga, ga, gb, ALU.add).then_inc(merged_done, 1)

            dve.wait_ge(row_in["g1"], 16)
            for n in range(NPROJ):
                dve.wait_ge(main_used, 4 * (GM + NPROJ + n + 1))
                for tb in range(TB):
                    t = zG[:, tb, D + n * COLS:D + (n + 1) * COLS]
                    cols = slice(n * COLS, (n + 1) * COLS)
                    chain(dve.scalar_tensor_tensor(out=t, in0=g1_row[:, cols], scalar=1.0, in1=bank[:, 2 * (n % 2) + tb, :],
                                                   op0=ALU.add, op1=ALU.mult))
                    dve.scalar_tensor_tensor(out=x[:, tb, cols], in0=x[:, tb, cols], scalar=ALPHA, in1=t,
                                             op0=ALU.mult, op1=ALU.add).then_inc(res_done, 1)

            def norm_stats(t, tb, var):
                for i in range(4):
                    ins = dve.bn_stats(st[:, 4 * tb + i, :], t[:, tb, i * COLS:(i + 1) * COLS])
                chain(ins)
                chain(dve.bn_aggr(mv[:, tb, :], st[:, 4 * tb:4 * tb + 4, :].rearrange("p a b -> p (a b)")))
                dve.tensor_scalar(mv[:, tb, 1:2], mv[:, tb, 1:2], EPS, None, ALU.add).then_inc(var, 1)

            def norm_apply(t, tb, std, gain, bias):
                dve.wait_ge(std, tb + 1)
                row = t[:, tb, :]
                chain(dve.reciprocal(rstd[:, tb:tb + 1], rstd[:, tb:tb + 1]))
                chain(dve.tensor_scalar(row, row, mv[:, tb, 0:1], rstd[:, tb:tb + 1], ALU.subtract, ALU.mult))
                chain(dve.tensor_tensor(row, row, gain[:, :], ALU.mult))
                return dve.tensor_tensor(row, row, bias[:, :], ALU.add)

            dve.wait_ge(res_done, 2 * NPROJ)
            for tb in range(TB):
                norm_stats(x, tb, var1)
            dve.wait_ge(cols2_done, 1)
            for tb in range(TB):
                for name in ("ln1g", "ln1b", "sc2", "sh2"):
                    dve.wait_ge(row_in[name], 16)
                chain(norm_apply(x, tb, std1, ln1g, ln1b))
                chain(dve.scalar_tensor_tensor(out=h2[:, tb, :], in0=sc2_row[:, :], scalar=1.0, in1=x[:, tb, :],
                                               op0=ALU.add, op1=ALU.mult))
                dve.tensor_tensor(h2[:, tb, :], h2[:, tb, :], sh2_row[:, :], ALU.add).then_inc(h2_done, 1)
            for tb in range(TB):
                dve.wait_ge(h2hi_done, tb + 1)
                dve.tensor_tensor(h2lo[:, tb, :], h2[:, tb, :], h2hi[:, tb, :].bitcast(F32), ALU.subtract).then_inc(h2lo_done, 1)

            dve.wait_ge(logit_done, 1)
            chain(dve.tensor_copy(logit[:, :, :], bank[:, 0, 0:2 * E].rearrange("p (t e) -> p t e", t=TB)))
            for tb in range(TB):
                chain(dve.max(top[:, tb, :], logit[:, tb, :]))
                chain(dve.max_index(topi[:, tb, :], top[:, tb, :], logit[:, tb, :]))
                chain(dve.tensor_copy(topf[:, tb, :], topi[:, tb, :]))
                dve.tensor_scalar(tops[:, tb:tb + 1], top[:, tb, 0:1], -1.0, None, ALU.mult).then_inc(top_done, 1)
                dve.wait_ge(topw_done, tb + 1)
                chain(dve.reciprocal(tops[:, 2 + tb:3 + tb], tops[:, 2 + tb:3 + tb]))
                chain(dve.tensor_scalar(topw[:, tb, 0:TOPK], topw[:, tb, 0:TOPK], tops[:, 2 + tb:3 + tb], None, ALU.mult))
                for i in range(TOPK):
                    hot = expert_id[:, :], topf[:, tb, i:i + 1]
                    if i == 0:
                        chain(dve.tensor_scalar(mask[:, tb, :], *hot, None, ALU.is_equal))
                        chain(dve.tensor_scalar(comb[:, tb, :], *hot, topw[:, tb, 0:1], ALU.is_equal, ALU.mult))
                    else:
                        chain(dve.tensor_scalar(onehot[:, 0, :], *hot, None, ALU.is_equal))
                        chain(dve.tensor_tensor(mask[:, tb, :], mask[:, tb, :], onehot[:, 0, :], ALU.add))
                        chain(dve.scalar_tensor_tensor(out=comb[:, tb, :], in0=onehot[:, 0, :], scalar=topw[:, tb, i:i + 1],
                                                       in1=comb[:, tb, :], op0=ALU.mult, op1=ALU.add))
                dve.sem_inc(mask_done, 1)
                dve.sem_inc(comb_done, 1)
            dve.wait_ge(pos_done, 1)
            for tb in range(TB):
                chain(dve.scalar_tensor_tensor(out=posm[:, tb, 0:E], in0=bank[:, 1, tb * E:(tb + 1) * E], scalar=1.0,
                                               in1=mask[:, tb, :], op0=ALU.add, op1=ALU.mult))
                chain(dve.tensor_scalar(posm[:, tb, 0:E], posm[:, tb, 0:E], -1.0, None, ALU.add))
                chain(dve.tensor_scalar(posm[:, tb, E:E + 1], posm[:, tb, 0:1], -float(SLOTS), None, ALU.add))
            chain(dve.tensor_reduce(npass_f[:, 0:1], bank[0:1, 1, 2 * E:3 * E], AX.X, ALU.max))
            for i in range(1, MAX_PASS):
                chain(dve.tensor_scalar(npass_f[:, i:i + 1], npass_f[:, 0:1], float(SLOTS * i), None, ALU.is_gt))
            chain(dve.tensor_reduce(npass_f[:, 4:5], npass_f[:, 1:MAX_PASS], AX.X, ALU.add))
            dve.tensor_scalar(npass_i[:, :], npass_f[:, 4:5], 1.0, None, ALU.add).then_inc(npass_done, 1)

            for i in range(8):
                dve.wait_ge(bias_done, i + 1)
                tb, n = i // 4, i % 4
                dve.tensor_copy(out_acc[:, tb, n * COLS:(n + 1) * COLS], bank[:, 7 if i % 2 == 0 else 0, :]).then_inc(bias_copied, 1)

            def lo_part(U, u):
                dve.wait_ge(hi_ready, U + 1)
                s, r = u % SPLIT_SLOTS, u % RAW_SLOTS
                dve.tensor_tensor(lo[s][:, :, :], raw[r][:, :, :], hi[s][:, :, :].bitcast(F32), ALU.subtract).then_inc(lo_ready, 1)

            def select(dst, width, idx, weight=None):
                for tb in range(TB):
                    pos = posm[:, tb, bass.ds(idx, 1)]
                    if weight is None:
                        ins = dve.tensor_scalar(dst[:, tb, :], slot_id[:, 0:width], pos, None, ALU.is_equal)
                    else:
                        ins = dve.tensor_scalar(dst[:, tb, :], slot_id[:, 0:width], pos, comb[:, tb, bass.ds(idx, 1)],
                                                ALU.is_equal, ALU.mult)
                return ins

            def add_back(j0):
                for i in range(8):
                    tb, n = i // 4, i % 4
                    dve.wait_ge(scattered, j0 + (i + 1))
                    o = out_acc[:, tb, n * COLS:(n + 1) * COLS]
                    dve.tensor_tensor(o, o, bank[:, 7 if i % 2 == 0 else 0, :], ALU.add).then_inc(scatter_added, 1)

            dve.wait_ge(consts_made, 9)
            dve.wait_ge(bias_copied, 8)
            select(sel, SLOTS, 0).then_inc(sel_ready, 1)
            dve.wait_ge(h2T_copied, 8)
            dve.wait_ge(logit_done, 1)
            for u in range(SPLIT_SLOTS):
                lo_part(u, u)
            npass = dve.value_load(npass_i[0:1, 0:1], min_val=1, max_val=MAX_PASS)
            with dve.Fori(0, npass) as ps:
                with dve.Fori(0, PAIRS) as q:
                    pair = ps * PAIRS + q
                    for m in range(2):
                        X = pair * 2 + m
                        U0 = pair * (2 * UNITS) + m * UNITS
                        e = q * 2 + m
                        dve.wait_ge(gathered, X * 4 + 4)
                        select(sel, SLOTS, e + 1).then_inc(sel_ready, 1)
                        dve.wait_ge(selwT_filled, X + 2)
                        select(selw, P, e, True).then_inc(selw_ready, 1)
                        for u in range(3, 10):
                            lo_part(U0 + u, u)

                        c0 = X * 5
                        gu = act[:, 0:2, :]
                        dve.wait_ge(tsum_done, X + 1)
                        bias = bgu[:, bass.ds(e, 1), :].rearrange("p a c -> p (a c)").unsqueeze(2).to_broadcast([P, 2 * FC, SLOTS])
                        dve.tensor_tensor(gu.rearrange("p a (c s) -> p (a c) s", s=SLOTS),
                                          bank[:, 6, :].rearrange("p (c s) -> p c s", s=SLOTS), bias, ALU.add).then_inc(swiglu_step, 1)
                        dve.wait_ge(swiglu_step, c0 + 1)
                        dve.tensor_scalar(act[:, 0, :], act[:, 0, :], LIMIT, None, ALU.min).then_inc(gate_ready, 1)
                        dve.tensor_scalar(act[:, 1, :], act[:, 1, :], LIMIT, -LIMIT, ALU.min, ALU.max).then_inc(swiglu_step, 1)
                        dve.wait_ge(gate_ready, X + 1)
                        dve.wait_ge(swiglu_step, c0 + 2)
                        dve.scalar_tensor_tensor(out=act[:, 1, :], in0=act[:, 1, :], scalar=1.0, in1=act[:, 0, :],
                                                 op0=ALU.add, op1=ALU.mult).then_inc(swiglu_step, 1)
                        dve.wait_ge(sig_ready, X + 1)
                        dve.wait_ge(swiglu_step, c0 + 3)
                        dve.tensor_tensor(act[:, 1, :], act[:, 1, :], act[:, 2, :], ALU.mult).then_inc(swiglu_step, 1)
                        dve.wait_ge(swiglu_step, c0 + 4)
                        a = act[:, 1, :].rearrange("p (c s) -> p c s", s=SLOTS)
                        dve.tensor_copy(actR[:, :, 0, :], a).then_inc(swiglu_step, 1)
                        dve.wait_ge(swiglu_step, c0 + 5)
                        dve.tensor_tensor(actR[:, :, 1, :], a, actR[:, :, 0, :].bitcast(F32), ALU.subtract).then_inc(act_ready, 1)
                        if m == 0:
                            add_back(pair * 8)
                        for u in range(10, 15):
                            lo_part(U0 + u, u)
                dve.wait_ge(sel_ready, (ps + 1) * E + 1)
                dve.wait_ge(selw_ready, (ps + 1) * E)
                dve.tensor_scalar(posm[:, :, :], posm[:, :, :], -float(SLOTS), None, ALU.add).then_inc(pos_moved, 1)
                dve.wait_ge(pos_moved, ps + 1)
            add_back(npass * (4 * E))

            dve.wait_ge(scatter_added, npass * (4 * E) + 8)
            dve.sem_inc(ffn_done, 1)
            for name in ("g2", "ln2g", "ln2b"):
                dve.wait_ge(row_in[name], 16)
            for tb in range(TB):
                o = out_acc[:, tb, :]
                chain(dve.scalar_tensor_tensor(out=o, in0=g2_row[:, :], scalar=1.0, in1=o, op0=ALU.add, op1=ALU.mult))
                chain(dve.scalar_tensor_tensor(out=o, in0=x[:, tb, :], scalar=ALPHA, in1=o, op0=ALU.mult, op1=ALU.add))
                norm_stats(out_acc, tb, var2)
            for tb in range(TB):
                norm_apply(out_acc, tb, std2, ln2g, ln2b).then_inc(out_ready, 1)


_INS = ['x', 'c', 'w_ada', 'b_ada', 'w_in', 'b_f', 'sgu_ln_g', 'spatial_w', 'spatial_b', 'w_proj_a', 'w_proj_b', 'w_o',
        'ln1_g', 'ln1_b', 'router_w', 'router_b', 'w_gate', 'b_gate', 'w_up', 'b_up', 'w_down', 'b_down', 'ln2_g', 'ln2_b']


def kernel(**inputs):
    import numpy as np
    import concourse.bacc as bacc
    from concourse.bass_utils import run_bass_kernel_spmd

    nc = bacc.Bacc("TRN2", target_bir_lowering=False, num_devices=1)
    arrays, args = {}, {}
    for name in _INS:
        a = np.ascontiguousarray(inputs[name])
        arrays[f"in_{name}"] = a
        args[name] = nc.dram_tensor(f"in_{name}", a.shape, mybir.dt.from_np(a.dtype), kind="ExternalInput").ap()
    out = nc.dram_tensor("out_0", (1, SEQ, D), F32, kind="ExternalOutput").ap()
    mod_dram = nc.dram_tensor("mod_rows", (4 * KD, P), F32).ap()
    layer(nc, args, mod_dram, out)
    r = run_bass_kernel_spmd(nc, [arrays], core_ids=[0])
    return r.results[0]["out_0"]
```

```python
from contextlib import ExitStack

import concourse.bass as bass
from concourse import mybir

F32 = mybir.dt.float32
F32R = mybir.dt.float32r
I32 = mybir.dt.int32
U32 = mybir.dt.uint32
ALU = mybir.AluOpType
ACT = mybir.ActivationFunctionType
AX = mybir.AxisListType

P = 128
D = 2048
SEQ = 256
TB = SEQ // P
KD = D // P
AW = 1024
HEADS = 8
E = 32
TOPK = 4
FE = 512
FC = FE // P
ALPHA = 2.0 ** 0.25
EPS = 1e-5
LIMIT = 7.0
SWI = 1.702
NEG = -1e30
SCALE = P ** -0.5
COLS = 512
SLOTS = 64
OVER = SEQ // SLOTS - 1
EXTRA = 16
TASKS = E + EXTRA
GA = 10
GG = 8
F_COL = GA * COLS
RAW_SLOTS = 6
EXP_SLOTS = 8
HI_SLOTS = 4
LO_SLOTS = 2
GU = 8
KPU = 4
PAIRS = E // 2
KB = 1024
U_, V_, Q_, K_, VB_ = 0, AW, 2 * AW, 3 * AW, 4 * AW
NADA1 = 2 * KD
NPROJ = D // COLS


def layer(nc, A, mod_dram, out):
    ctx = ExitStack()
    with ctx:
        def sem(name):
            return ctx.enter_context(nc.semaphore(name))

        room = 207 * KB + 512
        ctx.enter_context(nc.sbuf_tensor("arena", [P, room // 4], F32))
        base = nc.sbuf_base - room
        cursor = [0]

        def place(name, shape, dt=F32, at=None):
            size = 4
            for n in shape[1:]:
                size *= n
            size = (size + 31) // 32 * 32
            if at is None:
                at = cursor[0]
                cursor[0] += size
            assert at + size <= room, (name, at + size, room)
            return nc.alloc_sbuf_tensor_at(name, shape, dt, offset=base + at)

        raw = [place(f"raw{s}", [P, KPU, COLS]) for s in range(RAW_SLOTS)]
        x = place("x", [P, TB, D])
        ident = place("ident", [P, P])
        ones = place("ones", [P, P])
        tri_incl = place("tri_incl", [P, P])
        tri_excl = place("tri_excl", [P, P])
        twin = place("twin", [P, SLOTS])
        slot_i = place("slot_i", [P, SLOTS], I32)
        slot_id = place("slot_id", [P, SLOTS])
        expert_i = place("expert_i", [P, E], I32)
        expert_id = place("expert_id", [P, E])
        bgu = place("bgu", [P, E, 2 * FC])
        pos1 = place("pos1", [P, TB, TASKS])
        comb = place("comb", [P, TB, TASKS])
        st = place("st", [P, 16, 6])
        mv = place("mv", [P, 16, 2])
        rstd = place("rstd", [P, 16])
        expert96_i = place("expert96_i", [OVER * E, 1], I32)
        expert96 = place("expert96", [OVER * E, 1])
        least96 = place("least96", [OVER * E, 1])
        task_i = place("task_i", [1, TASKS], I32)
        turns_i = place("turns_i", [1, 1], I32)
        turns_f = place("turns_f", [1, 1])
        rb_row = place("rb_row", [1, E])
        phase = cursor[0]

        hT = place("hT", [P, KD, SEQ])
        zA = place("zA", [P, TB, F_COL])
        zG = place("zG", [P, TB, GG * COLS])
        acc = place("acc", [P, 4, D])
        tmp = place("tmp", [P, 2, 1536])
        condT = place("condT", [P, KD])
        bada2 = place("bada2", [64, P])
        modrow = place("modrow", [64, P])
        modcol = place("modcol", [P, 64])
        mod1 = place("mod1", [P, 2 * KD])
        badaT = place("badaT", [P, 2 * KD])
        bsT = place("bsT", [P, HEADS])
        wf = place("wf", [P, KD, HEADS])
        bf_row = place("bf_row", [1, HEADS])
        lf = place("lf", [P, TB * HEADS])
        lt = place("lt", [P, TB * HEADS])
        cum = place("cum", [P, TB * HEADS])
        mx = place("mx", [P, 2, 8])
        sums = place("sums", [P, 8])
        cT = place("cT", [P, 2, KD])
        o_hT = phase
        o_zA = o_hT + 16 * KB
        o_zG = o_zA + 40 * KB
        o_acc = o_zG + 32 * KB
        o_tmp = o_acc + 32 * KB
        o_end = o_tmp + 12 * KB
        acc1 = place("acc1", [P, 2, D], at=o_zG)
        mask3 = place("mask3", [P, 3, P])
        cumT = place("cumT", [HEADS, SEQ])
        probs = tmp[:, 1, :].rearrange("p (h c) -> p h c", h=4)
        probsT = tmp[:, 0, :].rearrange("p (h c) -> p h c", h=4)
        wsT = tmp[:, 0, 0:HEADS * P].rearrange("p (g t) -> p g t", g=HEADS)
        lng = tmp[:, 1, 0:AW]
        ws_raw = place("ws_raw", [P, HEADS, P], at=o_acc)
        c_rows = place("c_rows", [KD, P], at=o_acc + 4 * KB)
        bada_rows = place("bada_rows", [2 * KD, P], at=o_acc + 5 * KB)
        bs_rows = place("bs_rows", [HEADS, P], at=o_acc + 6 * KB)
        bg_rows = place("bg_rows", [P, P], at=o_acc + 7 * KB)
        bu_rows = place("bu_rows", [P, P], at=o_acc + 8 * KB)

        g1_row, ln1g, ln1b, sc2_row, sh2_row = [
            place(f"row_{n}", [P, D], at=o_zA + i * 8 * KB) for i, n in enumerate(["g1", "ln1g", "ln1b", "sc2", "sh2"])]
        h2 = place("h2", [P, TB, D], at=o_acc)
        h2T = place("h2T", [P, KD, SEQ], at=o_zG + 16 * KB)
        rw = place("rw", [P, KD, E], at=o_tmp)
        bdown = place("bdown", [E, D], at=o_tmp + 4 * KB)
        logit = place("logit", [P, TB, E], at=o_tmp + 2 * KB)
        mask = place("mask", [P, TB, E], at=o_tmp + 2 * KB + 256)
        onehot = place("onehot", [P, E], at=o_tmp + 2 * KB + 512)
        tops = place("tops", [P, 4], at=o_tmp + 2 * KB + 640)
        top = place("top", [P, TB, 8], at=o_tmp + 2 * KB + 768)
        topi = place("topi", [P, TB, 8], U32, at=o_tmp + 2 * KB + 832)
        topf = place("topf", [P, TB, 8], at=o_tmp + 2 * KB + 896)
        topw = place("topw", [P, TB, 8], at=o_tmp + 2 * KB + 960)
        combT = place("combT", [E, SEQ], at=o_tmp + 3 * KB)
        N96 = OVER * E
        o_over = o_acc + 8 * KB
        pc96 = place("pc96", [P, 2 * TB, N96], at=o_over)
        mask96 = place("mask96", [P, TB, N96], at=o_over + 2 * KB)
        pc96T = place("pc96T", [N96, 2 * SEQ], at=o_over + 3 * KB)
        flag96 = place("flag96", [N96, 1], at=o_over + 5 * KB)
        rank96 = place("rank96", [N96, 1], at=o_over + 5 * KB + 32)
        place96 = place("place96", [N96, EXTRA], at=o_over + 5 * KB + 64)
        n_over = place("n_over", [1, 1], at=o_over + 5 * KB + 128)
        halves = place("halves", [1, EXTRA // 2], at=o_over + 5 * KB + 160)

        h2hi = place("h2hi", [P, TB, D], F32R, at=o_hT)
        out_acc = place("out_acc", [P, TB, D], at=o_hT + 16 * KB)
        hi = [place(f"hi{s}", [P, KPU, COLS], F32R, at=o_hT + (32 + 8 * s) * KB) for s in range(HI_SLOTS)]
        lo = [place(f"lo{s}", [P, KPU, COLS], F32R, at=o_hT + (64 + 8 * s) * KB) for s in range(LO_SLOTS)]
        raw += [place(f"raw{6 + s}", [P, KPU, COLS], at=o_hT + (80 + 8 * s) * KB) for s in range(2)]
        y = place("y", [P, D], at=o_hT + 96 * KB)
        h2lo = place("h2lo", [P, TB, D], F32R, at=o_hT + 104 * KB)
        hsel = place("hsel", [P, KD, P], F32R, at=o_hT + 120 * KB)
        gu_sb = place("gu_sb", [P, 2, FE], at=o_hT + 128 * KB)
        gate_up_T = gu_sb[:, 0, :]
        act = [place(f"act{m}", [P, FC * SLOTS], at=o_hT + (132 + m) * KB) for m in range(2)]
        sel = place("sel", [P, TB, SLOTS], F32R, at=o_hT + 134 * KB)
        selw = place("selw", [P, TB, P], at=o_hT + 134 * KB + 512)
        selwT = place("selwT", [P, SEQ], at=o_hT + 135 * KB + 512)
        g2_row, ln2g, ln2b = [place(f"row_{n}", [P, D], at=o_hT + (32 + 8 * i) * KB) for i, n in enumerate(["g2", "ln2g", "ln2b"])]

        bank = ctx.enter_context(nc.psum_tensor("bank", [P, 8, COLS], F32))

        c_loaded = sem("c_loaded")
        x_loaded = sem("x_loaded")
        rows_loaded = sem("rows_loaded")
        landed = [sem(f"landed{s}") for s in range(EXP_SLOTS)]
        consts_made = sem("consts_made")
        acc1_zeroed = sem("acc1_zeroed")
        acc_zeroed = sem("acc_zeroed")
        ws_masked = sem("ws_masked")
        row_lng = sem("row_lng")
        wf_loaded = sem("wf_loaded")
        v_stat = sem("v_stat")
        v_agg = sem("v_agg")
        scored = sem("scored")
        scored_max = sem("scored_max")
        gated = sem("gated")
        loads_begun = sem("loads_begun")
        cT_done = sem("cT_done")
        sig_c = sem("sig_c")
        cond_done = sem("cond_done")
        rowsT_done = sem("rowsT_done")
        rowsT_copied = sem("rowsT_copied")
        xT_done = sem("xT_done")
        xT_copied = sem("xT_copied")
        ada1_done = sem("ada1_done")
        ada2_done = sem("ada2_done")
        ada1_cols = sem("ada1_cols")
        mod1_done = sem("mod1_done")
        h_done = sem("h_done")
        main_used = sem("main_used")
        z_copied = sem("z_copied")
        dve_step = sem("dve_step")
        act_step = sem("act_step")
        pool_step = sem("pool_step")
        v_var = sem("v_var")
        v_std = sem("v_std")
        vn_done = sem("vn_done")
        f_done = sem("f_done")
        lt_done = sem("lt_done")
        lf_done = sem("lf_done")
        qkT_done = sem("qkT_done")
        qkT_copied = sem("qkT_copied")
        sgu_done = sem("sgu_done")
        ya_done = sem("ya_done")
        cum_done = sem("cum_done")
        cum_copied = sem("cum_copied")
        scores_done = sem("scores_done")
        max_done = sem("max_done")
        exp_done = sem("exp_done")
        probs_done = sem("probs_done")
        pT_done = sem("pT_done")
        pT_copied = sem("pT_copied")
        oT_done = sem("oT_done")
        oT_copied = sem("oT_copied")
        yaT_done = sem("yaT_done")
        yaT_copied = sem("yaT_copied")
        cols2_done = sem("cols2_done")
        cols2_copied = sem("cols2_copied")
        modT_done = sem("modT_done")
        modrow_done = sem("modrow_done")
        mod_stored = sem("mod_stored")
        merged_done = sem("merged_done")
        mT_done = sem("mT_done")
        mT_copied = sem("mT_copied")
        row_in = {n: sem(f"in_{n}") for n in ("g1", "ln1g", "ln1b", "sc2", "sh2", "rw", "rb", "bdown", "g2", "ln2g", "ln2b")}
        res_done = sem("res_done")
        var1 = sem("var1")
        std1 = sem("std1")
        x1_done = sem("x1_done")
        h2_done = sem("h2_done")
        h2T_done = sem("h2T_done")
        h2T_copied = sem("h2T_copied")
        h2hi_done = sem("h2hi_done")
        h2lo_done = sem("h2lo_done")
        logit_done = sem("logit_done")
        top_done = sem("top_done")
        topw_done = sem("topw_done")
        mask_done = sem("mask_done")
        pos_done = sem("pos_done")
        comb_done = sem("comb_done")
        combT_done = sem("combT_done")
        combT_copied = sem("combT_copied")
        bias_done = sem("bias_done")
        bias_copied = sem("bias_copied")
        over_masked = sem("over_masked")
        over_counted = sem("over_counted")
        over_flagged = sem("over_flagged")
        over_ranked = sem("over_ranked")
        over_placed = sem("over_placed")
        over_tabled = sem("over_tabled")
        over_turned = sem("over_turned")
        over_copied = sem("over_copied")
        over_spread = sem("over_spread")
        tables_done = sem("tables_done")
        hi_ready = sem("hi_ready")
        lo_ready = sem("lo_ready")
        unit_used = sem("unit_used")
        down_used = sem("down_used")
        sel_ready = sem("sel_ready")
        gathered = sem("gathered")
        hsel_act = sem("hsel_act")
        hsel_dve = sem("hsel_dve")
        gu_copied = sem("gu_copied")
        tsum_done = sem("tsum_done")
        biased = sem("biased")
        gate_ready = sem("gate_ready")
        up_ready = sem("up_ready")
        gate_up = sem("gate_up")
        sig_ready = sem("sig_ready")
        act_ready = sem("act_ready")
        y_filled = sem("y_filled")
        selw_ready = sem("selw_ready")
        selwT_done = sem("selwT_done")
        selwT_filled = sem("selwT_filled")
        scattered = sem("scattered")
        scatter_added = sem("scatter_added")
        var2 = sem("var2")
        std2 = sem("std2")
        out_ready = sem("out_ready")
        out_stored = sem("out_stored")

        NCONST = 10
        n_rows = 7

        def ada_unit(k, j):
            return A["w_ada"][0, bass.ts(k, P), j * D:(j + 1) * D]

        def win_unit(g, u, gates=False):
            col = g * COLS + (HEADS if gates else 0)
            return A["w_in"][0, u * COLS:(u + 1) * COLS, bass.ds(col, COLS)].rearrange("(k p) f -> p k f", p=P)

        def square_unit(w, n, u):
            return w[0, u * COLS:(u + 1) * COLS, n * COLS:(n + 1) * COLS].rearrange("(k p) f -> p k f", p=P)

        def gu_unit(e, i):
            w = A["w_gate"] if i % 2 == 0 else A["w_up"]
            r = (i // 2) * KPU * P
            return w[0, e, r:r + KPU * P, :].rearrange("(k p) f -> p k f", p=P)

        def down_unit(e, c):
            return A["w_down"][0, e, c * P:(c + 1) * P, :].rearrange("p (n f) -> p n f", n=KPU)

        def flat(slot):
            return slot[:, :, :].rearrange("p k f -> p (k f)")

        MAIN_FILLS = NADA1 // RAW_SLOTS
        ADA_FILLS = NADA1 // RAW_SLOTS + 1
        EXP_FILLS = [ADA_FILLS + 2 * KD] * 2 + [MAIN_FILLS + GA + GG + 2 * NPROJ] * 4 + [0] * 2
        GM = GA + GG

        block = ctx.enter_context(nc.Block())

        @block.sync
        def _(sp):
            def ada1_load(i, m):
                sp.dma_start(flat(raw[m]), ada_unit(3 * i + m // 2, m % 2)).then_inc(landed[m], 16)

            for m in range(RAW_SLOTS):
                ada1_load(0, m)
            with sp.Fori(1, NADA1 // RAW_SLOTS) as i:
                for m in range(RAW_SLOTS):
                    sp.wait_ge(ada1_done, i * RAW_SLOTS + m - 5)
                    ada1_load(i, m)
            for m in range(2):
                sp.wait_ge(ada1_done, NADA1 - 2 + m - 5)
                ada1_load(NADA1 // RAW_SLOTS, m)

            def mixer_loads(g, gates, ada):
                first = isinstance(g, int) and g == 0
                for u in range(4):
                    if first:
                        sp.wait_ge(ada1_done, NADA1 - RAW_SLOTS + u + 1)
                    else:
                        sp.wait_ge(main_used, 4 * g + u - 3)
                    sp.dma_start(raw[2 + u][:, :, :], win_unit(g, u, gates)).then_inc(landed[2 + u], 16)
                    if ada:
                        j = u
                        if first and j < 2:
                            sp.wait_ge(ada1_done, NADA1 - 1 + j)
                        else:
                            sp.wait_ge(ada2_done, 4 * g + j - 1)
                        sp.dma_start(flat(raw[j % 2]), ada_unit(g, 2 + j)).then_inc(landed[j % 2], 16)

            mixer_loads(0, False, True)
            with sp.Fori(1, GA) as g:
                mixer_loads(g, False, True)
            for g in range(GA, GM):
                mixer_loads(g, True, g < KD)
            for n in range(NPROJ):
                for u in range(4):
                    sp.wait_ge(main_used, 4 * (GM + n) + u - 3)
                    w = A["w_proj_a"] if u < 2 else A["w_proj_b"]
                    sp.dma_start(raw[2 + u][:, :, :], square_unit(w, n, u % 2)).then_inc(landed[2 + u], 16)
            for n in range(NPROJ):
                for u in range(4):
                    sp.wait_ge(main_used, 4 * (GM + NPROJ + n) + u - 3)
                    sp.dma_start(raw[2 + u][:, :, :], square_unit(A["w_o"], n, u)).then_inc(landed[2 + u], 16)

            def task_load(s, src):
                sp.dma_start(raw[s][:, :, :], src).then_inc(landed[s], 16)

            sp.wait_ge(ada2_done, 4 * KD)
            for i in range(GU):
                if 2 <= i < RAW_SLOTS:
                    sp.wait_ge(main_used, 4 * (GM + 2 * NPROJ) - RAW_SLOTS + i + 1)
                if i == RAW_SLOTS:
                    sp.wait_ge(logit_done, 1)
                if i == RAW_SLOTS + 1:
                    sp.wait_ge(h2lo_done, TB)
                task_load(i, gu_unit(0, i))

            def turn_loads(X, m, more=True):
                if more:
                    e = sp.value_load(task_i[0:1, bass.ds(X, 1)], min_val=0, max_val=E - 1)
                e_down = sp.value_load(task_i[0:1, bass.ds(X - 1, 1)], min_val=0, max_val=E - 1)
                for i in range(GU):
                    if more:
                        if i < 4:
                            sp.wait_ge(lo_ready, X * GU - GU + 4 + i + 1)
                        else:
                            sp.wait_ge(down_used, X * FC - FC + (i - 4) + 1)
                        if i == 0:
                            sp.sem_inc(loads_begun, 1)
                        task_load((4 * m + i) % EXP_SLOTS, gu_unit(e, i))
                for c in range(FC):
                    if more:
                        sp.wait_ge(lo_ready, X * GU + c + 1)
                    elif c == 0:
                        sp.wait_ge(lo_ready, X * GU)
                    if c == 0:
                        sp.sem_inc(loads_begun, 1)
                    task_load((4 * m + c) % EXP_SLOTS, down_unit(e_down, c))

            sp.wait_ge(tables_done, 1)
            turns = sp.value_load(turns_i[0:1, 0:1], min_val=PAIRS - 1, max_val=PAIRS - 1 + EXTRA // 2)
            with sp.Fori(0, turns) as q:
                for m in range(2):
                    turn_loads(q * 2 + (m + 1), m)
            last = turns * 2 + 1
            turn_loads(last, 0)
            turn_loads(last + 1, 1, more=False)
            sp.wait_ge(unit_used, last * GU + GU)
            for name, dst, src in [("g2", g2_row, mod_dram[3 * KD:4 * KD, :].rearrange("k c -> (k c)")),
                                   ("ln2g", ln2g, A["ln2_g"][0, :]), ("ln2b", ln2b, A["ln2_b"][0, :])]:
                sp.dma_start(dst[:, :], src.partition_broadcast(P)).then_inc(row_in[name], 16)
            for tb in range(TB):
                sp.wait_ge(out_ready, tb + 1)
                sp.dma_start(out[0, tb * P:(tb + 1) * P, :], out_acc[:, tb, :]).then_inc(out_stored, 16)
            sp.wait_ge(out_stored, 16 * TB)

        @block.gpsimd
        def _(pool):
            steps = [0]

            def chain(ins):
                steps[0] += 1
                ins.then_inc(pool_step, 1)
                pool.wait_ge(pool_step, steps[0])

            def keep(t, op, base, partition, pattern, fill=0.0):
                return pool.affine_select(out=t, in_=t, compare_op=op, fill=fill, base=base, pattern=pattern,
                                          channel_multiplier=partition)

            pool.memset(acc1[:, :, :], 0.0).then_inc(acc1_zeroed, 1)
            chain(pool.memset(ident[:, :], 0.0))
            keep(ident[:, :], ALU.not_equal, 0, 1, [[-1, P]], 1.0).then_inc(consts_made, 1)
            pool.memset(ones[:, :], 1.0).then_inc(consts_made, 1)
            chain(pool.memset(tri_incl[:, :], 1.0))
            keep(tri_incl[:, :], ALU.is_ge, 0, -1, [[1, P]]).then_inc(consts_made, 1)
            chain(pool.memset(tri_excl[:, :], 1.0))
            keep(tri_excl[:, :], ALU.is_gt, 0, -1, [[1, P]]).then_inc(consts_made, 1)
            chain(pool.memset(twin[:, :], 0.0))
            chain(keep(twin[:, :], ALU.not_equal, 0, 1, [[-1, SLOTS]], 1.0))
            keep(twin[:, :], ALU.not_equal, -SLOTS, 1, [[-1, SLOTS]], 1.0).then_inc(consts_made, 1)
            chain(pool.iota(slot_i[:, :], pattern=[[1, SLOTS]], base=1, channel_multiplier=0))
            pool.tensor_copy(slot_id[:, :], slot_i[:, :]).then_inc(consts_made, 1)
            chain(pool.iota(expert_i[:, :], pattern=[[1, E]], base=0, channel_multiplier=0))
            pool.tensor_copy(expert_id[:, :], expert_i[:, :]).then_inc(consts_made, 1)
            for b in range(OVER):
                rows = slice(b * E, (b + 1) * E)
                chain(pool.iota(expert96_i[rows, :], pattern=[[1, 1]], base=0, channel_multiplier=1))
                chain(pool.memset(least96[rows, :], float((b + 1) * SLOTS)))
            pool.tensor_copy(expert96[:, :], expert96_i[:, :]).then_inc(consts_made, 1)
            chain(pool.memset(mask3[:, :, :], 0.0))
            for b in (0, 2):
                keep(mask3[:, b, :], ALU.is_ge, 0, 1, [[-1, P]], NEG).then_inc(consts_made, 1)

            pool.wait_ge(rowsT_done, 1)
            for j in range(4):
                pool.memset(acc[:, j, :], 0.0).then_inc(acc_zeroed, 1)
            pool.wait_ge(rowsT_copied, 3)
            for g in range(HEADS):
                keep(wsT[:, g, :], ALU.is_ge, 0, -1, [[1, P]]).then_inc(ws_masked, 1)

            pool.wait_ge(modrow_done, 1)
            pool.dma_start(mod_dram[:, :], modrow[:, :]).then_inc(mod_stored, 16)
            pool.wait_ge(mod_stored, 16)
            pool.wait_ge(main_used, 4 * (GM + NPROJ))
            for name, dst, src in [("g1", g1_row, mod_dram[0:KD, :].rearrange("k c -> (k c)")),
                                   ("ln1g", ln1g, A["ln1_g"][0, :]), ("ln1b", ln1b, A["ln1_b"][0, :]),
                                   ("sc2", sc2_row, mod_dram[2 * KD:3 * KD, :].rearrange("k c -> (k c)")),
                                   ("sh2", sh2_row, mod_dram[KD:2 * KD, :].rearrange("k c -> (k c)"))]:
                pool.dma_start(dst[:, :], src.partition_broadcast(P)).then_inc(row_in[name], 16)
            pool.dma_start(rw[:, :, :], A["router_w"][0].rearrange("(k p) e -> p k e", p=P)).then_inc(row_in["rw"], 16)
            pool.dma_start(rb_row[:, :], A["router_b"][0:1, :]).then_inc(row_in["rb"], 16)
            pool.dma_start(bdown[:, :], A["b_down"][0]).then_inc(row_in["bdown"], 16)

            pool.memset(selwT[:, :], 0.0).then_inc(selwT_filled, 1)
            pool.wait_ge(tables_done, 1)
            for n in range(4):
                pool.memset(y[:, n * COLS:(n + 1) * COLS], 0.0).then_inc(y_filled, 1)

        @block.tensor
        def _(pe):
            def T(dst, src, rows=P):
                return pe.transpose(dst, src, ident[0:rows, 0:rows])

            pe.wait_ge(consts_made, 1)
            pe.wait_ge(c_loaded, 16)
            T(bank[:, 0, 0:KD], c_rows[:, :], KD).then_inc(cT_done, 1)
            pe.wait_ge(rows_loaded, 16 * n_rows)
            T(bank[:, 1, 0:2 * KD], bada_rows[:, :], 2 * KD)
            T(bank[:, 1, 32:32 + HEADS], bs_rows[:, :], HEADS)
            T(bank[:, 1, P:2 * P], bg_rows[:, :])
            T(bank[:, 1, 2 * P:3 * P], bu_rows[:, :])
            for g in range(HEADS):
                last = T(bank[:, 2 + g // 4, (g % 4) * P:(g % 4 + 1) * P], ws_raw[:, g, :])
            last.then_inc(rowsT_done, 1)
            pe.wait_ge(x_loaded, 16)
            for b in range(8):
                if b == 4:
                    pe.wait_ge(sig_c, 1)
                    pe.wait_ge(rowsT_copied, 3)
                for i in range(4):
                    k, tb = 2 * b + i // 2, i % 2
                    last = T(bank[:, (4 + b) % 8, i * P:(i + 1) * P], x[:, tb, k * P:(k + 1) * P])
                last.then_inc(xT_done, 1)

            pe.wait_ge(consts_made, 2)
            pe.wait_ge(xT_copied, 8)
            pe.wait_ge(ada1_done, NADA1)
            for j in range(2):
                for k in range(KD):
                    last = pe.matmul(bank[:, 0, j * KD + k:j * KD + k + 1], acc1[:, j, k * P:(k + 1) * P], ones[:, 0:1],
                                     start=True, stop=True)
            last.then_inc(ada1_cols, 1)

            def main_unit(G, u):
                pe.wait_ge(landed[2 + u], (G + MAIN_FILLS + 1) * 16)

            def group(G, lhsT, banks):
                for u in range(4):
                    main_unit(G, u)
                    if isinstance(G, int) and G == 0:
                        pe.wait_ge(h_done, 4 * (u + 1))
                    for tb in range(TB):
                        for kk in range(KPU):
                            last = pe.matmul(bank[:, banks[tb], :], lhsT[:, u * KPU + kk, tb * P:(tb + 1) * P],
                                             raw[2 + u][:, kk, :], start=(u == 0 and kk == 0),
                                             stop=(u == 3 and kk == KPU - 1))
                    last.then_inc(main_used, 1)

            def win_group(G, parity):
                if not (isinstance(G, int) and G < 2):
                    pe.wait_ge(z_copied, G * 2 - 2)
                group(G, hT, [2 * parity, 2 * parity + 1])

            pe.wait_ge(mod1_done, 1)
            for G in range(2):
                win_group(G, G)
            with pe.Fori(1, GA // 2) as i:
                for parity in range(2):
                    win_group(i * 2 + parity, parity)

            pe.wait_ge(wf_loaded, 16)
            for tb in range(TB):
                for k in range(KD):
                    pe.matmul(bank[:, 4, tb * HEADS:(tb + 1) * HEADS], hT[:, k, tb * P:(tb + 1) * P], wf[:, k, :],
                              start=(k == 0), stop=False)
                last = pe.matmul(bank[:, 4, tb * HEADS:(tb + 1) * HEADS], ones[0:1, :], bf_row[:, :], start=False, stop=True)
            last.then_inc(f_done, 1)

            def qkT(half):
                for h in range(4 * half, 4 * half + 4):
                    b = 4 + h % 4
                    if h == 0:
                        pe.wait_ge(z_copied, 2 * GA)
                        pe.wait_ge(lt_done, 1)
                        pe.wait_ge(lf_done, 1)
                    if h >= 4:
                        pe.wait_ge(qkT_copied, 2 * (h - 4) + 2)
                    for i, off in enumerate((Q_, Q_, K_, K_)):
                        last = T(bank[:, b, i * P:(i + 1) * P], zA[:, i % 2, off + h * P:off + (h + 1) * P])
                    last.then_inc(qkT_done, 1)

            def sgu():
                pe.wait_ge(vn_done, 2 * TB)
                pe.wait_ge(ws_masked, HEADS)
                pe.wait_ge(qkT_copied, 2 * HEADS)
                for g in range(HEADS):
                    pe.matmul(bank[:, 4 + g // 2, (g % 2) * SEQ:(g % 2 + 1) * SEQ], wsT[:, g, :],
                              zA[:, 0:TB, V_ + g * P:V_ + (g + 1) * P], start=True, stop=True).then_inc(sgu_done, 1)

            def cumulate():
                pe.wait_ge(ya_done, HEADS)
                pe.wait_ge(lf_done, 2)
                l0, l1 = lf[:, 0:HEADS], lf[:, HEADS:2 * HEADS]
                pe.matmul(bank[:, 4, 0:HEADS], tri_incl[:, :], l0, start=True, stop=True)
                pe.matmul(bank[:, 4, HEADS:2 * HEADS], ones[:, :], l0, start=True, stop=False)
                pe.matmul(bank[:, 4, HEADS:2 * HEADS], tri_incl[:, :], l1, start=False, stop=True)
                pe.matmul(bank[0:HEADS, 5, 0:P], l0, tri_incl[:, :], start=True, stop=True)
                pe.matmul(bank[0:HEADS, 5, P:SEQ], l0, ones[:, :], start=True, stop=False)
                pe.matmul(bank[0:HEADS, 5, P:SEQ], l1, tri_incl[:, :], start=False, stop=True).then_inc(cum_done, 1)

            def scores(half):
                pe.wait_ge(cum_copied, 2)
                if half:
                    pe.wait_ge(oT_copied, 4)
                for hh in range(4):
                    h = 4 * half + hh
                    for tb in range(TB):
                        o = bank[:, 4 + hh, tb * P:tb * P + (tb + 1) * P]
                        pe.matmul(o, zA[:, tb, Q_ + h * P:Q_ + (h + 1) * P], zA[:, 0:tb + 1, K_ + h * P:K_ + (h + 1) * P],
                                  start=True, stop=False)
                        last = pe.matmul(o, ident[0:HEADS, h:h + 1].to_broadcast([HEADS, P]), cumT[:, 0:(tb + 1) * P],
                                         start=False, stop=True)
                    last.then_inc(scores_done, 1)

            def probsT_of(half):
                for hh in range(4):
                    pe.wait_ge(probs_done, 4 * half + hh + 1)
                    for b in range(3):
                        last = T(bank[:, 4 + hh, b * P:(b + 1) * P], probs[:, hh, b * P:(b + 1) * P])
                    last.then_inc(pT_done, 1)

            def oT(half):
                for hh in range(4):
                    h = 4 * half + hh
                    pe.wait_ge(pT_copied, h + 1)
                    pe.matmul(bank[:, 4 + hh, 0:SEQ], zA[:, 0, VB_ + h * P:VB_ + (h + 1) * P], probsT[:, hh, 0:SEQ],
                              start=True, stop=False)
                    pe.matmul(bank[:, 4 + hh, P:SEQ], zA[:, 1, VB_ + h * P:VB_ + (h + 1) * P], probsT[:, hh, SEQ:3 * P],
                              start=False, stop=True).then_inc(oT_done, 1)

            def yaT():
                pe.wait_ge(z_copied, 2 * GM)
                for b in range(4):
                    for i in range(4):
                        tb, c = i // 2, 2 * b + i % 2
                        last = T(bank[:, b, i * P:(i + 1) * P], zA[:, tb, U_ + c * P:U_ + (c + 1) * P])
                    last.then_inc(yaT_done, 1)

            after = {10: [lambda: qkT(0)], 11: [lambda: qkT(1)], 12: [sgu], 13: [cumulate], 14: [lambda: scores(0)],
                     15: [lambda: probsT_of(0)], 16: [lambda: oT(0), lambda: scores(1)],
                     17: [lambda: probsT_of(1), yaT, lambda: oT(1)]}
            for G in range(GA, GM):
                win_group(G, G % 2)
                for stage in after[G]:
                    stage()

            pe.wait_ge(oT_copied, 8)
            pe.wait_ge(ada2_done, 4 * KD)
            for j in range(4):
                for k in range(KD):
                    last = pe.matmul(bank[:, 7, j * KD + k:j * KD + k + 1], acc[:, j, k * P:(k + 1) * P], ones[:, 0:1],
                                     start=True, stop=True)
            last.then_inc(cols2_done, 1)

            def project(n):
                s = 4 * (n % 2)
                if n == 0:
                    pe.wait_ge(yaT_copied, 4)
                if n == 1:
                    pe.wait_ge(modrow_done, 1)
                if n >= 2:
                    pe.wait_ge(mT_copied, 2 * (n - 1))
                for u in range(4):
                    main_unit(GM + n, u)
                    off = V_ if u < 2 else Q_
                    for tb in range(TB):
                        for kk in range(KPU):
                            c = (u % 2) * KPU + kk
                            last = pe.matmul(bank[:, s + 2 * (u // 2) + tb, :], zA[:, tb, off + c * P:off + (c + 1) * P],
                                             raw[2 + u][:, kk, :], start=(c == 0), stop=(c == 7))
                    last.then_inc(main_used, 1)

            def mergedT(n):
                s = 4 * (n % 2)
                pe.wait_ge(merged_done, 2 * (n + 1))
                for b in range(2):
                    for i in range(4):
                        k, tb = 2 * b + i // 2, i % 2
                        last = T(bank[:, s + b, i * P:(i + 1) * P], zG[:, tb, n * COLS + k * P:n * COLS + (k + 1) * P])
                    last.then_inc(mT_done, 1)

            for n in range(NPROJ):
                project(n)
                if n == 0:
                    pe.wait_ge(cols2_copied, 1)
                    T(bank[0:4 * KD, 6, 0:P], modcol[:, :]).then_inc(modT_done, 1)
                if n:
                    mergedT(n - 1)
            mergedT(NPROJ - 1)

            for n in range(NPROJ):
                if n == 0:
                    pe.wait_ge(mT_copied, 2 * NPROJ)
                if n >= 2:
                    pe.wait_ge(res_done, 2 * (n - 1))
                group(GM + NPROJ + n, hT, [2 * (n % 2), 2 * (n % 2) + 1])

            for b in range(8):
                if b == 0:
                    pe.wait_ge(res_done, 2 * NPROJ)
                pe.wait_ge(h2_done, 2)
                for i in range(4):
                    k, tb = 2 * b + i // 2, i % 2
                    last = T(bank[:, b, i * P:(i + 1) * P], h2[:, tb, k * P:(k + 1) * P])
                last.then_inc(h2T_done, 1)
            pe.wait_ge(h2T_copied, 8)
            pe.wait_ge(row_in["rw"], 16)
            pe.wait_ge(row_in["rb"], 16)
            for tb in range(TB):
                for k in range(KD):
                    pe.matmul(bank[:, 0, tb * E:(tb + 1) * E], h2T[:, k, tb * P:(tb + 1) * P], rw[:, k, :],
                              start=(k == 0), stop=False)
                last = pe.matmul(bank[:, 0, tb * E:(tb + 1) * E], ones[0:1, :], rb_row[:, :], start=False, stop=True)
            last.then_inc(logit_done, 1)
            pe.wait_ge(mask_done, 2)
            pe.matmul(bank[:, 1, 0:E], tri_excl[:, :], mask[:, 0, :], start=True, stop=True)
            pe.matmul(bank[:, 1, E:2 * E], ones[:, :], mask[:, 0, :], start=True, stop=False)
            pe.matmul(bank[:, 1, E:2 * E], tri_excl[:, :], mask[:, 1, :], start=False, stop=True).then_inc(pos_done, 1)
            pe.wait_ge(over_masked, 1)
            for tb in range(TB):
                last = pe.matmul(bank[0:N96, 3, 0:1], mask96[:, tb, :], ones[:, 0:1], start=(tb == 0), stop=(tb == TB - 1))
            last.then_inc(over_counted, 1)
            pe.wait_ge(comb_done, 2)
            for tb in range(TB):
                last = T(bank[0:E, 2, tb * P:(tb + 1) * P], comb[:, tb, 0:E])
            last.then_inc(combT_done, 1)
            pe.wait_ge(over_flagged, 1)
            pe.matmul(bank[0:N96, 6, 0:1], tri_incl[0:N96, 0:N96], flag96[:, :], start=True, stop=True)
            pe.matmul(bank[0:1, 6, 32:33], flag96[:, :], ones[0:N96, 0:1], start=True, stop=True).then_inc(over_ranked, 1)
            pe.wait_ge(over_tabled, 2)
            for i in range(2 * TB):
                last = T(bank[0:N96, 4, i * P:(i + 1) * P], pc96[:, i, :])
            last.then_inc(over_turned, 1)
            pe.wait_ge(over_placed, 1)
            pe.wait_ge(over_copied, 1)
            pe.matmul(bank[0:1, 5, 4 * EXTRA:5 * EXTRA], expert96[:, :], place96[:, :], start=True, stop=True)
            for i in range(2 * TB):
                last = pe.matmul(bank[:, 5, i * EXTRA:(i + 1) * EXTRA], pc96T[:, i * P:(i + 1) * P], place96[:, :],
                                 start=True, stop=True)
            last.then_inc(over_spread, 1)
            pe.wait_ge(combT_copied, 1)
            pe.wait_ge(row_in["bdown"], 16)
            for i in range(8):
                tb, n = i // 4, i % 4
                if i >= 2:
                    pe.wait_ge(bias_copied, i - 1)
                pe.matmul(bank[:, 7 if i % 2 == 0 else 0, :], combT[:, tb * P:(tb + 1) * P],
                          bdown[:, n * COLS:(n + 1) * COLS], start=True, stop=True).then_inc(bias_done, 1)

            def hsel_copied(b, n):
                pe.wait_ge(hsel_act if b % 2 else hsel_dve, n * 2 + b // 2)

            def gather(X):
                pe.wait_ge(sel_ready, X + 1)
                for c in range(KD):
                    for part, src in ((0, h2hi), (1, h2lo)):
                        o = bank[:, 2 + c // 4, (c % 4) * P + part * SLOTS:(c % 4) * P + (part + 1) * SLOTS]
                        for tb in range(TB):
                            last = pe.matmul(o, src[:, tb, c * P:(c + 1) * P], sel[:, tb, :], start=(tb == 0), stop=(tb == 1))
                    if c % 4 == 3:
                        last.then_inc(gathered, 1)

            def gate_and_up(X):
                for i in range(GU):
                    if i % 2 == 0:
                        hsel_copied(2 + i // 2, X)
                    pe.wait_ge(lo_ready, X * GU + (i + 1))
                    for kk in range(KPU):
                        for part in (hi[i % HI_SLOTS], lo[i % LO_SLOTS]):
                            last = pe.matmul(bank[:, i % 2, :], hsel[:, (i // 2) * KPU + kk, :], part[:, kk, :],
                                             start=(i < 2 and kk == 0 and part is hi[i % HI_SLOTS]),
                                             stop=(i >= GU - 2 and kk == KPU - 1 and part is lo[i % LO_SLOTS]))
                    last.then_inc(unit_used, 1)

            def turn_gate_up(X):
                pe.wait_ge(gu_copied, X * 2 + 2)
                for c in range(2 * FC):
                    last = pe.matmul(bank[:, 6, c * SLOTS:(c + 1) * SLOTS], gu_sb[:, c // FC, (c % FC) * P:(c % FC + 1) * P],
                                     twin[:, :], start=True, stop=True)
                last.then_inc(tsum_done, 1)

            def scatter(X, q):
                pe.wait_ge(y_filled, X * 4)
                pe.wait_ge(selwT_filled, q + 1)
                for i in range(8):
                    tb, n = i // 4, i % 4
                    if i >= 2:
                        pe.wait_ge(scatter_added, q * 8 + (i - 1))
                    pe.matmul(bank[:, 7 if i % 2 == 0 else 6, :], selwT[:, tb * P:(tb + 1) * P],
                              y[:, n * COLS:(n + 1) * COLS], start=True, stop=True).then_inc(scattered, 1)

            def turn_weights(q):
                pe.wait_ge(selw_ready, q + 1)
                for tb in range(TB):
                    last = T(bank[:, 7, tb * P:(tb + 1) * P], selw[:, tb, :])
                last.then_inc(selwT_done, 1)

            def down(X, q, off, parity, gather_behind=True):
                pe.wait_ge(act_ready, X)
                if not gather_behind:
                    pe.wait_ge(y_filled, X * 4)
                for c in range(FC):
                    s = (off + c) % EXP_SLOTS
                    pe.wait_ge(landed[s], (q * 3 + ((off + c) // EXP_SLOTS + EXP_FILLS[s] + 1)) * 16)
                    for n in range(4):
                        if c == 0 and gather_behind:
                            hsel_copied(2 + n, X + 1)
                        last = pe.matmul(bank[0:SLOTS, 2 + n, :], act[parity][:, c * SLOTS:(c + 1) * SLOTS],
                                         raw[s][:, n, :], start=(c == 0), stop=(c == FC - 1))
                    last.then_inc(down_used, 1)

            pe.wait_ge(h2lo_done, TB)
            pe.wait_ge(tables_done, 1)
            gather(0)
            pe.sem_inc(down_used, FC)
            pe.wait_ge(bias_copied, 8)
            gate_and_up(0)
            gather(1)
            turn_gate_up(0)
            turns = pe.value_load(turns_i[0:1, 0:1], min_val=PAIRS - 1, max_val=PAIRS - 1 + EXTRA // 2)
            with pe.Fori(0, turns) as q:
                for m in range(2):
                    X = q * 2 + (m + 1)
                    gate_and_up(X)
                    pe.wait_ge(biased, X)
                    if m == 0:
                        scatter(X, q)
                    pe.wait_ge(y_filled, X * 4)
                    gather(X + 1)
                    if m == 0:
                        pe.wait_ge(scatter_added, q * 8 + 8)
                    turn_gate_up(X)
                    if m == 1:
                        turn_weights(q)
                    down(X, q, 16 + 12 * m, m)
            last_task = turns * 2 + 1
            gate_and_up(last_task)
            pe.wait_ge(biased, last_task)
            scatter(last_task, turns)
            pe.wait_ge(scatter_added, turns * 8 + 8)
            turn_gate_up(last_task)
            down(last_task, turns, 16, 0, False)
            turn_weights(turns)
            down(last_task + 1, turns, 20, 1, False)
            pe.wait_ge(biased, last_task + 1)
            scatter(last_task + 2, turns + 1)

        @block.scalar
        def _(act_):
            def copy(dst, src, **k):
                return act_.activation(dst, src, ACT.Copy, **k)

            act_.dma_start(c_rows[:, :], A["c"][0, :].rearrange("(k p) -> k p", p=P)).then_inc(c_loaded, 16)
            for dst, src in ((bada_rows[:, :], A["b_ada"][0, 0:2 * D].rearrange("(k p) -> k p", p=P)),
                             (bs_rows[:, :], A["spatial_b"][0]),
                             (bg_rows[:, :], A["b_gate"][0].rearrange("e (c p) -> (e c) p", p=P)),
                             (bu_rows[:, :], A["b_up"][0].rearrange("e (c p) -> (e c) p", p=P)),
                             (ws_raw[:, :, :], A["spatial_w"][0].rearrange("g t s -> t g s")),
                             (bf_row[:, :], A["b_f"][0:1, :]),
                             (bada2[:, :], A["b_ada"][0, 2 * D:6 * D].rearrange("(k p) -> k p", p=P))):
                act_.dma_start(dst, src).then_inc(rows_loaded, 16)
            act_.dma_start(x[:, :, :], A["x"][0].rearrange("(t p) d -> p t d", p=P)).then_inc(x_loaded, 16)
            act_.dma_start(lng, A["sgu_ln_g"][0].rearrange("g c -> (g c)").partition_broadcast(P)).then_inc(row_lng, 16)
            act_.dma_start(wf[:, :, :], A["w_in"][0, :, F_COL:F_COL + HEADS].rearrange("(k p) f -> p k f", p=P)).then_inc(wf_loaded, 16)

            act_.wait_ge(cT_done, 1)
            copy(cT[:, 0, :], bank[:, 0, 0:KD]).then_inc(sig_c, 1)
            act_.activation(cT[:, 1, :], bank[:, 0, 0:KD], ACT.Sigmoid).then_inc(sig_c, 1)
            act_.wait_ge(rowsT_done, 1)
            copy(wsT[:, 0:4, :], bank[:, 2, :]).then_inc(rowsT_copied, 1)
            copy(wsT[:, 4:8, :], bank[:, 3, :]).then_inc(rowsT_copied, 1)
            copy(badaT[:, :], bank[:, 1, 0:2 * KD])
            copy(bsT[:, :], bank[:, 1, 32:32 + HEADS])
            copy(bgu[:, :, 0:FC], bank[:, 1, P:2 * P].rearrange("p (e c) -> p e c", e=E))
            copy(bgu[:, :, FC:2 * FC], bank[:, 1, 2 * P:3 * P].rearrange("p (e c) -> p e c", e=E)).then_inc(rowsT_copied, 1)
            for b in range(8):
                act_.wait_ge(xT_done, b + 1)
                copy(hT[:, 2 * b:2 * b + 2, :], bank[:, (4 + b) % 8, :]).then_inc(xT_copied, 1)

            def z_out(G, parity, dst, func):
                act_.wait_ge(main_used, G * 4 + 4)
                for tb in range(TB):
                    act_.activation(dst(tb), bank[:, 2 * parity + tb, :], func).then_inc(z_copied, 1)

            def zA_cols(G):
                return lambda tb: zA[:, tb, bass.ds(G * COLS, COLS)]

            with act_.Fori(0, 2) as i:
                for parity in range(2):
                    G = i * 2 + parity
                    z_out(G, parity, zA_cols(G), ACT.Gelu_apprx_tanh)
            for G in range(4, 6):
                z_out(G, G % 2, zA_cols(G), ACT.Copy)
            act_.wait_ge(v_var, 1)
            act_.activation(rstd[:, :], mv[:, :, 1], ACT.Sqrt).then_inc(v_std, 1)
            with act_.Fori(3, 5) as i:
                for parity in range(2):
                    G = i * 2 + parity
                    z_out(G, parity, zA_cols(G), ACT.Copy)

            act_.wait_ge(f_done, 1)
            act_.activation(lt[:, :], bank[:, 4, 0:2 * HEADS], ACT.Abs).then_inc(act_step, 1)
            act_.wait_ge(act_step, 1)
            act_.activation(lt[:, :], lt[:, :], ACT.Exp, scale=-1.0).then_inc(act_step, 1)
            act_.wait_ge(act_step, 2)
            act_.activation(lt[:, :], lt[:, :], ACT.Ln, bias=1.0).then_inc(lt_done, 1)

            def gate_out(G):
                z_out(G, G % 2, lambda tb: zG[:, tb, (G - GA) * COLS:(G - GA + 1) * COLS], ACT.Sigmoid)

            def qkT_out(half):
                for h in range(4 * half, 4 * half + 4):
                    act_.wait_ge(qkT_done, h + 1)
                    copy(zA[:, 0:TB, Q_ + h * P:Q_ + (h + 1) * P], bank[:, 4 + h % 4, 0:SEQ].rearrange("p (t c) -> p t c", t=TB),
                         scale=SCALE).then_inc(qkT_copied, 1)
                    copy(zA[:, 0:TB, K_ + h * P:K_ + (h + 1) * P], bank[:, 4 + h % 4, SEQ:2 * SEQ].rearrange("p (t c) -> p t c", t=TB)
                         ).then_inc(qkT_copied, 1)

            def cum_out():
                act_.wait_ge(cum_done, 1)
                copy(cum[:, :], bank[:, 4, 0:2 * HEADS]).then_inc(cum_copied, 1)
                copy(cumT[:, :], bank[0:HEADS, 5, 0:SEQ], scale=-1.0).then_inc(cum_copied, 1)

            def exps(half):
                act_.wait_ge(max_done, half + 1)
                for hh in range(4):
                    act_.activation(probs[:, hh, 0:P], probs[:, hh, 0:P], ACT.Exp, bias=mx[:, 1, 2 * hh:2 * hh + 1],
                                    accum_out=sums[:, 2 * hh:2 * hh + 1]).then_inc(exp_done, 1)
                    act_.activation(probs[:, hh, P:3 * P], probs[:, hh, P:3 * P], ACT.Exp, bias=mx[:, 1, 2 * hh + 1:2 * hh + 2],
                                    accum_out=sums[:, 2 * hh + 1:2 * hh + 2]).then_inc(exp_done, 1)

            def pT_out(half):
                for hh in range(4):
                    act_.wait_ge(pT_done, 4 * half + hh + 1)
                    copy(probsT[:, hh, :], bank[:, 4 + hh, 0:3 * P]).then_inc(pT_copied, 1)

            def oT_out(half):
                for h in range(4 * half, 4 * half + 4):
                    act_.wait_ge(oT_done, h + 1)
                    copy(zA[:, 0:TB, Q_ + h * P:Q_ + (h + 1) * P],
                         bank[:, 4 + h % 4, 0:SEQ].rearrange("p (t c) -> p t c", t=TB)).then_inc(oT_copied, 1)

            def yaT_out():
                for b in range(4):
                    act_.wait_ge(yaT_done, b + 1)
                    copy(zA[:, 0:TB, V_ + 2 * b * P:V_ + 2 * (b + 1) * P],
                         bank[:, b, :].rearrange("p (t c) -> p t c", t=TB)).then_inc(yaT_copied, 1)

            gate_out(10)
            qkT_out(0)
            gate_out(11)
            qkT_out(1)
            gate_out(12)
            gate_out(13)
            cum_out()
            gate_out(14)
            exps(0)
            gate_out(15)
            pT_out(0)
            gate_out(16)
            oT_out(0)
            exps(1)
            gate_out(17)
            pT_out(1)
            yaT_out()
            oT_out(1)
            act_.wait_ge(cols2_done, 1)
            copy(modcol[:, :], bank[:, 7, 0:4 * KD]).then_inc(cols2_copied, 1)
            for n in range(NPROJ):
                for b in range(2):
                    act_.wait_ge(mT_done, 2 * n + b + 1)
                    copy(hT[:, 4 * n + 2 * b:4 * n + 2 * b + 2, :], bank[:, 4 * (n % 2) + b, :]).then_inc(mT_copied, 1)
            for tb in range(TB):
                act_.wait_ge(var1, tb + 1)
                act_.activation(rstd[:, tb:tb + 1], mv[:, tb, 1:2], ACT.Sqrt).then_inc(std1, 1)
            for b in range(8):
                act_.wait_ge(h2T_done, b + 1)
                copy(h2T[:, 2 * b:2 * b + 2, :], bank[:, b, :]).then_inc(h2T_copied, 1)
            act_.wait_ge(mT_done, 2 * NPROJ)
            act_.wait_ge(main_used, 4 * (GM + 2 * NPROJ))
            for tb in range(TB):
                copy(h2hi[:, tb, :], h2[:, tb, :]).then_inc(h2hi_done, 1)
            for tb in range(TB):
                act_.wait_ge(top_done, tb + 1)
                act_.activation(topw[:, tb, 0:TOPK], top[:, tb, 0:TOPK], ACT.Exp, bias=tops[:, tb:tb + 1],
                                accum_out=tops[:, 2 + tb:3 + tb]).then_inc(topw_done, 1)
            act_.wait_ge(combT_done, 1)
            copy(combT[:, :], bank[0:E, 2, 0:SEQ]).then_inc(combT_copied, 1)

            def hi_part(X, q, m, i):
                first = isinstance(X, int) and X == 0
                off = i if first else 8 + 12 * m + i
                s = off % EXP_SLOTS
                act_.wait_ge(landed[s], (q * 3 + (off // EXP_SLOTS + EXP_FILLS[s] + 1)) * 16)
                if not (first and i < HI_SLOTS):
                    act_.wait_ge(unit_used, X * GU + (i + 1 - HI_SLOTS))
                copy(hi[i % HI_SLOTS][:, :, :], raw[s][:, :, :]).then_inc(hi_ready, 1)

            def hsel_odd(X):
                for b in (3, 5):
                    act_.wait_ge(gathered, X * 4 + (b - 1))
                    copy(hsel[:, 4 * b - 8:4 * b - 4, :], bank[:, b, :]).then_inc(hsel_act, 1)

            def sigmoid(X, parity):
                act_.wait_ge(gate_ready, X + 1)
                act_.activation(act[parity][:, :], gate_up_T[:, 0:FC * SLOTS], ACT.Sigmoid, scale=SWI).then_inc(sig_ready, 1)

            def weights_out(q):
                act_.wait_ge(selwT_done, q + 1)
                copy(selwT[:, :], bank[:, 7, 0:SEQ]).then_inc(selwT_filled, 1)

            def rows_out(X, parity):
                act_.wait_ge(down_used, X * FC + FC)
                for n in range(4):
                    copy(y[parity * SLOTS:(parity + 1) * SLOTS, n * COLS:(n + 1) * COLS],
                         bank[0:SLOTS, 2 + n, :]).then_inc(y_filled, 1)

            def turn(X, q, m, first=False, last=False):
                parity = 1 - m
                for i in range(HI_SLOTS, GU):
                    hi_part(X, 0 if first else q, m, i)
                if not first:
                    act_.wait_ge(act_ready, X)
                for i in range(2):
                    act_.wait_ge(unit_used, X * GU + (GU - 1 + i))
                    copy(gu_sb[:, i, :], bank[:, i, :]).then_inc(gu_copied, 1)
                if last:
                    sigmoid(X, parity)
                    rows_out(X, m)
                    return
                hsel_odd(X + 1)
                ahead = (q, 1) if m == 0 else (q + 1, 0)
                hi_part(X + 1, *ahead, 0)
                sigmoid(X, parity)
                for i in range(1, HI_SLOTS):
                    hi_part(X + 1, *ahead, i)
                if m == 1 and not first:
                    weights_out(q)
                if not first:
                    rows_out(X, m)

            act_.wait_ge(h2_done, 2)
            for i in range(HI_SLOTS):
                hi_part(0, 0, 1, i)
            hsel_odd(0)
            turn(0, -1, 1, first=True)
            act_.wait_ge(tables_done, 1)
            turns = act_.value_load(turns_i[0:1, 0:1], min_val=PAIRS - 1, max_val=PAIRS - 1 + EXTRA // 2)
            with act_.Fori(0, turns) as q:
                for m in range(2):
                    turn(q * 2 + (m + 1), q, m)
            last_task = turns * 2 + 1
            turn(last_task, turns, 0, last=True)
            weights_out(turns)
            rows_out(last_task + 1, 1)
            for tb in range(TB):
                act_.wait_ge(var2, tb + 1)
                act_.activation(rstd[:, tb:tb + 1], mv[:, tb, 1:2], ACT.Sqrt).then_inc(std2, 1)

        @block.vector
        def _(dve):
            steps = [0]

            def chain(ins):
                steps[0] += 1
                ins.then_inc(dve_step, 1)
                dve.wait_ge(dve_step, steps[0])

            dve.wait_ge(sig_c, 2)
            chain(dve.tensor_tensor(condT[:, :], cT[:, 0, :], cT[:, 1, :], ALU.mult))
            dve.wait_ge(acc1_zeroed, 1)

            def add_unit(dst, slot, k, done):
                return dve.scalar_tensor_tensor(out=dst, in0=flat(slot), scalar=condT[:, k], in1=dst,
                                                op0=ALU.mult, op1=ALU.add).then_inc(done, 1)

            def ada1(i, m):
                n = i * RAW_SLOTS + m
                if not (isinstance(n, int) and n < 2):
                    dve.wait_ge(ada1_done, n - 1)
                dve.wait_ge(landed[m], (i + 1) * 16)
                add_unit(acc1[:, m % 2, :], raw[m], bass.ds(i * 3 + m // 2, 1), ada1_done)

            for m in range(RAW_SLOTS):
                ada1(0, m)
            with dve.Fori(1, NADA1 // RAW_SLOTS) as i:
                for m in range(RAW_SLOTS):
                    ada1(i, m)
            for m in range(2):
                ada1(NADA1 // RAW_SLOTS, m)
            dve.wait_ge(ada1_cols, 1)
            dve.wait_ge(rowsT_copied, 3)
            dve.tensor_tensor(mod1[:, 0:KD], bank[:, 0, 0:KD], badaT[:, 0:KD], ALU.add).then_inc(mod1_done, 1)
            dve.scalar_tensor_tensor(out=mod1[:, KD:2 * KD], in0=bank[:, 0, KD:2 * KD], scalar=1.0, in1=badaT[:, KD:2 * KD],
                                     op0=ALU.add, op1=ALU.add).then_inc(mod1_done, 1)
            dve.wait_ge(mod1_done, 2)
            dve.wait_ge(xT_copied, 8)
            for k in range(KD):
                dve.tensor_scalar(hT[:, k, :], hT[:, k, :], mod1[:, KD + k:KD + k + 1], mod1[:, k:k + 1],
                                  ALU.mult, ALU.add).then_inc(h_done, 1)

            def ada2(k):
                for j in range(4):
                    if not (isinstance(k, int) and k == 0):
                        dve.wait_ge(ada2_done, k * 4 + j - 3)
                    dve.wait_ge(landed[j % 2], (k * 2 + j // 2 + ADA_FILLS + 1) * 16)
                    add_unit(acc[:, j, :], raw[j % 2], bass.ds(k, 1), ada2_done)

            dve.wait_ge(acc_zeroed, 4)
            ada2(0)
            with dve.Fori(1, 5) as k:
                ada2(k)

            dve.wait_ge(z_copied, 8)
            for tb in range(TB):
                for g in range(HEADS):
                    dve.bn_stats(st[:, tb * HEADS + g, :], zA[:, tb, V_ + g * P:V_ + (g + 1) * P]).then_inc(v_stat, 1)
            for i in range(TB * HEADS):
                dve.wait_ge(v_stat, i + 1)
                dve.bn_aggr(mv[:, i, :], st[:, i, :]).then_inc(v_agg, 1)
            dve.wait_ge(v_agg, TB * HEADS)
            dve.tensor_scalar(mv[:, :, 1], mv[:, :, 1], EPS, None, ALU.add).then_inc(v_var, 1)
            with dve.Fori(5, 8) as k:
                ada2(k)
            dve.wait_ge(v_std, 1)
            chain(dve.reciprocal(rstd[:, :], rstd[:, :]))
            for tb in range(TB):
                for g in range(HEADS):
                    v = zA[:, tb, V_ + g * P:V_ + (g + 1) * P]
                    i = tb * HEADS + g
                    ins = dve.tensor_scalar(v, v, mv[:, i, 0:1], rstd[:, i:i + 1], ALU.subtract, ALU.mult)
                ins.then_inc(vn_done, 1)
            for tb in range(TB):
                if tb == 0:
                    dve.wait_ge(row_lng, 16)
                dve.wait_ge(vn_done, TB)
                v = zA[:, tb, V_:V_ + AW]
                dve.tensor_tensor(v, v, lng, ALU.mult).then_inc(vn_done, 1)
            with dve.Fori(8, 10) as k:
                ada2(k)

            dve.wait_ge(lt_done, 1)
            chain(dve.tensor_scalar(lf[:, :], bank[:, 4, 0:2 * HEADS], 0.0, None, ALU.min))
            dve.tensor_tensor(lf[:, :], lf[:, :], lt[:, :], ALU.subtract).then_inc(lf_done, 2)

            def gate_u():
                for g in range(HEADS):
                    dve.wait_ge(sgu_done, g + 1 if g % 2 else g + 2)
                    u = zA[:, 0:TB, U_ + g * P:U_ + (g + 1) * P]
                    dve.scalar_tensor_tensor(out=u, in0=bank[:, 4 + g // 2, (g % 2) * SEQ:(g % 2 + 1) * SEQ].rearrange("p (t c) -> p t c", t=TB),
                                             scalar=bsT[:, g:g + 1], in1=u, op0=ALU.add, op1=ALU.mult).then_inc(ya_done, 1)

            def maxima(half):
                if half:
                    dve.wait_ge(pT_done, 4)
                for hh in range(4):
                    h = 4 * half + hh
                    dve.wait_ge(scores_done, h + 1)
                    dve.scalar_tensor_tensor(out=probs[:, hh, 0:P], in0=bank[:, 4 + hh, 0:P], scalar=cum[:, h:h + 1],
                                             in1=mask3[:, 0, :], op0=ALU.add, op1=ALU.add).then_inc(scored, 1)
                    dve.scalar_tensor_tensor(out=probs[:, hh, P:3 * P], in0=bank[:, 4 + hh, P:3 * P], scalar=cum[:, HEADS + h:HEADS + h + 1],
                                             in1=mask3[:, 1:3, :].rearrange("p b c -> p (b c)"), op0=ALU.add, op1=ALU.add).then_inc(scored, 1)
                for hh in range(4):
                    dve.wait_ge(scored, 8 * half + 2 * hh + 2)
                    dve.tensor_reduce(mx[:, 0, 2 * hh:2 * hh + 1], probs[:, hh, 0:P], AX.X, ALU.max).then_inc(scored_max, 1)
                    dve.tensor_reduce(mx[:, 0, 2 * hh + 1:2 * hh + 2], probs[:, hh, P:3 * P], AX.X, ALU.max).then_inc(scored_max, 1)
                dve.wait_ge(scored_max, 8 * half + 8)
                dve.tensor_scalar(mx[:, 1, :], mx[:, 0, :], -1.0, None, ALU.mult).then_inc(max_done, 1)

            def normalise(half):
                dve.wait_ge(exp_done, 8 * (half + 1))
                chain(dve.reciprocal(sums[:, :], sums[:, :]))
                for hh in range(4):
                    dve.tensor_scalar(probs[:, hh, 0:P], probs[:, hh, 0:P], sums[:, 2 * hh:2 * hh + 1], None, ALU.mult)
                    dve.tensor_scalar(probs[:, hh, P:3 * P], probs[:, hh, P:3 * P], sums[:, 2 * hh + 1:2 * hh + 2], None,
                                      ALU.mult).then_inc(probs_done, 1)

            ada2(10)
            ada2(11)
            ada2(12)
            gate_u()
            ada2(13)
            ada2(14)
            dve.wait_ge(cum_copied, 2)
            maxima(0)
            ada2(15)
            normalise(0)
            maxima(1)
            normalise(1)

            dve.wait_ge(modT_done, 1)
            dve.tensor_tensor(modrow[:, :], bank[0:4 * KD, 6, 0:P], bada2[:, :], ALU.add).then_inc(modrow_done, 1)

            for n in range(NPROJ):
                dve.wait_ge(main_used, 4 * (GM + n + 1))
                for tb in range(TB):
                    ga = zG[:, tb, n * COLS:(n + 1) * COLS]
                    gb = zG[:, tb, D + n * COLS:D + (n + 1) * COLS]
                    dve.tensor_tensor(ga, bank[:, 4 * (n % 2) + tb, :], ga, ALU.mult).then_inc(gated, 1)
                    dve.tensor_tensor(gb, bank[:, 4 * (n % 2) + 2 + tb, :], gb, ALU.mult).then_inc(gated, 1)
                for tb in range(TB):
                    ga = zG[:, tb, n * COLS:(n + 1) * COLS]
                    gb = zG[:, tb, D + n * COLS:D + (n + 1) * COLS]
                    dve.wait_ge(gated, 4 * n + 2 * tb + 2)
                    dve.tensor_tensor(ga, ga, gb, ALU.add).then_inc(merged_done, 1)

            dve.wait_ge(row_in["g1"], 16)
            for n in range(NPROJ):
                dve.wait_ge(main_used, 4 * (GM + NPROJ + n + 1))
                for tb in range(TB):
                    t = zG[:, tb, D + n * COLS:D + (n + 1) * COLS]
                    cols = slice(n * COLS, (n + 1) * COLS)
                    chain(dve.scalar_tensor_tensor(out=t, in0=g1_row[:, cols], scalar=1.0, in1=bank[:, 2 * (n % 2) + tb, :],
                                                   op0=ALU.add, op1=ALU.mult))
                    dve.scalar_tensor_tensor(out=x[:, tb, cols], in0=x[:, tb, cols], scalar=ALPHA, in1=t,
                                             op0=ALU.mult, op1=ALU.add).then_inc(res_done, 1)

            def norm_stats(t, tb, var):
                for i in range(4):
                    ins = dve.bn_stats(st[:, 4 * tb + i, :], t[:, tb, i * COLS:(i + 1) * COLS])
                chain(ins)
                chain(dve.bn_aggr(mv[:, tb, :], st[:, 4 * tb:4 * tb + 4, :].rearrange("p a b -> p (a b)")))
                dve.tensor_scalar(mv[:, tb, 1:2], mv[:, tb, 1:2], EPS, None, ALU.add).then_inc(var, 1)

            def norm_apply(t, tb, std, gain, bias):
                dve.wait_ge(std, tb + 1)
                row = t[:, tb, :]
                chain(dve.reciprocal(rstd[:, tb:tb + 1], rstd[:, tb:tb + 1]))
                chain(dve.tensor_scalar(row, row, mv[:, tb, 0:1], rstd[:, tb:tb + 1], ALU.subtract, ALU.mult))
                chain(dve.tensor_tensor(row, row, gain[:, :], ALU.mult))
                return dve.tensor_tensor(row, row, bias[:, :], ALU.add)

            dve.wait_ge(res_done, 2 * NPROJ)
            for tb in range(TB):
                norm_stats(x, tb, var1)
            dve.wait_ge(cols2_done, 1)
            for tb in range(TB):
                for name in ("ln1g", "ln1b", "sc2", "sh2"):
                    dve.wait_ge(row_in[name], 16)
                chain(norm_apply(x, tb, std1, ln1g, ln1b))
                chain(dve.scalar_tensor_tensor(out=h2[:, tb, :], in0=sc2_row[:, :], scalar=1.0, in1=x[:, tb, :],
                                               op0=ALU.add, op1=ALU.mult))
                dve.tensor_tensor(h2[:, tb, :], h2[:, tb, :], sh2_row[:, :], ALU.add).then_inc(h2_done, 1)
            for tb in range(TB):
                dve.wait_ge(h2hi_done, tb + 1)
                dve.tensor_tensor(h2lo[:, tb, :], h2[:, tb, :], h2hi[:, tb, :].bitcast(F32), ALU.subtract).then_inc(h2lo_done, 1)

            dve.wait_ge(logit_done, 1)
            chain(dve.tensor_copy(logit[:, :, :], bank[:, 0, 0:2 * E].rearrange("p (t e) -> p t e", t=TB)))
            for tb in range(TB):
                chain(dve.max(top[:, tb, :], logit[:, tb, :]))
                chain(dve.max_index(topi[:, tb, :], top[:, tb, :], logit[:, tb, :]))
                chain(dve.tensor_copy(topf[:, tb, :], topi[:, tb, :]))
                dve.tensor_scalar(tops[:, tb:tb + 1], top[:, tb, 0:1], -1.0, None, ALU.mult).then_inc(top_done, 1)
                dve.wait_ge(topw_done, tb + 1)
                chain(dve.reciprocal(tops[:, 2 + tb:3 + tb], tops[:, 2 + tb:3 + tb]))
                chain(dve.tensor_scalar(topw[:, tb, 0:TOPK], topw[:, tb, 0:TOPK], tops[:, 2 + tb:3 + tb], None, ALU.mult))
                for i in range(TOPK):
                    hot = expert_id[:, :], topf[:, tb, i:i + 1]
                    if i == 0:
                        chain(dve.tensor_scalar(mask[:, tb, :], *hot, None, ALU.is_equal))
                        chain(dve.tensor_scalar(comb[:, tb, 0:E], *hot, topw[:, tb, 0:1], ALU.is_equal, ALU.mult))
                    else:
                        chain(dve.tensor_scalar(onehot[:, :], *hot, None, ALU.is_equal))
                        chain(dve.tensor_tensor(mask[:, tb, :], mask[:, tb, :], onehot[:, :], ALU.add))
                        chain(dve.scalar_tensor_tensor(out=comb[:, tb, 0:E], in0=onehot[:, :], scalar=topw[:, tb, i:i + 1],
                                                       in1=comb[:, tb, 0:E], op0=ALU.mult, op1=ALU.add))
                dve.sem_inc(mask_done, 1)
                dve.sem_inc(comb_done, 1)

            def thrice(t):
                return t.unsqueeze(1).to_broadcast([P, OVER, E])

            for tb in range(TB):
                ins = dve.tensor_copy(mask96[:, tb, :].rearrange("p (b e) -> p b e", b=OVER), thrice(mask[:, tb, :]))
            ins.then_inc(over_masked, 1)
            for tb in range(TB):
                ins = dve.tensor_copy(pc96[:, TB + tb, :].rearrange("p (b e) -> p b e", b=OVER), thrice(comb[:, tb, 0:E]))
            ins.then_inc(over_tabled, 1)
            dve.wait_ge(pos_done, 1)
            chain(dve.scalar_tensor_tensor(out=pos1[:, :, 0:E], in0=bank[:, 1, 0:2 * E].rearrange("p (t e) -> p t e", t=TB),
                                           scalar=1.0, in1=mask[:, :, :], op0=ALU.add, op1=ALU.mult))
            dve.wait_ge(consts_made, NCONST)
            for b in range(OVER):
                ins = dve.tensor_scalar(pc96[:, 0:TB, b * E:(b + 1) * E], pos1[:, :, 0:E], -float((b + 1) * SLOTS), None, ALU.add)
            ins.then_inc(over_tabled, 1)
            dve.wait_ge(over_counted, 1)
            dve.tensor_scalar(flag96[:, :], bank[0:N96, 3, 0:1], least96[:, :], None, ALU.is_gt).then_inc(over_flagged, 1)
            dve.wait_ge(over_turned, 1)
            dve.tensor_copy(pc96T[:, :], bank[0:N96, 4, :]).then_inc(over_copied, 1)
            dve.wait_ge(over_ranked, 1)
            chain(dve.tensor_copy(rank96[:, :], bank[0:N96, 6, 0:1]))
            dve.tensor_scalar(place96[:, :], slot_id[0:N96, 0:EXTRA], rank96[:, :], flag96[:, :], ALU.is_equal, ALU.mult
                              ).then_inc(over_placed, 1)
            chain(dve.tensor_copy(n_over[:, :], bank[0:1, 6, 32:33]))
            chain(dve.tensor_scalar(halves[:, :], slot_id[0:1, 0:EXTRA:2], n_over[:, :], None, ALU.is_le))
            chain(dve.tensor_reduce(turns_f[:, :], halves[:, :], AX.X, ALU.add))
            dve.tensor_scalar(turns_i[:, :], turns_f[:, :], float(PAIRS - 1), None, ALU.add)
            dve.tensor_copy(task_i[:, 0:E], expert_id[0:1, :])
            dve.wait_ge(over_spread, 1)
            dve.tensor_copy(pos1[:, :, E:TASKS], bank[:, 5, 0:2 * EXTRA].rearrange("p (t j) -> p t j", t=TB))
            dve.tensor_copy(comb[:, :, E:TASKS], bank[:, 5, 2 * EXTRA:4 * EXTRA].rearrange("p (t j) -> p t j", t=TB))
            dve.tensor_copy(task_i[:, E:TASKS], bank[0:1, 5, 4 * EXTRA:5 * EXTRA]).then_inc(tables_done, 1)

            def select(X):
                for tb in range(TB):
                    ins = dve.tensor_scalar(sel[:, tb, :], slot_id[:, :], pos1[:, tb, bass.ds(X, 1)], None, ALU.is_equal)
                ins.then_inc(sel_ready, 1)

            def select_weighted(X, q):
                dve.wait_ge(selwT_filled, q + 1)
                for j in range(2):
                    for tb in range(TB):
                        ins = dve.tensor_scalar(selw[:, tb, j * SLOTS:(j + 1) * SLOTS], slot_id[:, :], pos1[:, tb, bass.ds(X + j, 1)],
                                                comb[:, tb, bass.ds(X + j, 1)], ALU.is_equal, ALU.mult)
                ins.then_inc(selw_ready, 1)

            def lo_part(X, m, i, first=False):
                s = i if first else (8 + 12 * m + i) % EXP_SLOTS
                dve.wait_ge(hi_ready, X * GU + (i + 1))
                if not (first and i < LO_SLOTS):
                    dve.wait_ge(unit_used, X * GU + (i + 1 - LO_SLOTS))
                dve.tensor_tensor(lo[i % LO_SLOTS][:, :, :], raw[s][:, :, :], hi[i % HI_SLOTS][:, :, :].bitcast(F32),
                                  ALU.subtract).then_inc(lo_ready, 1)

            def hsel_even(X):
                for b in (2, 4):
                    dve.wait_ge(gathered, X * 4 + (b - 1))
                    dve.tensor_copy(hsel[:, 4 * b - 8:4 * b - 4, :], bank[:, b, :]).then_inc(hsel_dve, 1)

            def add_back(q):
                for i in range(8):
                    tb, n = i // 4, i % 4
                    dve.wait_ge(scattered, q * 8 + (i + 1))
                    o = out_acc[:, tb, n * COLS:(n + 1) * COLS]
                    dve.tensor_tensor(o, o, bank[:, 7 if i % 2 == 0 else 6, :], ALU.add).then_inc(scatter_added, 1)

            def activate(X, e, parity):
                g, u = gate_up_T[:, 0:FC * SLOTS], gate_up_T[:, FC * SLOTS:2 * FC * SLOTS]
                bias = bgu[:, bass.ds(e, 1), :].rearrange("p a c -> p (a c)").unsqueeze(2).to_broadcast([P, 2 * FC, SLOTS])
                dve.wait_ge(tsum_done, X + 1)
                dve.tensor_tensor(gate_up_T.rearrange("p (c s) -> p c s", s=SLOTS),
                                  bank[:, 6, :].rearrange("p (c s) -> p c s", s=SLOTS), bias, ALU.add).then_inc(biased, 1)
                dve.wait_ge(biased, X + 1)
                dve.tensor_scalar(g, g, LIMIT, None, ALU.min).then_inc(gate_ready, 1)
                dve.tensor_scalar(u, u, LIMIT, -LIMIT, ALU.min, ALU.max).then_inc(up_ready, 1)
                dve.wait_ge(gate_ready, X + 1)
                dve.wait_ge(up_ready, X + 1)
                dve.scalar_tensor_tensor(out=u, in0=u, scalar=1.0, in1=g, op0=ALU.add, op1=ALU.mult).then_inc(gate_up, 1)
                dve.wait_ge(sig_ready, X + 1)
                dve.wait_ge(gate_up, X + 1)
                dve.tensor_tensor(act[parity][:, :], u, act[parity][:, :], ALU.mult).then_inc(act_ready, 1)

            dve.wait_ge(tables_done, 1)
            select(0)
            for i in range(LO_SLOTS):
                lo_part(0, 1, i, first=True)
            for i in range(8):
                dve.wait_ge(bias_done, i + 1)
                tb, n = i // 4, i % 4
                dve.tensor_copy(out_acc[:, tb, n * COLS:(n + 1) * COLS], bank[:, 7 if i % 2 == 0 else 0, :]).then_inc(bias_copied, 1)
            hsel_even(0)
            dve.wait_ge(gathered, 4)
            select(1)
            for i in range(LO_SLOTS, GU):
                lo_part(0, 1, i, first=True)
            hsel_even(1)
            activate(0, 0, 0)
            for i in range(LO_SLOTS):
                lo_part(1, 0, i)
            turns = dve.value_load(turns_i[0:1, 0:1], min_val=PAIRS - 1, max_val=PAIRS - 1 + EXTRA // 2)
            with dve.Fori(0, turns) as q:
                for m in range(2):
                    X = q * 2 + (m + 1)
                    e = dve.value_load(task_i[0:1, bass.ds(X, 1)], min_val=0, max_val=E - 1)
                    dve.wait_ge(gathered, X * 4 + 4)
                    select(X + 1)
                    if m == 1:
                        select_weighted(X - 2, q)
                    for i in range(LO_SLOTS, GU):
                        lo_part(X, m, i)
                    if m == 0:
                        add_back(q)
                    hsel_even(X + 1)
                    activate(X, e, 1 - m)
                    for i in range(LO_SLOTS):
                        lo_part(X + 1, 1 - m, i)
            last_task = turns * 2 + 1
            e = dve.value_load(task_i[0:1, bass.ds(last_task, 1)], min_val=0, max_val=E - 1)
            select_weighted(last_task - 1, turns)
            for i in range(LO_SLOTS, GU):
                lo_part(last_task, 0, i)
            add_back(turns)
            activate(last_task, e, 1)
            add_back(turns + 1)
            dve.wait_ge(scatter_added, turns * 8 + 16)

            for name in ("g2", "ln2g", "ln2b"):
                dve.wait_ge(row_in[name], 16)
            for tb in range(TB):
                o = out_acc[:, tb, :]
                chain(dve.scalar_tensor_tensor(out=o, in0=g2_row[:, :], scalar=1.0, in1=o, op0=ALU.add, op1=ALU.mult))
                chain(dve.scalar_tensor_tensor(out=o, in0=x[:, tb, :], scalar=ALPHA, in1=o, op0=ALU.mult, op1=ALU.add))
                norm_stats(out_acc, tb, var2)
            for tb in range(TB):
                norm_apply(out_acc, tb, std2, ln2g, ln2b).then_inc(out_ready, 1)


_INS = ['x', 'c', 'w_ada', 'b_ada', 'w_in', 'b_f', 'sgu_ln_g', 'spatial_w', 'spatial_b', 'w_proj_a', 'w_proj_b', 'w_o',
        'ln1_g', 'ln1_b', 'router_w', 'router_b', 'w_gate', 'b_gate', 'w_up', 'b_up', 'w_down', 'b_down', 'ln2_g', 'ln2_b']


def kernel(**inputs):
    import numpy as np
    import concourse.bacc as bacc
    from concourse.bass_utils import run_bass_kernel_spmd

    nc = bacc.Bacc("TRN2", target_bir_lowering=False, num_devices=1)
    arrays, args = {}, {}
    for name in _INS:
        a = np.ascontiguousarray(inputs[name])
        arrays[f"in_{name}"] = a
        args[name] = nc.dram_tensor(f"in_{name}", a.shape, mybir.dt.from_np(a.dtype), kind="ExternalInput").ap()
    out = nc.dram_tensor("out_0", (1, SEQ, D), F32, kind="ExternalOutput").ap()
    mod_dram = nc.dram_tensor("mod_rows", (4 * KD, P), F32).ap()
    layer(nc, args, mod_dram, out)
    r = run_bass_kernel_spmd(nc, [arrays], core_ids=[0])
    return r.results[0]["out_0"]
```

```python
from contextlib import ExitStack

import concourse.bass as bass
from concourse import mybir

F32 = mybir.dt.float32
F32R = mybir.dt.float32r
I32 = mybir.dt.int32
U32 = mybir.dt.uint32
ALU = mybir.AluOpType
ACT = mybir.ActivationFunctionType
AX = mybir.AxisListType

P = 128
D = 2048
SEQ = 256
TB = SEQ // P
KD = D // P
AW = 1024
HEADS = 8
E = 32
TOPK = 4
FE = 512
FC = FE // P
ALPHA = 2.0 ** 0.25
EPS = 1e-5
LIMIT = 7.0
SWI = 1.702
NEG = -1e30
SCALE = P ** -0.5
COLS = 512
SLOTS = 64
OVER = SEQ // SLOTS - 1
EXTRA = 16
TASKS = E + EXTRA + 2
GA = 10
GG = 8
F_COL = GA * COLS
RAW_SLOTS = 6
EXP_SLOTS = 8
HI_SLOTS = 4
LO_SLOTS = 4
GU = 8
TURN = GU + FC
KPU = 4
PAIRS = E // 2
KB = 1024
U_, V_, Q_, K_, VB_ = 0, AW, 2 * AW, 3 * AW, 4 * AW
NADA1 = 2 * KD
NPROJ = D // COLS


def layer(nc, A, mod_dram, x1_dram, out):
    ctx = ExitStack()
    with ctx:
        def sem(name):
            return ctx.enter_context(nc.semaphore(name))

        room = 207 * KB + 512
        ctx.enter_context(nc.sbuf_tensor("arena", [P, room // 4], F32))
        base = nc.sbuf_base - room
        cursor = [0]

        def place(name, shape, dt=F32, at=None):
            size = 4
            for n in shape[1:]:
                size *= n
            size = (size + 31) // 32 * 32
            if at is None:
                at = cursor[0]
                cursor[0] += size
            assert at + size <= room, (name, at + size, room)
            return nc.alloc_sbuf_tensor_at(name, shape, dt, offset=base + at)

        raw = [place(f"raw{s}", [P, KPU, COLS]) for s in range(RAW_SLOTS)]
        x = place("x", [P, TB, D])
        ident = place("ident", [P, P])
        ones = place("ones", [P, P])
        tri_incl = place("tri_incl", [P, P])
        tri_excl = place("tri_excl", [P, P])
        twin = place("twin", [P, SLOTS])
        slot_i = place("slot_i", [P, SLOTS], I32)
        slot_id = place("slot_id", [P, SLOTS])
        expert_i = place("expert_i", [P, E], I32)
        expert_id = place("expert_id", [P, E])
        bgu = place("bgu", [P, E, 2 * FC])
        pos1 = place("pos1", [P, TB, TASKS])
        comb = place("comb", [P, TB, TASKS])
        st = place("st", [P, 16, 6])
        mv = place("mv", [P, 16, 2])
        rstd = place("rstd", [P, 16])
        expert96_i = place("expert96_i", [OVER * E, 1], I32)
        expert96 = place("expert96", [OVER * E, 1])
        least96 = place("least96", [OVER * E, 1])
        task_i = place("task_i", [1, TASKS], I32)
        turns_i = place("turns_i", [1, 1], I32)
        turns_f = place("turns_f", [1, 1])
        rb_row = place("rb_row", [1, E])
        warm = place("warm", [P, 1])
        phase = cursor[0]

        hT = place("hT", [P, KD, SEQ])
        zA = place("zA", [P, TB, F_COL])
        zG = place("zG", [P, TB, GG * COLS])
        acc = place("acc", [P, 4, D])
        tmp = place("tmp", [P, 2, 1536])
        condT = place("condT", [P, KD])
        bada2 = place("bada2", [64, P])
        modrow = place("modrow", [64, P])
        modcol = place("modcol", [P, 64])
        mod1 = place("mod1", [P, 2 * KD])
        badaT = place("badaT", [P, 2 * KD])
        bsT = place("bsT", [P, HEADS])
        wf = place("wf", [P, KD, HEADS])
        bf_row = place("bf_row", [1, HEADS])
        lf = place("lf", [P, TB * HEADS])
        lt = place("lt", [P, TB * HEADS])
        cum = place("cum", [P, TB * HEADS])
        mx = place("mx", [P, 2, 8])
        sums = place("sums", [P, 8])
        cT = place("cT", [P, 2, KD])
        o_hT = phase
        o_zA = o_hT + 16 * KB
        o_zG = o_zA + 40 * KB
        o_acc = o_zG + 32 * KB
        o_tmp = o_acc + 32 * KB
        o_end = o_tmp + 12 * KB
        acc1 = place("acc1", [P, 2, D], at=o_zG)
        mask3 = place("mask3", [P, 3, P])
        cumT = place("cumT", [HEADS, SEQ])
        probs = tmp[:, 1, :].rearrange("p (h c) -> p h c", h=4)
        probsT = tmp[:, 0, :].rearrange("p (h c) -> p h c", h=4)
        wsT = tmp[:, 0, 0:HEADS * P].rearrange("p (g t) -> p g t", g=HEADS)
        lng = tmp[:, 1, 0:AW]
        ws_raw = place("ws_raw", [P, HEADS, P], at=o_acc)
        c_rows = place("c_rows", [KD, P], at=o_acc + 4 * KB)
        bada_rows = place("bada_rows", [2 * KD, P], at=o_acc + 5 * KB)
        bs_rows = place("bs_rows", [HEADS, P], at=o_acc + 6 * KB)
        bg_rows = place("bg_rows", [P, P], at=o_acc + 7 * KB)
        bu_rows = place("bu_rows", [P, P], at=o_acc + 8 * KB)

        g1_row, ln1g, sc2_row, sh2_row, ln1b = [
            place(f"row_{n}", [P, D], at=o_zA + i * 8 * KB) for n, i in (("g1", 0), ("ln1g", 1), ("sc2", 2), ("sh2", 3), ("ln1b", 5))]
        h2 = place("h2", [P, TB, D], at=o_acc)
        h2T = place("h2T", [P, KD, SEQ], at=o_zG + 16 * KB)
        rw = place("rw", [P, KD, E], at=o_tmp)
        bdown = place("bdown", [E, D], at=o_hT + 112 * KB)
        logit = place("logit", [P, TB, E], at=o_tmp + 2 * KB)
        mask = place("mask", [P, TB, E], at=o_tmp + 2 * KB + 256)
        onehot = place("onehot", [P, E], at=o_tmp + 2 * KB + 512)
        tops = place("tops", [P, 4], at=o_tmp + 2 * KB + 640)
        top = place("top", [P, TB, 8], at=o_tmp + 2 * KB + 768)
        topi = place("topi", [P, TB, 8], U32, at=o_tmp + 2 * KB + 832)
        topf = place("topf", [P, TB, 8], at=o_tmp + 2 * KB + 896)
        topw = place("topw", [P, TB, 8], at=o_tmp + 2 * KB + 960)
        combT = place("combT", [E, SEQ], at=o_hT + 136 * KB)
        N96 = OVER * E
        o_over = o_hT + 16 * KB
        pc96 = place("pc96", [P, 2 * TB, N96], at=o_over)
        mask96 = place("mask96", [P, TB, N96], at=o_over + 2 * KB)
        pc96T = place("pc96T", [N96, 2 * SEQ], at=o_over + 3 * KB)
        flag96 = place("flag96", [N96, 1], at=o_over + 5 * KB)
        rank96 = place("rank96", [N96, 1], at=o_over + 5 * KB + 32)
        place96 = place("place96", [N96, EXTRA], at=o_over + 5 * KB + 64)
        n_over = place("n_over", [1, 1], at=o_over + 5 * KB + 128)
        halves = place("halves", [1, EXTRA // 2], at=o_over + 5 * KB + 160)

        out_acc = place("out_acc", [P, TB, D], at=o_hT + 16 * KB)
        hi = [place(f"hi{s}", [P, KPU, COLS], F32R, at=o_hT + (32 + 8 * s) * KB) for s in range(HI_SLOTS)]
        lo = [place(f"lo{s}", [P, KPU, COLS], F32R, at=o_hT + o * KB) for s, o in enumerate((0, 8, 64, 72))]
        raw += [place(f"raw{6 + s}", [P, KPU, COLS], at=o_hT + o * KB) for s, o in enumerate((104, 80))]
        y = place("y", [P, D], at=o_hT + 112 * KB)
        hsel = place("hsel", [P, KD, P], F32R, at=o_hT + 120 * KB)
        gu_sb = place("gu_sb", [P, 2, FE], at=o_hT + 128 * KB)
        gate_up_T = gu_sb[:, 0, :]
        act = place("act", [P, FC * SLOTS], at=o_hT + 132 * KB)
        sel = place("sel", [P, TB, P], at=o_hT + 133 * KB)
        selw = place("selw", [P, TB, P], at=o_hT + 134 * KB)
        selwT = place("selwT", [P, SEQ], at=o_hT + 135 * KB)
        pair = place("pair", [P, KD, P], at=RAW_SLOTS * 8 * KB)
        x1_back = place("x1_back", [P, D], at=o_hT + 56 * KB)
        g2_row, ln2g, ln2b = [place(f"row_{n}", [P, D], at=o_hT + (32 + 8 * i) * KB) for i, n in enumerate(["g2", "ln2g", "ln2b"])]

        bank = ctx.enter_context(nc.psum_tensor("bank", [P, 8, COLS], F32))

        c_loaded = sem("c_loaded")
        x_loaded = sem("x_loaded")
        rows_loaded = sem("rows_loaded")
        landed = [sem(f"landed{s}") for s in range(EXP_SLOTS)]
        consts_made = sem("consts_made")
        acc1_zeroed = sem("acc1_zeroed")
        acc_zeroed = sem("acc_zeroed")
        ws_masked = sem("ws_masked")
        row_lng = sem("row_lng")
        wf_loaded = sem("wf_loaded")
        v_stat = sem("v_stat")
        v_agg = sem("v_agg")
        scored = sem("scored")
        scored_max = sem("scored_max")
        gated = sem("gated")
        loads_begun = sem("loads_begun")
        cT_done = sem("cT_done")
        sig_c = sem("sig_c")
        cond_done = sem("cond_done")
        rowsT_done = sem("rowsT_done")
        rowsT_copied = sem("rowsT_copied")
        xT_done = sem("xT_done")
        xT_copied = sem("xT_copied")
        ada1_done = sem("ada1_done")
        ada2_done = sem("ada2_done")
        ada1_cols = sem("ada1_cols")
        mod1_done = sem("mod1_done")
        h_done = sem("h_done")
        main_used = sem("main_used")
        z_copied = sem("z_copied")
        dve_step = sem("dve_step")
        act_step = sem("act_step")
        pool_step = sem("pool_step")
        v_var = sem("v_var")
        v_std = sem("v_std")
        vn_done = sem("vn_done")
        f_done = sem("f_done")
        lt_done = sem("lt_done")
        lf_done = sem("lf_done")
        qkT_done = sem("qkT_done")
        qkT_copied = sem("qkT_copied")
        sgu_done = sem("sgu_done")
        ya_done = sem("ya_done")
        cum_done = sem("cum_done")
        cum_copied = sem("cum_copied")
        scores_done = sem("scores_done")
        max_done = sem("max_done")
        exp_done = sem("exp_done")
        probs_done = sem("probs_done")
        pT_done = sem("pT_done")
        pT_copied = sem("pT_copied")
        oT_done = sem("oT_done")
        oT_copied = sem("oT_copied")
        yaT_done = sem("yaT_done")
        yaT_copied = sem("yaT_copied")
        cols2_done = sem("cols2_done")
        cols2_copied = sem("cols2_copied")
        modT_done = sem("modT_done")
        modrow_done = sem("modrow_done")
        mod_stored = sem("mod_stored")
        merged_done = sem("merged_done")
        mT_done = sem("mT_done")
        mT_copied = sem("mT_copied")
        row_in = {n: sem(f"in_{n}") for n in ("g1", "ln1g", "ln1b", "sc2", "sh2", "rw", "rb", "bdown", "g2", "ln2g", "ln2b")}
        res_done = sem("res_done")
        var1 = sem("var1")
        std1 = sem("std1")
        h2_done = sem("h2_done")
        h2T_done = sem("h2T_done")
        h2T_copied = sem("h2T_copied")
        logit_done = sem("logit_done")
        top_done = sem("top_done")
        topw_done = sem("topw_done")
        mask_done = sem("mask_done")
        pos_done = sem("pos_done")
        comb_done = sem("comb_done")
        combT_done = sem("combT_done")
        combT_copied = sem("combT_copied")
        bias_done = sem("bias_done")
        bias_copied = sem("bias_copied")
        over_masked = sem("over_masked")
        over_counted = sem("over_counted")
        over_flagged = sem("over_flagged")
        over_ranked = sem("over_ranked")
        over_placed = sem("over_placed")
        over_tabled = sem("over_tabled")
        over_turned = sem("over_turned")
        over_copied = sem("over_copied")
        over_spread = sem("over_spread")
        tables_done = sem("tables_done")
        hi_ready = sem("hi_ready")
        lo_ready = sem("lo_ready")
        unit_used = sem("unit_used")
        down_used = sem("down_used")
        sel_ready = sem("sel_ready")
        gathered = sem("gathered")
        pair_copied = sem("pair_copied")
        x1_done = sem("x1_done")
        x1_stored = sem("x1_stored")
        x1_loaded = sem("x1_loaded")
        hsel_hi = sem("hsel_hi")
        hsel_lo = sem("hsel_lo")
        gu_copied = sem("gu_copied")
        tsum_done = sem("tsum_done")
        biased = sem("biased")
        gate_ready = sem("gate_ready")
        up_ready = sem("up_ready")
        gate_up = sem("gate_up")
        sig_ready = sem("sig_ready")
        act_ready = sem("act_ready")
        y_filled = sem("y_filled")
        selw_ready = sem("selw_ready")
        selwT_done = sem("selwT_done")
        selwT_filled = sem("selwT_filled")
        scattered = sem("scattered")
        scatter_added = sem("scatter_added")
        var2 = sem("var2")
        std2 = sem("std2")
        out_ready = sem("out_ready")
        out_stored = sem("out_stored")

        NCONST = 10
        n_rows = 7

        def ada_unit(k, j):
            return A["w_ada"][0, bass.ts(k, P), j * D:(j + 1) * D]

        def win_unit(g, u, gates=False):
            col = g * COLS + (HEADS if gates else 0)
            return A["w_in"][0, u * COLS:(u + 1) * COLS, bass.ds(col, COLS)].rearrange("(k p) f -> p k f", p=P)

        def square_unit(w, n, u):
            return w[0, u * COLS:(u + 1) * COLS, n * COLS:(n + 1) * COLS].rearrange("(k p) f -> p k f", p=P)

        def gu_unit(e, i):
            w = A["w_gate"] if i % 2 == 0 else A["w_up"]
            r = (i // 2) * KPU * P
            return w[0, e, r:r + KPU * P, :].rearrange("(k p) f -> p k f", p=P)

        def down_unit(e, c):
            return A["w_down"][0, e, c * P:(c + 1) * P, :].rearrange("p (n f) -> p n f", n=KPU)

        def flat(slot):
            return slot[:, :, :].rearrange("p k f -> p (k f)")

        MAIN_FILLS = NADA1 // RAW_SLOTS
        ADA_FILLS = NADA1 // RAW_SLOTS + 1
        PLAN = {0: (0, 4), 1: (0, 5), 2: (-1, 0), 3: (0, 6), 4: (0, 7), 5: (-1, 1),
                6: (1, 0), 7: (1, 1), 8: (-1, 2), 9: (1, 2), 10: (1, 3), 11: (-1, 3)}
        LAST_PLAN = {0: (0, 4), 1: (0, 5), 2: (-1, 0), 3: (0, 6), 4: (0, 7), 5: (-1, 1), 6: (-1, 2), 7: (-1, 3)}
        TAIL_DOWN = [8, 9, 10, 11]
        LO_BEHIND = {0: 0, 2: 1, 3: 2, 5: 3, 6: 4, 8: 5, 9: 6, 11: 7}
        DOWN_BEHIND = {1: -3, 4: -2, 7: -1, 10: 0}

        def place_of(plan, unit):
            return [j for j, u in plan.items() if u == unit][0]

        EXP_FILLS = [ADA_FILLS + 2 * KD] * 2 + [MAIN_FILLS + GA + GG + 2 * NPROJ] * 4 + [0] * 2
        GM = GA + GG

        block = ctx.enter_context(nc.Block())

        @block.sync
        def _(sp):
            def ada1_load(i, m):
                sp.dma_start(flat(raw[m]), ada_unit(3 * i + m // 2, m % 2)).then_inc(landed[m], 16)

            for m in range(RAW_SLOTS):
                ada1_load(0, m)
            with sp.Fori(1, NADA1 // RAW_SLOTS) as i:
                for m in range(RAW_SLOTS):
                    sp.wait_ge(ada1_done, i * RAW_SLOTS + m - 5)
                    ada1_load(i, m)
            for m in range(2):
                sp.wait_ge(ada1_done, NADA1 - 2 + m - 5)
                ada1_load(NADA1 // RAW_SLOTS, m)

            def mixer_loads(g, gates, ada):
                first = isinstance(g, int) and g == 0
                for u in range(4):
                    if first:
                        sp.wait_ge(ada1_done, NADA1 - RAW_SLOTS + u + 1)
                    else:
                        sp.wait_ge(main_used, 4 * g + u - 3)
                    sp.dma_start(raw[2 + u][:, :, :], win_unit(g, u, gates)).then_inc(landed[2 + u], 16)
                    if ada:
                        j = u
                        if first and j < 2:
                            sp.wait_ge(ada1_done, NADA1 - 1 + j)
                        else:
                            sp.wait_ge(ada2_done, 4 * g + j - 1)
                        sp.dma_start(flat(raw[j % 2]), ada_unit(g, 2 + j)).then_inc(landed[j % 2], 16)

            mixer_loads(0, False, True)
            with sp.Fori(1, GA) as g:
                mixer_loads(g, False, True)
            for g in range(GA, GM):
                mixer_loads(g, True, g < KD)
            for n in range(NPROJ):
                for u in range(4):
                    sp.wait_ge(main_used, 4 * (GM + n) + u - 3)
                    w = A["w_proj_a"] if u < 2 else A["w_proj_b"]
                    sp.dma_start(raw[2 + u][:, :, :], square_unit(w, n, u % 2)).then_inc(landed[2 + u], 16)
            for n in range(NPROJ):
                for u in range(4):
                    sp.wait_ge(main_used, 4 * (GM + NPROJ + n) + u - 3)
                    sp.dma_start(raw[2 + u][:, :, :], square_unit(A["w_o"], n, u)).then_inc(landed[2 + u], 16)

            def task_load(s, src):
                sp.dma_start(raw[s][:, :, :], src).then_inc(landed[s], 16)

            sp.wait_ge(ada2_done, 4 * KD)
            for i in range(GU):
                if 2 <= i < RAW_SLOTS:
                    sp.wait_ge(main_used, 4 * (GM + 2 * NPROJ) - RAW_SLOTS + i + 1)
                if i == RAW_SLOTS:
                    sp.wait_ge(cols2_done, 1)
                if i == RAW_SLOTS + 1:
                    sp.wait_ge(logit_done, TB)
                task_load(i, gu_unit(0, i))
            for i in range(GU // 2):
                sp.wait_ge(lo_ready, i + 1)
                task_load(i, gu_unit(1, i))

            def expert_of(X):
                return sp.value_load(task_i[0:1, bass.ds(X, 1)], min_val=0, max_val=E - 1)

            def await_slot(X, j):
                if j in DOWN_BEHIND:
                    sp.wait_ge(down_used, X * FC + (DOWN_BEHIND[j] + 1))
                else:
                    sp.wait_ge(lo_ready, X * GU + LO_BEHIND[j])

            def turn_loads(X, m, plan):
                experts = {k: expert_of(X + k) for k in sorted({k for k, _ in plan.values()})}
                for j, (k, i) in plan.items():
                    await_slot(X, j)
                    if (k == -1 and i == 0) or (k == 1 and i < 2):
                        sp.sem_inc(loads_begun, 1)
                    task_load((TURN * (m + 1) + j) % EXP_SLOTS, down_unit(experts[k], i) if k == -1 else gu_unit(experts[k], i))

            sp.wait_ge(tables_done, 1)
            turns = sp.value_load(turns_i[0:1, 0:1], min_val=PAIRS - 1, max_val=PAIRS - 1 + EXTRA // 2)
            with sp.Fori(0, turns) as q:
                for m in range(2):
                    turn_loads(q * 2 + (m + 1), m, PLAN)
            last = turns * 2 + 1
            turn_loads(last, 0, LAST_PLAN)
            e = expert_of(last)
            for c, j in enumerate(TAIL_DOWN):
                await_slot(last, j)
                if c == 0:
                    sp.sem_inc(loads_begun, 1)
                task_load((TURN + j) % EXP_SLOTS, down_unit(e, c))
            sp.wait_ge(unit_used, last * GU + GU)
            for name, dst, src in [("g2", g2_row, mod_dram[3 * KD:4 * KD, :].rearrange("k c -> (k c)")),
                                   ("ln2g", ln2g, A["ln2_g"][0, :]), ("ln2b", ln2b, A["ln2_b"][0, :])]:
                sp.dma_start(dst[:, :], src.partition_broadcast(P)).then_inc(row_in[name], 16)
            sp.wait_ge(x1_stored, 16)
            sp.dma_start(x1_back[:, :], x1_dram[:, :]).then_inc(x1_loaded, 16)
            for tb in range(TB):
                sp.wait_ge(out_ready, tb + 1)
                sp.dma_start(out[0, tb * P:(tb + 1) * P, :], out_acc[:, tb, :]).then_inc(out_stored, 16)
            sp.wait_ge(out_stored, 16 * TB)

        @block.gpsimd
        def _(pool):
            steps = [0]

            def chain(ins):
                steps[0] += 1
                ins.then_inc(pool_step, 1)
                pool.wait_ge(pool_step, steps[0])

            def keep(t, op, base, partition, pattern, fill=0.0):
                return pool.affine_select(out=t, in_=t, compare_op=op, fill=fill, base=base, pattern=pattern,
                                          channel_multiplier=partition)

            pool.memset(acc1[:, :, :], 0.0).then_inc(acc1_zeroed, 1)
            chain(pool.memset(ident[:, :], 0.0))
            keep(ident[:, :], ALU.not_equal, 0, 1, [[-1, P]], 1.0).then_inc(consts_made, 1)
            pool.memset(ones[:, :], 1.0).then_inc(consts_made, 1)
            chain(pool.memset(tri_incl[:, :], 1.0))
            keep(tri_incl[:, :], ALU.is_ge, 0, -1, [[1, P]]).then_inc(consts_made, 1)
            chain(pool.memset(tri_excl[:, :], 1.0))
            keep(tri_excl[:, :], ALU.is_gt, 0, -1, [[1, P]]).then_inc(consts_made, 1)
            chain(pool.memset(twin[:, :], 0.0))
            chain(keep(twin[:, :], ALU.not_equal, 0, 1, [[-1, SLOTS]], 1.0))
            keep(twin[:, :], ALU.not_equal, -SLOTS, 1, [[-1, SLOTS]], 1.0).then_inc(consts_made, 1)
            chain(pool.iota(slot_i[:, :], pattern=[[1, SLOTS]], base=1, channel_multiplier=0))
            pool.tensor_copy(slot_id[:, :], slot_i[:, :]).then_inc(consts_made, 1)
            chain(pool.iota(expert_i[:, :], pattern=[[1, E]], base=0, channel_multiplier=0))
            pool.tensor_copy(expert_id[:, :], expert_i[:, :]).then_inc(consts_made, 1)
            for b in range(OVER):
                rows = slice(b * E, (b + 1) * E)
                chain(pool.iota(expert96_i[rows, :], pattern=[[1, 1]], base=0, channel_multiplier=1))
                chain(pool.memset(least96[rows, :], float((b + 1) * SLOTS)))
            pool.tensor_copy(expert96[:, :], expert96_i[:, :]).then_inc(consts_made, 1)
            chain(pool.memset(mask3[:, :, :], 0.0))
            for b in (0, 2):
                keep(mask3[:, b, :], ALU.is_ge, 0, 1, [[-1, P]], NEG).then_inc(consts_made, 1)

            pool.wait_ge(rowsT_done, 1)
            for j in range(4):
                pool.memset(acc[:, j, :], 0.0).then_inc(acc_zeroed, 1)
            pool.wait_ge(rowsT_copied, 3)
            for g in range(HEADS):
                keep(wsT[:, g, :], ALU.is_ge, 0, -1, [[1, P]]).then_inc(ws_masked, 1)

            pool.wait_ge(modrow_done, 1)
            pool.dma_start(mod_dram[:, :], modrow[:, :]).then_inc(mod_stored, 16)
            pool.wait_ge(mod_stored, 16)
            pool.wait_ge(main_used, 4 * (GM + NPROJ))
            for name, dst, src in [("g1", g1_row, mod_dram[0:KD, :].rearrange("k c -> (k c)")),
                                   ("ln1g", ln1g, A["ln1_g"][0, :]),
                                   ("sc2", sc2_row, mod_dram[2 * KD:3 * KD, :].rearrange("k c -> (k c)")),
                                   ("sh2", sh2_row, mod_dram[KD:2 * KD, :].rearrange("k c -> (k c)")),
                                   ("ln1b", ln1b, A["ln1_b"][0, :])]:
                if name == "ln1b":
                    pool.wait_ge(mT_done, 2 * NPROJ)
                pool.dma_start(dst[:, :], src.partition_broadcast(P)).then_inc(row_in[name], 16)
            pool.dma_start(rw[:, :, :], A["router_w"][0].rearrange("(k p) e -> p k e", p=P)).then_inc(row_in["rw"], 16)
            pool.dma_start(rb_row[:, :], A["router_b"][0:1, :]).then_inc(row_in["rb"], 16)
            pool.dma_start(bdown[:, :], A["b_down"][0]).then_inc(row_in["bdown"], 16)

            pool.memset(selwT[:, :], 0.0).then_inc(selwT_filled, 1)
            pool.wait_ge(x1_done, 1)
            pool.dma_start(x1_dram[:, :], x[:, 0, :]).then_inc(x1_stored, 16)
            pool.wait_ge(bias_done, 8)
            for n in range(4):
                pool.memset(y[:, n * COLS:(n + 1) * COLS], 0.0).then_inc(y_filled, 1)

        @block.tensor
        def _(pe):
            def T(dst, src, rows=P):
                return pe.transpose(dst, src, ident[0:rows, 0:rows])

            pe.wait_ge(consts_made, 1)
            pe.wait_ge(c_loaded, 16)
            T(bank[:, 0, 0:KD], c_rows[:, :], KD).then_inc(cT_done, 1)
            pe.wait_ge(rows_loaded, 16 * n_rows)
            T(bank[:, 1, 0:2 * KD], bada_rows[:, :], 2 * KD)
            T(bank[:, 1, 32:32 + HEADS], bs_rows[:, :], HEADS)
            T(bank[:, 1, P:2 * P], bg_rows[:, :])
            T(bank[:, 1, 2 * P:3 * P], bu_rows[:, :])
            for g in range(HEADS):
                last = T(bank[:, 2 + g // 4, (g % 4) * P:(g % 4 + 1) * P], ws_raw[:, g, :])
            last.then_inc(rowsT_done, 1)
            pe.wait_ge(x_loaded, 16)
            for b in range(8):
                if b == 4:
                    pe.wait_ge(sig_c, 1)
                    pe.wait_ge(rowsT_copied, 3)
                for i in range(4):
                    k, tb = 2 * b + i // 2, i % 2
                    last = T(bank[:, (4 + b) % 8, i * P:(i + 1) * P], x[:, tb, k * P:(k + 1) * P])
                last.then_inc(xT_done, 1)

            pe.wait_ge(consts_made, 2)
            pe.wait_ge(xT_copied, 8)
            pe.wait_ge(ada1_done, NADA1)
            for j in range(2):
                for k in range(KD):
                    last = pe.matmul(bank[:, 0, j * KD + k:j * KD + k + 1], acc1[:, j, k * P:(k + 1) * P], ones[:, 0:1],
                                     start=True, stop=True)
            last.then_inc(ada1_cols, 1)

            def main_unit(G, u):
                pe.wait_ge(landed[2 + u], (G + MAIN_FILLS + 1) * 16)

            def group(G, lhsT, banks):
                for u in range(4):
                    main_unit(G, u)
                    if isinstance(G, int) and G == 0:
                        pe.wait_ge(h_done, 4 * (u + 1))
                    for tb in range(TB):
                        for kk in range(KPU):
                            last = pe.matmul(bank[:, banks[tb], :], lhsT[:, u * KPU + kk, tb * P:(tb + 1) * P],
                                             raw[2 + u][:, kk, :], start=(u == 0 and kk == 0),
                                             stop=(u == 3 and kk == KPU - 1))
                    last.then_inc(main_used, 1)

            def win_group(G, parity):
                if not (isinstance(G, int) and G < 2):
                    pe.wait_ge(z_copied, G * 2 - 2)
                group(G, hT, [2 * parity, 2 * parity + 1])

            pe.wait_ge(mod1_done, 1)
            for G in range(2):
                win_group(G, G)
            with pe.Fori(1, GA // 2) as i:
                for parity in range(2):
                    win_group(i * 2 + parity, parity)

            pe.wait_ge(wf_loaded, 16)
            for tb in range(TB):
                for k in range(KD):
                    pe.matmul(bank[:, 4, tb * HEADS:(tb + 1) * HEADS], hT[:, k, tb * P:(tb + 1) * P], wf[:, k, :],
                              start=(k == 0), stop=False)
                last = pe.matmul(bank[:, 4, tb * HEADS:(tb + 1) * HEADS], ones[0:1, :], bf_row[:, :], start=False, stop=True)
            last.then_inc(f_done, 1)

            def qkT(half):
                for h in range(4 * half, 4 * half + 4):
                    b = 4 + h % 4
                    if h == 0:
                        pe.wait_ge(z_copied, 2 * GA)
                        pe.wait_ge(lt_done, 1)
                        pe.wait_ge(lf_done, 1)
                    if h >= 4:
                        pe.wait_ge(qkT_copied, 2 * (h - 4) + 2)
                    for i, off in enumerate((Q_, Q_, K_, K_)):
                        last = T(bank[:, b, i * P:(i + 1) * P], zA[:, i % 2, off + h * P:off + (h + 1) * P])
                    last.then_inc(qkT_done, 1)

            def sgu():
                pe.wait_ge(vn_done, 2 * TB)
                pe.wait_ge(ws_masked, HEADS)
                pe.wait_ge(qkT_copied, 2 * HEADS)
                for g in range(HEADS):
                    pe.matmul(bank[:, 4 + g // 2, (g % 2) * SEQ:(g % 2 + 1) * SEQ], wsT[:, g, :],
                              zA[:, 0:TB, V_ + g * P:V_ + (g + 1) * P], start=True, stop=True).then_inc(sgu_done, 1)

            def cumulate():
                pe.wait_ge(ya_done, HEADS)
                pe.wait_ge(lf_done, 2)
                l0, l1 = lf[:, 0:HEADS], lf[:, HEADS:2 * HEADS]
                pe.matmul(bank[:, 4, 0:HEADS], tri_incl[:, :], l0, start=True, stop=True)
                pe.matmul(bank[:, 4, HEADS:2 * HEADS], ones[:, :], l0, start=True, stop=False)
                pe.matmul(bank[:, 4, HEADS:2 * HEADS], tri_incl[:, :], l1, start=False, stop=True)
                pe.matmul(bank[0:HEADS, 5, 0:P], l0, tri_incl[:, :], start=True, stop=True)
                pe.matmul(bank[0:HEADS, 5, P:SEQ], l0, ones[:, :], start=True, stop=False)
                pe.matmul(bank[0:HEADS, 5, P:SEQ], l1, tri_incl[:, :], start=False, stop=True).then_inc(cum_done, 1)

            def scores(half):
                pe.wait_ge(cum_copied, 2)
                if half:
                    pe.wait_ge(oT_copied, 4)
                for hh in range(4):
                    h = 4 * half + hh
                    for tb in range(TB):
                        o = bank[:, 4 + hh, tb * P:tb * P + (tb + 1) * P]
                        pe.matmul(o, zA[:, tb, Q_ + h * P:Q_ + (h + 1) * P], zA[:, 0:tb + 1, K_ + h * P:K_ + (h + 1) * P],
                                  start=True, stop=False)
                        last = pe.matmul(o, ident[0:HEADS, h:h + 1].to_broadcast([HEADS, P]), cumT[:, 0:(tb + 1) * P],
                                         start=False, stop=True)
                    last.then_inc(scores_done, 1)

            def probsT_of(half):
                for hh in range(4):
                    pe.wait_ge(probs_done, 4 * half + hh + 1)
                    for b in range(3):
                        last = T(bank[:, 4 + hh, b * P:(b + 1) * P], probs[:, hh, b * P:(b + 1) * P])
                    last.then_inc(pT_done, 1)

            def oT(half):
                for hh in range(4):
                    h = 4 * half + hh
                    pe.wait_ge(pT_copied, h + 1)
                    pe.matmul(bank[:, 4 + hh, 0:SEQ], zA[:, 0, VB_ + h * P:VB_ + (h + 1) * P], probsT[:, hh, 0:SEQ],
                              start=True, stop=False)
                    pe.matmul(bank[:, 4 + hh, P:SEQ], zA[:, 1, VB_ + h * P:VB_ + (h + 1) * P], probsT[:, hh, SEQ:3 * P],
                              start=False, stop=True).then_inc(oT_done, 1)

            def yaT():
                pe.wait_ge(z_copied, 2 * GM)
                for b in range(4):
                    for i in range(4):
                        tb, c = i // 2, 2 * b + i % 2
                        last = T(bank[:, b, i * P:(i + 1) * P], zA[:, tb, U_ + c * P:U_ + (c + 1) * P])
                    last.then_inc(yaT_done, 1)

            after = {10: [lambda: qkT(0)], 11: [lambda: qkT(1)], 12: [sgu], 13: [cumulate], 14: [lambda: scores(0)],
                     15: [lambda: probsT_of(0)], 16: [lambda: oT(0), lambda: scores(1)],
                     17: [lambda: probsT_of(1), yaT, lambda: oT(1)]}
            for G in range(GA, GM):
                win_group(G, G % 2)
                for stage in after[G]:
                    stage()

            pe.wait_ge(oT_copied, 8)
            pe.wait_ge(ada2_done, 4 * KD)
            for j in range(4):
                for k in range(KD):
                    last = pe.matmul(bank[:, 7, j * KD + k:j * KD + k + 1], acc[:, j, k * P:(k + 1) * P], ones[:, 0:1],
                                     start=True, stop=True)
            last.then_inc(cols2_done, 1)

            def project(n):
                s = 4 * (n % 2)
                if n == 0:
                    pe.wait_ge(yaT_copied, 4)
                if n == 1:
                    pe.wait_ge(modrow_done, 1)
                if n >= 2:
                    pe.wait_ge(mT_copied, 2 * (n - 1))
                for u in range(4):
                    main_unit(GM + n, u)
                    off = V_ if u < 2 else Q_
                    for tb in range(TB):
                        for kk in range(KPU):
                            c = (u % 2) * KPU + kk
                            last = pe.matmul(bank[:, s + 2 * (u // 2) + tb, :], zA[:, tb, off + c * P:off + (c + 1) * P],
                                             raw[2 + u][:, kk, :], start=(c == 0), stop=(c == 7))
                    last.then_inc(main_used, 1)

            def mergedT(n):
                s = 4 * (n % 2)
                pe.wait_ge(merged_done, 2 * (n + 1))
                for b in range(2):
                    for i in range(4):
                        k, tb = 2 * b + i // 2, i % 2
                        last = T(bank[:, s + b, i * P:(i + 1) * P], zG[:, tb, n * COLS + k * P:n * COLS + (k + 1) * P])
                    last.then_inc(mT_done, 1)

            for n in range(NPROJ):
                project(n)
                if n == 0:
                    pe.wait_ge(cols2_copied, 1)
                    T(bank[0:4 * KD, 6, 0:P], modcol[:, :]).then_inc(modT_done, 1)
                if n:
                    mergedT(n - 1)
            mergedT(NPROJ - 1)

            for n in range(NPROJ):
                if n == 0:
                    pe.wait_ge(mT_copied, 2 * NPROJ)
                if n >= 2:
                    pe.wait_ge(res_done, 2 * (n - 1))
                group(GM + NPROJ + n, hT, [2 * (n % 2), 2 * (n % 2) + 1])

            pe.wait_ge(res_done, 2 * NPROJ)
            for tb in range(TB):
                pe.wait_ge(h2_done, tb + 1)
                for b in range(4):
                    for i in range(4):
                        k = 4 * b + i
                        last = T(bank[:, 4 * tb + b, i * P:(i + 1) * P], h2[:, tb, k * P:(k + 1) * P])
                    last.then_inc(h2T_done, 1)
            for tb in range(TB):
                pe.wait_ge(h2T_copied, 4 * (tb + 1))
                if tb == 0:
                    pe.wait_ge(row_in["rw"], 16)
                    pe.wait_ge(row_in["rb"], 16)
                for k in range(KD):
                    pe.matmul(bank[:, tb, 0:E], h2T[:, k, tb * P:(tb + 1) * P], rw[:, k, :],
                              start=(k == 0), stop=False)
                pe.matmul(bank[:, tb, 0:E], ones[0:1, :], rb_row[:, :], start=False, stop=True).then_inc(logit_done, 1)
            pe.wait_ge(mask_done, 2)
            pe.matmul(bank[:, 1, 0:E], tri_excl[:, :], mask[:, 0, :], start=True, stop=True)
            pe.matmul(bank[:, 1, E:2 * E], ones[:, :], mask[:, 0, :], start=True, stop=False)
            pe.matmul(bank[:, 1, E:2 * E], tri_excl[:, :], mask[:, 1, :], start=False, stop=True).then_inc(pos_done, 1)
            pe.wait_ge(over_masked, 1)
            for tb in range(TB):
                last = pe.matmul(bank[0:N96, 3, 0:1], mask96[:, tb, :], ones[:, 0:1], start=(tb == 0), stop=(tb == TB - 1))
            last.then_inc(over_counted, 1)
            pe.wait_ge(comb_done, 2)
            for tb in range(TB):
                last = T(bank[0:E, 2, tb * P:(tb + 1) * P], comb[:, tb, 0:E])
            last.then_inc(combT_done, 1)

            pe.wait_ge(over_flagged, 1)
            pe.matmul(bank[0:N96, 3, 32:33], tri_incl[0:N96, 0:N96], flag96[:, :], start=True, stop=True)
            pe.matmul(bank[0:1, 3, 64:65], flag96[:, :], ones[0:N96, 0:1], start=True, stop=True).then_inc(over_ranked, 1)
            pe.wait_ge(over_tabled, 2)
            for i in range(2 * TB):
                last = T(bank[0:N96, 4, i * P:(i + 1) * P], pc96[:, i, :])
            last.then_inc(over_turned, 1)

            def gather(g, pieces):
                for b in pieces:
                    if b == 0:
                        pe.wait_ge(sel_ready, g + 1)
                    if b >= 2:
                        pe.wait_ge(pair_copied, g * 4 + (b - 1))
                    for c in range(4 * b, 4 * b + 4):
                        for tb in range(TB):
                            last = pe.matmul(bank[:, 6 + b % 2, (c % 4) * P:(c % 4 + 1) * P], h2[:, tb, c * P:(c + 1) * P],
                                             sel[:, tb, :], start=(tb == 0), stop=(tb == TB - 1))
                    last.then_inc(gathered, 1)

            gather(0, range(4))
            pe.wait_ge(over_placed, 1)
            pe.wait_ge(over_copied, 1)
            pe.matmul(bank[0:1, 5, 4 * EXTRA:5 * EXTRA], expert96[:, :], place96[:, :], start=True, stop=True)
            for i in range(2 * TB):
                last = pe.matmul(bank[:, 5, i * EXTRA:(i + 1) * EXTRA], pc96T[:, i * P:(i + 1) * P], place96[:, :],
                                 start=True, stop=True)
            last.then_inc(over_spread, 1)
            def gate_and_up(X, i):
                if i == 0:
                    pe.wait_ge(hsel_lo, X * 2 + 1)
                if i == GU // 2:
                    pe.wait_ge(hsel_lo, X * 2 + 2)
                pe.wait_ge(lo_ready, X * GU + (i + 1))
                for kk in range(KPU):
                    for part in (hi[i % HI_SLOTS], lo[i % LO_SLOTS]):
                        last = pe.matmul(bank[:, i % 2, :], hsel[:, (i // 2) * KPU + kk, :], part[:, kk, :],
                                         start=(i < 2 and kk == 0 and part is hi[i % HI_SLOTS]),
                                         stop=(i >= GU - 2 and kk == KPU - 1 and part is lo[i % LO_SLOTS]))
                last.then_inc(unit_used, 1)

            def turn_gate_up(X):
                pe.wait_ge(gu_copied, X * 2 + 2)
                for c in range(2 * FC):
                    last = pe.matmul(bank[:, 6, c * SLOTS:(c + 1) * SLOTS], gu_sb[:, c // FC, (c % FC) * P:(c % FC + 1) * P],
                                     twin[:, :], start=True, stop=True)
                last.then_inc(tsum_done, 1)

            def scatter(q, pieces):
                for i in pieces:
                    tb, n = i // 4, i % 4
                    if i >= 2:
                        pe.wait_ge(scatter_added, q * 8 + (i - 1))
                    pe.matmul(bank[:, 7 if i % 2 == 0 else 6, :], selwT[:, tb * P:(tb + 1) * P],
                              y[:, n * COLS:(n + 1) * COLS], start=True, stop=True).then_inc(scattered, 1)

            def turn_weights(q):
                pe.wait_ge(selw_ready, q + 1)
                for tb in range(TB):
                    last = T(bank[:, 7, tb * P:(tb + 1) * P], selw[:, tb, :])
                last.then_inc(selwT_done, 1)

            def down(X, q, off, c):
                if c == 0:
                    pe.wait_ge(act_ready, X)
                    pe.wait_ge(y_filled, X * 4)
                s = off % EXP_SLOTS
                pe.wait_ge(landed[s], (q * 3 + (off // EXP_SLOTS + EXP_FILLS[s] + 1)) * 16)
                for n in range(4):
                    last = pe.matmul(bank[0:SLOTS, 2 + n, :], act[:, c * SLOTS:(c + 1) * SLOTS],
                                     raw[s][:, n, :], start=(c == 0), stop=(c == FC - 1))
                last.then_inc(down_used, 1)

            def turn(X, q, m, plan):
                offs = [TURN * (m + 1) + place_of(plan, (-1, c)) for c in range(FC)]
                gate_and_up(X, 0)
                if m == 0:
                    pe.wait_ge(pair_copied, q * 4 + 8)
                else:
                    pe.wait_ge(scatter_added, q * 8 + 8)
                turn_gate_up(X - 1)
                for i in range(1, 4):
                    gate_and_up(X, i)
                if m == 0:
                    pe.wait_ge(y_filled, X * 4)
                    pe.wait_ge(selwT_filled, q + 1)
                    scatter(q, [0])
                    pe.wait_ge(biased, X)
                    scatter(q, [1])
                else:
                    pe.wait_ge(hsel_lo, X * 2 + 2)
                    pe.wait_ge(biased, X)
                    gather(q + 2, [0, 1])
                down(X, q, offs[0], 0)
                if m == 0:
                    scatter(q, [2, 3])
                else:
                    gather(q + 2, [2, 3])
                gate_and_up(X, 4)
                down(X, q, offs[1], 1)
                if m == 0:
                    scatter(q, [4, 5])
                gate_and_up(X, 5)
                gate_and_up(X, 6)
                if m == 0:
                    scatter(q, [6, 7])
                else:
                    pe.wait_ge(pair_copied, q * 4 + 12)
                    turn_weights(q)
                down(X, q, offs[2], 2)
                gate_and_up(X, 7)
                down(X, q, offs[3], 3)

            pe.sem_inc(down_used, FC)
            pe.wait_ge(tables_done, 1)
            pe.wait_ge(combT_copied, 1)
            pe.wait_ge(row_in["bdown"], 16)
            for i in range(GU):
                tb, n = i // 4, i % 4
                gate_and_up(0, i)
                if i >= 2:
                    pe.wait_ge(bias_copied, i - 1)
                pe.matmul(bank[:, 4 + i % 2, :], combT[:, tb * P:(tb + 1) * P],
                          bdown[:, n * COLS:(n + 1) * COLS], start=True, stop=True).then_inc(bias_done, 1)
                if i == GU // 2 - 1:
                    pe.wait_ge(hsel_lo, 2)
                if i >= GU // 2 - 1 and i < GU - 1:
                    gather(1, [i - (GU // 2 - 1)])
            pe.wait_ge(bias_copied, GU)
            turns = pe.value_load(turns_i[0:1, 0:1], min_val=PAIRS - 1, max_val=PAIRS - 1 + EXTRA // 2)
            with pe.Fori(0, turns) as q:
                for m in range(2):
                    turn(q * 2 + (m + 1), q, m, PLAN)
            last_task = turns * 2 + 1
            turn(last_task, turns, 0, LAST_PLAN)
            pe.wait_ge(scatter_added, turns * 8 + 8)
            turn_gate_up(last_task)
            turn_weights(turns)
            for c in range(FC):
                down(last_task + 1, turns, TURN + TAIL_DOWN[c], c)
            pe.wait_ge(y_filled, last_task * 4 + 8)
            pe.wait_ge(selwT_filled, turns + 2)
            pe.wait_ge(biased, last_task + 1)
            scatter(turns + 1, range(8))

        @block.scalar
        def _(act_):
            def copy(dst, src, **k):
                return act_.activation(dst, src, ACT.Copy, **k)

            act_.dma_start(c_rows[:, :], A["c"][0, :].rearrange("(k p) -> k p", p=P)).then_inc(c_loaded, 16)
            for dst, src in ((bada_rows[:, :], A["b_ada"][0, 0:2 * D].rearrange("(k p) -> k p", p=P)),
                             (bs_rows[:, :], A["spatial_b"][0]),
                             (bg_rows[:, :], A["b_gate"][0].rearrange("e (c p) -> (e c) p", p=P)),
                             (bu_rows[:, :], A["b_up"][0].rearrange("e (c p) -> (e c) p", p=P)),
                             (ws_raw[:, :, :], A["spatial_w"][0].rearrange("g t s -> t g s")),
                             (bf_row[:, :], A["b_f"][0:1, :]),
                             (bada2[:, :], A["b_ada"][0, 2 * D:6 * D].rearrange("(k p) -> k p", p=P))):
                act_.dma_start(dst, src).then_inc(rows_loaded, 16)
            act_.dma_start(x[:, :, :], A["x"][0].rearrange("(t p) d -> p t d", p=P)).then_inc(x_loaded, 16)
            act_.dma_start(lng, A["sgu_ln_g"][0].rearrange("g c -> (g c)").partition_broadcast(P)).then_inc(row_lng, 16)
            act_.dma_start(wf[:, :, :], A["w_in"][0, :, F_COL:F_COL + HEADS].rearrange("(k p) f -> p k f", p=P)).then_inc(wf_loaded, 16)

            act_.wait_ge(cT_done, 1)
            copy(cT[:, 0, :], bank[:, 0, 0:KD]).then_inc(sig_c, 1)
            act_.activation(cT[:, 1, :], bank[:, 0, 0:KD], ACT.Sigmoid).then_inc(sig_c, 1)
            act_.wait_ge(rowsT_done, 1)
            copy(wsT[:, 0:4, :], bank[:, 2, :]).then_inc(rowsT_copied, 1)
            copy(wsT[:, 4:8, :], bank[:, 3, :]).then_inc(rowsT_copied, 1)
            copy(badaT[:, :], bank[:, 1, 0:2 * KD])
            copy(bsT[:, :], bank[:, 1, 32:32 + HEADS])
            copy(bgu[:, :, 0:FC], bank[:, 1, P:2 * P].rearrange("p (e c) -> p e c", e=E))
            copy(bgu[:, :, FC:2 * FC], bank[:, 1, 2 * P:3 * P].rearrange("p (e c) -> p e c", e=E)).then_inc(rowsT_copied, 1)
            for b in range(8):
                act_.wait_ge(xT_done, b + 1)
                copy(hT[:, 2 * b:2 * b + 2, :], bank[:, (4 + b) % 8, :]).then_inc(xT_copied, 1)

            def z_out(G, parity, dst, func):
                act_.wait_ge(main_used, G * 4 + 4)
                for tb in range(TB):
                    act_.activation(dst(tb), bank[:, 2 * parity + tb, :], func).then_inc(z_copied, 1)

            def zA_cols(G):
                return lambda tb: zA[:, tb, bass.ds(G * COLS, COLS)]

            with act_.Fori(0, 2) as i:
                for parity in range(2):
                    G = i * 2 + parity
                    z_out(G, parity, zA_cols(G), ACT.Gelu_apprx_tanh)
            for G in range(4, 6):
                z_out(G, G % 2, zA_cols(G), ACT.Copy)
            act_.wait_ge(v_var, 1)
            act_.activation(rstd[:, :], mv[:, :, 1], ACT.Sqrt).then_inc(v_std, 1)
            with act_.Fori(3, 5) as i:
                for parity in range(2):
                    G = i * 2 + parity
                    z_out(G, parity, zA_cols(G), ACT.Copy)

            act_.wait_ge(f_done, 1)
            act_.activation(lt[:, :], bank[:, 4, 0:2 * HEADS], ACT.Abs).then_inc(act_step, 1)
            act_.wait_ge(act_step, 1)
            act_.activation(lt[:, :], lt[:, :], ACT.Exp, scale=-1.0).then_inc(act_step, 1)
            act_.wait_ge(act_step, 2)
            act_.activation(lt[:, :], lt[:, :], ACT.Ln, bias=1.0).then_inc(lt_done, 1)

            def gate_out(G):
                z_out(G, G % 2, lambda tb: zG[:, tb, (G - GA) * COLS:(G - GA + 1) * COLS], ACT.Sigmoid)

            def qkT_out(half):
                for h in range(4 * half, 4 * half + 4):
                    act_.wait_ge(qkT_done, h + 1)
                    copy(zA[:, 0:TB, Q_ + h * P:Q_ + (h + 1) * P], bank[:, 4 + h % 4, 0:SEQ].rearrange("p (t c) -> p t c", t=TB),
                         scale=SCALE).then_inc(qkT_copied, 1)
                    copy(zA[:, 0:TB, K_ + h * P:K_ + (h + 1) * P], bank[:, 4 + h % 4, SEQ:2 * SEQ].rearrange("p (t c) -> p t c", t=TB)
                         ).then_inc(qkT_copied, 1)

            def cum_out():
                act_.wait_ge(cum_done, 1)
                copy(cum[:, :], bank[:, 4, 0:2 * HEADS]).then_inc(cum_copied, 1)
                copy(cumT[:, :], bank[0:HEADS, 5, 0:SEQ], scale=-1.0).then_inc(cum_copied, 1)

            def exps(half):
                act_.wait_ge(max_done, half + 1)
                for hh in range(4):
                    act_.activation(probs[:, hh, 0:P], probs[:, hh, 0:P], ACT.Exp, bias=mx[:, 1, 2 * hh:2 * hh + 1],
                                    accum_out=sums[:, 2 * hh:2 * hh + 1]).then_inc(exp_done, 1)
                    act_.activation(probs[:, hh, P:3 * P], probs[:, hh, P:3 * P], ACT.Exp, bias=mx[:, 1, 2 * hh + 1:2 * hh + 2],
                                    accum_out=sums[:, 2 * hh + 1:2 * hh + 2]).then_inc(exp_done, 1)

            def pT_out(half):
                for hh in range(4):
                    act_.wait_ge(pT_done, 4 * half + hh + 1)
                    copy(probsT[:, hh, :], bank[:, 4 + hh, 0:3 * P]).then_inc(pT_copied, 1)

            def oT_out(half):
                for h in range(4 * half, 4 * half + 4):
                    act_.wait_ge(oT_done, h + 1)
                    copy(zA[:, 0:TB, Q_ + h * P:Q_ + (h + 1) * P],
                         bank[:, 4 + h % 4, 0:SEQ].rearrange("p (t c) -> p t c", t=TB)).then_inc(oT_copied, 1)

            def yaT_out():
                for b in range(4):
                    act_.wait_ge(yaT_done, b + 1)
                    copy(zA[:, 0:TB, V_ + 2 * b * P:V_ + 2 * (b + 1) * P],
                         bank[:, b, :].rearrange("p (t c) -> p t c", t=TB)).then_inc(yaT_copied, 1)

            gate_out(10)
            qkT_out(0)
            gate_out(11)
            qkT_out(1)
            gate_out(12)
            gate_out(13)
            cum_out()
            gate_out(14)
            exps(0)
            gate_out(15)
            pT_out(0)
            gate_out(16)
            oT_out(0)
            exps(1)
            gate_out(17)
            pT_out(1)
            yaT_out()
            oT_out(1)
            act_.wait_ge(cols2_done, 1)
            copy(modcol[:, :], bank[:, 7, 0:4 * KD]).then_inc(cols2_copied, 1)
            for n in range(NPROJ):
                for b in range(2):
                    act_.wait_ge(mT_done, 2 * n + b + 1)
                    copy(hT[:, 4 * n + 2 * b:4 * n + 2 * b + 2, :], bank[:, 4 * (n % 2) + b, :]).then_inc(mT_copied, 1)
            for tb in range(TB):
                act_.wait_ge(var1, tb + 1)
                act_.activation(rstd[:, tb:tb + 1], mv[:, tb, 1:2], ACT.Sqrt).then_inc(std1, 1)
            for tb in range(TB):
                for b in range(4):
                    act_.wait_ge(h2T_done, 4 * tb + b + 1)
                    copy(h2T[:, 4 * b:4 * b + 4, tb * P:(tb + 1) * P],
                         bank[:, 4 * tb + b, :].rearrange("p (k c) -> p k c", k=4)).then_inc(h2T_copied, 1)

            def hi_part(X, i, off, q=0):
                s = off % EXP_SLOTS
                act_.wait_ge(landed[s], (q * 3 + (off // EXP_SLOTS + EXP_FILLS[s] + 1)) * 16)
                if not (isinstance(X, int) and X == 0 and i < HI_SLOTS):
                    act_.wait_ge(unit_used, X * GU + (i + 1 - HI_SLOTS))
                copy(hi[i % HI_SLOTS][:, :, :], raw[s][:, :, :]).then_inc(hi_ready, 1)

            act_.wait_ge(h2_done, 2)
            for i in range(3):
                hi_part(0, i, i)
            for tb in range(TB):
                act_.wait_ge(top_done, tb + 1)
                act_.activation(topw[:, tb, 0:TOPK], top[:, tb, 0:TOPK], ACT.Exp, bias=tops[:, tb:tb + 1],
                                accum_out=tops[:, 2 + tb:3 + tb]).then_inc(topw_done, 1)
            act_.wait_ge(combT_done, 1)
            copy(combT[:, :], bank[0:E, 2, 0:SEQ]).then_inc(combT_copied, 1)

            def pair_out(g, pieces=range(4)):
                for b in pieces:
                    act_.wait_ge(gathered, g * 4 + (b + 1))
                    copy(pair[:, 4 * b:4 * b + 4, :], bank[:, 6 + b % 2, :]).then_inc(pair_copied, 1)

            def tokens_hi(g, half):
                act_.wait_ge(pair_copied, g * 4 + 4)
                for b in range(2):
                    copy(hsel[:, 8 * b:8 * b + 8, 0:SLOTS], pair[:, 8 * b:8 * b + 8, half * SLOTS:(half + 1) * SLOTS]
                         ).then_inc(hsel_hi, 1)

            def rows_of(X, i):
                act_.wait_ge(unit_used, X * GU + (GU - 1 + i))
                copy(gu_sb[:, i, :], bank[:, i, :]).then_inc(gu_copied, 1)

            def sigmoid(X):
                act_.wait_ge(gate_ready, X + 1)
                act_.activation(act[:, :], gate_up_T[:, 0:FC * SLOTS], ACT.Sigmoid, scale=SWI).then_inc(sig_ready, 1)

            def weights_out(q):
                act_.wait_ge(selwT_done, q + 1)
                copy(selwT[:, :], bank[:, 7, 0:SEQ]).then_inc(selwT_filled, 1)

            def rows_down(X, half):
                act_.wait_ge(down_used, X * FC + FC)
                for n in range(4):
                    copy(y[half * SLOTS:(half + 1) * SLOTS, n * COLS:(n + 1) * COLS],
                         bank[0:SLOTS, 2 + n, :]).then_inc(y_filled, 1)

            def turn(X, q, m, plan, last=False):
                def own(i):
                    hi_part(X, i, TURN * (m + 1) + place_of(plan, (0, i)), q)

                def ahead(i):
                    if not last:
                        hi_part(X + 1, i, TURN * (m + 1) + place_of(plan, (1, i)), q)

                own(4)
                sigmoid(X - 1)
                own(5)
                own(6)
                if m == 1:
                    pair_out(q + 2, [0, 1])
                own(7)
                if m == 1:
                    pair_out(q + 2, [2, 3])
                ahead(0)
                ahead(1)
                ahead(2)
                if m == 1:
                    weights_out(q)
                act_.wait_ge(act_ready, X)
                rows_of(X, 0)
                rows_of(X, 1)
                if not last:
                    tokens_hi(q + 1 if m == 0 else q + 2, 1 - m)
                ahead(3)
                rows_down(X, m)

            act_.wait_ge(x1_done, TB)
            act_.wait_ge(x1_stored, 16)
            pair_out(0)
            tokens_hi(0, 0)
            for i in range(HI_SLOTS - 1, GU):
                hi_part(0, i, i)
            hi_part(1, 0, GU)
            pair_out(1, [0])
            hi_part(1, 1, GU + 1)
            pair_out(1, [1])
            hi_part(1, 2, GU + 2)
            pair_out(1, [2, 3])
            rows_of(0, 0)
            rows_of(0, 1)
            tokens_hi(1, 0)
            hi_part(1, 3, GU + 3)
            act_.activation(warm[:, :], ones[:, 0:1], ACT.Sigmoid)
            act_.wait_ge(tables_done, 1)
            turns = act_.value_load(turns_i[0:1, 0:1], min_val=PAIRS - 1, max_val=PAIRS - 1 + EXTRA // 2)
            with act_.Fori(0, turns) as q:
                for m in range(2):
                    turn(q * 2 + (m + 1), q, m, PLAN)
            last_task = turns * 2 + 1
            turn(last_task, turns, 0, LAST_PLAN, last=True)
            sigmoid(last_task)
            weights_out(turns)
            rows_down(last_task + 1, 1)
            for tb in range(TB):
                act_.wait_ge(var2, tb + 1)
                act_.activation(rstd[:, tb:tb + 1], mv[:, tb, 1:2], ACT.Sqrt).then_inc(std2, 1)

        @block.vector
        def _(dve):
            steps = [0]

            def chain(ins):
                steps[0] += 1
                ins.then_inc(dve_step, 1)
                dve.wait_ge(dve_step, steps[0])

            dve.wait_ge(sig_c, 2)
            chain(dve.tensor_tensor(condT[:, :], cT[:, 0, :], cT[:, 1, :], ALU.mult))
            dve.wait_ge(acc1_zeroed, 1)

            def add_unit(dst, slot, k, done):
                return dve.scalar_tensor_tensor(out=dst, in0=flat(slot), scalar=condT[:, k], in1=dst,
                                                op0=ALU.mult, op1=ALU.add).then_inc(done, 1)

            def ada1(i, m):
                n = i * RAW_SLOTS + m
                if not (isinstance(n, int) and n < 2):
                    dve.wait_ge(ada1_done, n - 1)
                dve.wait_ge(landed[m], (i + 1) * 16)
                add_unit(acc1[:, m % 2, :], raw[m], bass.ds(i * 3 + m // 2, 1), ada1_done)

            for m in range(RAW_SLOTS):
                ada1(0, m)
            with dve.Fori(1, NADA1 // RAW_SLOTS) as i:
                for m in range(RAW_SLOTS):
                    ada1(i, m)
            for m in range(2):
                ada1(NADA1 // RAW_SLOTS, m)
            dve.wait_ge(ada1_cols, 1)
            dve.wait_ge(rowsT_copied, 3)
            dve.tensor_tensor(mod1[:, 0:KD], bank[:, 0, 0:KD], badaT[:, 0:KD], ALU.add).then_inc(mod1_done, 1)
            dve.scalar_tensor_tensor(out=mod1[:, KD:2 * KD], in0=bank[:, 0, KD:2 * KD], scalar=1.0, in1=badaT[:, KD:2 * KD],
                                     op0=ALU.add, op1=ALU.add).then_inc(mod1_done, 1)
            dve.wait_ge(mod1_done, 2)
            dve.wait_ge(xT_copied, 8)
            for k in range(KD):
                dve.tensor_scalar(hT[:, k, :], hT[:, k, :], mod1[:, KD + k:KD + k + 1], mod1[:, k:k + 1],
                                  ALU.mult, ALU.add).then_inc(h_done, 1)

            def ada2(k):
                for j in range(4):
                    if not (isinstance(k, int) and k == 0):
                        dve.wait_ge(ada2_done, k * 4 + j - 3)
                    dve.wait_ge(landed[j % 2], (k * 2 + j // 2 + ADA_FILLS + 1) * 16)
                    add_unit(acc[:, j, :], raw[j % 2], bass.ds(k, 1), ada2_done)

            dve.wait_ge(acc_zeroed, 4)
            ada2(0)
            with dve.Fori(1, 5) as k:
                ada2(k)

            dve.wait_ge(z_copied, 8)
            for tb in range(TB):
                for g in range(HEADS):
                    dve.bn_stats(st[:, tb * HEADS + g, :], zA[:, tb, V_ + g * P:V_ + (g + 1) * P]).then_inc(v_stat, 1)
            for i in range(TB * HEADS):
                dve.wait_ge(v_stat, i + 1)
                dve.bn_aggr(mv[:, i, :], st[:, i, :]).then_inc(v_agg, 1)
            dve.wait_ge(v_agg, TB * HEADS)
            dve.tensor_scalar(mv[:, :, 1], mv[:, :, 1], EPS, None, ALU.add).then_inc(v_var, 1)
            with dve.Fori(5, 8) as k:
                ada2(k)
            dve.wait_ge(v_std, 1)
            chain(dve.reciprocal(rstd[:, :], rstd[:, :]))
            for tb in range(TB):
                for g in range(HEADS):
                    v = zA[:, tb, V_ + g * P:V_ + (g + 1) * P]
                    i = tb * HEADS + g
                    ins = dve.tensor_scalar(v, v, mv[:, i, 0:1], rstd[:, i:i + 1], ALU.subtract, ALU.mult)
                ins.then_inc(vn_done, 1)
            for tb in range(TB):
                if tb == 0:
                    dve.wait_ge(row_lng, 16)
                dve.wait_ge(vn_done, TB)
                v = zA[:, tb, V_:V_ + AW]
                dve.tensor_tensor(v, v, lng, ALU.mult).then_inc(vn_done, 1)
            with dve.Fori(8, 10) as k:
                ada2(k)

            dve.wait_ge(lt_done, 1)
            chain(dve.tensor_scalar(lf[:, :], bank[:, 4, 0:2 * HEADS], 0.0, None, ALU.min))
            dve.tensor_tensor(lf[:, :], lf[:, :], lt[:, :], ALU.subtract).then_inc(lf_done, 2)

            def gate_u():
                for g in range(HEADS):
                    dve.wait_ge(sgu_done, g + 1 if g % 2 else g + 2)
                    u = zA[:, 0:TB, U_ + g * P:U_ + (g + 1) * P]
                    dve.scalar_tensor_tensor(out=u, in0=bank[:, 4 + g // 2, (g % 2) * SEQ:(g % 2 + 1) * SEQ].rearrange("p (t c) -> p t c", t=TB),
                                             scalar=bsT[:, g:g + 1], in1=u, op0=ALU.add, op1=ALU.mult).then_inc(ya_done, 1)

            def maxima(half):
                if half:
                    dve.wait_ge(pT_done, 4)
                for hh in range(4):
                    h = 4 * half + hh
                    dve.wait_ge(scores_done, h + 1)
                    dve.scalar_tensor_tensor(out=probs[:, hh, 0:P], in0=bank[:, 4 + hh, 0:P], scalar=cum[:, h:h + 1],
                                             in1=mask3[:, 0, :], op0=ALU.add, op1=ALU.add).then_inc(scored, 1)
                    dve.scalar_tensor_tensor(out=probs[:, hh, P:3 * P], in0=bank[:, 4 + hh, P:3 * P], scalar=cum[:, HEADS + h:HEADS + h + 1],
                                             in1=mask3[:, 1:3, :].rearrange("p b c -> p (b c)"), op0=ALU.add, op1=ALU.add).then_inc(scored, 1)
                for hh in range(4):
                    dve.wait_ge(scored, 8 * half + 2 * hh + 2)
                    dve.tensor_reduce(mx[:, 0, 2 * hh:2 * hh + 1], probs[:, hh, 0:P], AX.X, ALU.max).then_inc(scored_max, 1)
                    dve.tensor_reduce(mx[:, 0, 2 * hh + 1:2 * hh + 2], probs[:, hh, P:3 * P], AX.X, ALU.max).then_inc(scored_max, 1)
                dve.wait_ge(scored_max, 8 * half + 8)
                dve.tensor_scalar(mx[:, 1, :], mx[:, 0, :], -1.0, None, ALU.mult).then_inc(max_done, 1)

            def normalise(half):
                dve.wait_ge(exp_done, 8 * (half + 1))
                chain(dve.reciprocal(sums[:, :], sums[:, :]))
                for hh in range(4):
                    dve.tensor_scalar(probs[:, hh, 0:P], probs[:, hh, 0:P], sums[:, 2 * hh:2 * hh + 1], None, ALU.mult)
                    dve.tensor_scalar(probs[:, hh, P:3 * P], probs[:, hh, P:3 * P], sums[:, 2 * hh + 1:2 * hh + 2], None,
                                      ALU.mult).then_inc(probs_done, 1)

            ada2(10)
            ada2(11)
            ada2(12)
            gate_u()
            ada2(13)
            ada2(14)
            dve.wait_ge(cum_copied, 2)
            maxima(0)
            ada2(15)
            normalise(0)
            maxima(1)
            normalise(1)

            dve.wait_ge(modT_done, 1)
            dve.tensor_tensor(modrow[:, :], bank[0:4 * KD, 6, 0:P], bada2[:, :], ALU.add).then_inc(modrow_done, 1)

            for n in range(NPROJ):
                dve.wait_ge(main_used, 4 * (GM + n + 1))
                for tb in range(TB):
                    ga = zG[:, tb, n * COLS:(n + 1) * COLS]
                    gb = zG[:, tb, D + n * COLS:D + (n + 1) * COLS]
                    dve.tensor_tensor(ga, bank[:, 4 * (n % 2) + tb, :], ga, ALU.mult).then_inc(gated, 1)
                    dve.tensor_tensor(gb, bank[:, 4 * (n % 2) + 2 + tb, :], gb, ALU.mult).then_inc(gated, 1)
                for tb in range(TB):
                    ga = zG[:, tb, n * COLS:(n + 1) * COLS]
                    gb = zG[:, tb, D + n * COLS:D + (n + 1) * COLS]
                    dve.wait_ge(gated, 4 * n + 2 * tb + 2)
                    dve.tensor_tensor(ga, ga, gb, ALU.add).then_inc(merged_done, 1)

            dve.wait_ge(row_in["g1"], 16)
            for n in range(NPROJ):
                dve.wait_ge(main_used, 4 * (GM + NPROJ + n + 1))
                for tb in range(TB):
                    t = zG[:, tb, D + n * COLS:D + (n + 1) * COLS]
                    cols = slice(n * COLS, (n + 1) * COLS)
                    chain(dve.scalar_tensor_tensor(out=t, in0=g1_row[:, cols], scalar=1.0, in1=bank[:, 2 * (n % 2) + tb, :],
                                                   op0=ALU.add, op1=ALU.mult))
                    dve.scalar_tensor_tensor(out=x[:, tb, cols], in0=x[:, tb, cols], scalar=ALPHA, in1=t,
                                             op0=ALU.mult, op1=ALU.add).then_inc(res_done, 1)
                if n == 0:
                    for name in ("ln1g", "sc2", "sh2", "ln1b"):
                        dve.wait_ge(row_in[name], 16)
                    dve.wait_ge(cols2_done, 1)
                    chain(dve.scalar_tensor_tensor(out=h2[:, 0, :], in0=sc2_row[:, :], scalar=1.0, in1=ln1b[:, :],
                                                   op0=ALU.add, op1=ALU.mult))
                    chain(dve.tensor_tensor(sh2_row[:, :], sh2_row[:, :], h2[:, 0, :], ALU.add))
                    chain(dve.scalar_tensor_tensor(out=sc2_row[:, :], in0=sc2_row[:, :], scalar=1.0, in1=ln1g[:, :],
                                                   op0=ALU.add, op1=ALU.mult))
                if n < NPROJ - 1:
                    for tb in range(TB):
                        dve.wait_ge(res_done, 2 * n + tb + 1)
                        chain(dve.bn_stats(st[:, 4 * tb + n, :], x[:, tb, cols]))

            def norm_stats(t, tb, var, pieces=range(4)):
                for i in pieces:
                    ins = dve.bn_stats(st[:, 4 * tb + i, :], t[:, tb, i * COLS:(i + 1) * COLS])
                chain(ins)
                chain(dve.bn_aggr(mv[:, tb, :], st[:, 4 * tb:4 * tb + 4, :].rearrange("p a b -> p (a b)")))
                dve.tensor_scalar(mv[:, tb, 1:2], mv[:, tb, 1:2], EPS, None, ALU.add).then_inc(var, 1)

            def normalise_rows(t, tb, std):
                dve.wait_ge(std, tb + 1)
                row = t[:, tb, :]
                chain(dve.reciprocal(rstd[:, tb:tb + 1], rstd[:, tb:tb + 1]))
                chain(dve.tensor_scalar(row, row, mv[:, tb, 0:1], rstd[:, tb:tb + 1], ALU.subtract, ALU.mult))

            def gain_and_shift(dst, row, gain, shift):
                chain(dve.tensor_tensor(dst, row, gain[:, :], ALU.mult))
                return dve.tensor_tensor(dst, dst, shift[:, :], ALU.add)

            dve.wait_ge(res_done, 2 * NPROJ)
            for tb in range(TB):
                norm_stats(x, tb, var1, [NPROJ - 1])
            for tb in range(TB):
                normalise_rows(x, tb, std1)
                gain_and_shift(h2[:, tb, :], x[:, tb, :], sc2_row, sh2_row).then_inc(h2_done, 1)

            for tb in range(TB):
                dve.wait_ge(logit_done, tb + 1)
                chain(dve.tensor_copy(logit[:, tb, :], bank[:, tb, 0:E]))
                chain(dve.max(top[:, tb, :], logit[:, tb, :]))
                chain(dve.max_index(topi[:, tb, :], top[:, tb, :], logit[:, tb, :]))
                chain(dve.tensor_copy(topf[:, tb, :], topi[:, tb, :]))
                dve.tensor_scalar(tops[:, tb:tb + 1], top[:, tb, 0:1], -1.0, None, ALU.mult).then_inc(top_done, 1)
                dve.wait_ge(topw_done, tb + 1)
                chain(dve.reciprocal(tops[:, 2 + tb:3 + tb], tops[:, 2 + tb:3 + tb]))
                chain(dve.tensor_scalar(topw[:, tb, 0:TOPK], topw[:, tb, 0:TOPK], tops[:, 2 + tb:3 + tb], None, ALU.mult))
                for i in range(TOPK):
                    hot = expert_id[:, :], topf[:, tb, i:i + 1]
                    if i == 0:
                        chain(dve.tensor_scalar(mask[:, tb, :], *hot, None, ALU.is_equal))
                        chain(dve.tensor_scalar(comb[:, tb, 0:E], *hot, topw[:, tb, 0:1], ALU.is_equal, ALU.mult))
                    else:
                        chain(dve.tensor_scalar(onehot[:, :], *hot, None, ALU.is_equal))
                        chain(dve.tensor_tensor(mask[:, tb, :], mask[:, tb, :], onehot[:, :], ALU.add))
                        chain(dve.scalar_tensor_tensor(out=comb[:, tb, 0:E], in0=onehot[:, :], scalar=topw[:, tb, i:i + 1],
                                                       in1=comb[:, tb, 0:E], op0=ALU.mult, op1=ALU.add))
                dve.sem_inc(mask_done, 1)
                dve.sem_inc(comb_done, 1)

            def select(X):
                for j in range(2):
                    for tb in range(TB):
                        ins = dve.tensor_scalar(sel[:, tb, j * SLOTS:(j + 1) * SLOTS], slot_id[:, :],
                                                pos1[:, tb, bass.ds(X + j, 1)], None, ALU.is_equal)
                ins.then_inc(sel_ready, 1)

            def lo_part(X, i, off):
                dve.wait_ge(hi_ready, X * GU + (i + 1))
                dve.tensor_tensor(lo[i % LO_SLOTS][:, :, :], raw[off % EXP_SLOTS][:, :, :], hi[i % HI_SLOTS][:, :, :].bitcast(F32),
                                  ALU.subtract).then_inc(lo_ready, 1)

            def thrice(t):
                return t.unsqueeze(1).to_broadcast([P, OVER, E])

            for tb in range(TB):
                ins = dve.tensor_copy(mask96[:, tb, :].rearrange("p (b e) -> p b e", b=OVER), thrice(mask[:, tb, :]))
            ins.then_inc(over_masked, 1)
            for tb in range(TB):
                ins = dve.tensor_copy(pc96[:, TB + tb, :].rearrange("p (b e) -> p b e", b=OVER), thrice(comb[:, tb, 0:E]))
            ins.then_inc(over_tabled, 1)
            dve.wait_ge(pos_done, 1)
            chain(dve.scalar_tensor_tensor(out=pos1[:, :, 0:E], in0=bank[:, 1, 0:2 * E].rearrange("p (t e) -> p t e", t=TB),
                                           scalar=1.0, in1=mask[:, :, :], op0=ALU.add, op1=ALU.mult))
            dve.wait_ge(consts_made, NCONST)
            select(0)
            for b in range(OVER):
                ins = dve.tensor_scalar(pc96[:, 0:TB, b * E:(b + 1) * E], pos1[:, :, 0:E], -float((b + 1) * SLOTS), None, ALU.add)
            ins.then_inc(over_tabled, 1)
            dve.wait_ge(over_counted, 1)
            dve.tensor_scalar(flag96[:, :], bank[0:N96, 3, 0:1], least96[:, :], None, ALU.is_gt).then_inc(over_flagged, 1)
            dve.wait_ge(over_turned, 1)
            dve.tensor_copy(pc96T[:, :], bank[0:N96, 4, :]).then_inc(over_copied, 1)
            dve.wait_ge(over_ranked, 1)
            chain(dve.tensor_copy(rank96[:, :], bank[0:N96, 3, 32:33]))
            dve.tensor_scalar(place96[:, :], slot_id[0:N96, 0:EXTRA], rank96[:, :], flag96[:, :], ALU.is_equal, ALU.mult
                              ).then_inc(over_placed, 1)
            chain(dve.tensor_copy(n_over[:, :], bank[0:1, 3, 64:65]))
            chain(dve.tensor_scalar(halves[:, :], slot_id[0:1, 0:EXTRA:2], n_over[:, :], None, ALU.is_le))
            chain(dve.tensor_reduce(turns_f[:, :], halves[:, :], AX.X, ALU.add))
            dve.tensor_scalar(turns_i[:, :], turns_f[:, :], float(PAIRS - 1), None, ALU.add)
            dve.tensor_copy(task_i[:, 0:E], expert_id[0:1, :])
            lo_part(0, 0, 0)
            gain_and_shift(x[:, 0, :], x[:, 0, :], ln1g, ln1b).then_inc(x1_done, 1)
            lo_part(0, 1, 1)
            lo_part(0, 2, 2)
            gain_and_shift(x[:, 1, :], x[:, 1, :], ln1g, ln1b).then_inc(x1_done, 1)
            dve.wait_ge(over_spread, 1)
            dve.tensor_copy(pos1[:, :, E:E + EXTRA], bank[:, 5, 0:2 * EXTRA].rearrange("p (t j) -> p t j", t=TB))
            dve.memset(pos1[:, :, E + EXTRA:TASKS], 0.0)
            dve.tensor_copy(comb[:, :, E:E + EXTRA], bank[:, 5, 2 * EXTRA:4 * EXTRA].rearrange("p (t j) -> p t j", t=TB))
            dve.tensor_copy(task_i[:, E:E + EXTRA], bank[0:1, 5, 4 * EXTRA:5 * EXTRA]).then_inc(tables_done, 1)

            def select_weighted(X, q):
                dve.wait_ge(selwT_filled, q + 1)
                for j in range(2):
                    for tb in range(TB):
                        ins = dve.tensor_scalar(selw[:, tb, j * SLOTS:(j + 1) * SLOTS], slot_id[:, :], pos1[:, tb, bass.ds(X + j, 1)],
                                                comb[:, tb, bass.ds(X + j, 1)], ALU.is_equal, ALU.mult)
                ins.then_inc(selw_ready, 1)

            def tokens_lo(X, half):
                for b in range(2):
                    dve.wait_ge(hsel_hi, X * 2 + (b + 1))
                    dve.tensor_tensor(hsel[:, 8 * b:8 * b + 8, SLOTS:P], pair[:, 8 * b:8 * b + 8, half * SLOTS:(half + 1) * SLOTS],
                                      hsel[:, 8 * b:8 * b + 8, 0:SLOTS].bitcast(F32), ALU.subtract).then_inc(hsel_lo, 1)

            def add_back(q, pieces=range(8)):
                for i in pieces:
                    tb, n = i // 4, i % 4
                    dve.wait_ge(scattered, q * 8 + (i + 1))
                    o = out_acc[:, tb, n * COLS:(n + 1) * COLS]
                    dve.tensor_tensor(o, o, bank[:, 7 if i % 2 == 0 else 6, :], ALU.add).then_inc(scatter_added, 1)

            def activate(X, e):
                g, u = gate_up_T[:, 0:FC * SLOTS], gate_up_T[:, FC * SLOTS:2 * FC * SLOTS]
                bias = bgu[:, bass.ds(e, 1), :].rearrange("p a c -> p (a c)").unsqueeze(2).to_broadcast([P, 2 * FC, SLOTS])
                dve.wait_ge(tsum_done, X + 1)
                dve.tensor_tensor(gate_up_T.rearrange("p (c s) -> p c s", s=SLOTS),
                                  bank[:, 6, :].rearrange("p (c s) -> p c s", s=SLOTS), bias, ALU.add).then_inc(biased, 1)
                dve.wait_ge(biased, X + 1)
                dve.tensor_scalar(g, g, LIMIT, None, ALU.min).then_inc(gate_ready, 1)
                dve.tensor_scalar(u, u, LIMIT, -LIMIT, ALU.min, ALU.max).then_inc(up_ready, 1)
                dve.wait_ge(gate_ready, X + 1)
                dve.wait_ge(up_ready, X + 1)
                dve.scalar_tensor_tensor(out=u, in0=u, scalar=1.0, in1=g, op0=ALU.add, op1=ALU.mult).then_inc(gate_up, 1)
                dve.wait_ge(sig_ready, X + 1)
                dve.wait_ge(gate_up, X + 1)
                dve.tensor_tensor(act[:, :], u, act[:, :], ALU.mult).then_inc(act_ready, 1)

            def turn(X, q, m, plan, e, last=False):
                def own(i):
                    lo_part(X, i, TURN * (m + 1) + place_of(plan, (0, i)))

                activate(X - 1, e)
                own(4)
                own(5)
                if m == 0:
                    add_back(q, [0, 1])
                if m == 1:
                    select_weighted(X - 2, q)
                own(6)
                if m == 0:
                    add_back(q, [2, 3])
                own(7)
                if m == 0:
                    add_back(q, [4, 5])
                if not last:
                    lo_part(X + 1, 0, TURN * (m + 1) + place_of(plan, (1, 0)))
                if m == 0:
                    add_back(q, [6, 7])
                if m == 0 and not last:
                    dve.wait_ge(gathered, q * 4 + 8)
                    select(X + 2)
                if not last:
                    for i in range(1, 3):
                        lo_part(X + 1, i, TURN * (m + 1) + place_of(plan, (1, i)))
                    tokens_lo(X + 1, 1 - m)
                    lo_part(X + 1, 3, TURN * (m + 1) + place_of(plan, (1, 3)))

            dve.wait_ge(tables_done, 1)
            tokens_lo(0, 0)
            dve.wait_ge(gathered, 4)
            select(1)
            for i in range(GU):
                tb, n = i // 4, i % 4
                lo_part(0, i + 3, i + 3) if i + 3 < GU else lo_part(1, i + 3 - GU, i + 3)
                dve.wait_ge(bias_done, i + 1)
                dve.tensor_copy(out_acc[:, tb, n * COLS:(n + 1) * COLS], bank[:, 4 + i % 2, :]).then_inc(bias_copied, 1)
            tokens_lo(1, 0)
            lo_part(1, 3, GU + 3)
            turns = dve.value_load(turns_i[0:1, 0:1], min_val=PAIRS - 1, max_val=PAIRS - 1 + EXTRA // 2)
            with dve.Fori(0, turns) as q:
                for m in range(2):
                    X = q * 2 + (m + 1)
                    e = dve.value_load(task_i[0:1, bass.ds(X - 1, 1)], min_val=0, max_val=E - 1)
                    turn(X, q, m, PLAN, e)
            last_task = turns * 2 + 1
            e = dve.value_load(task_i[0:1, bass.ds(last_task - 1, 1)], min_val=0, max_val=E - 1)
            turn(last_task, turns, 0, LAST_PLAN, e, last=True)
            select_weighted(last_task - 1, turns)
            e = dve.value_load(task_i[0:1, bass.ds(last_task, 1)], min_val=0, max_val=E - 1)
            activate(last_task, e)
            add_back(turns + 1)
            dve.wait_ge(scatter_added, turns * 8 + 16)

            for name in ("g2", "ln2g", "ln2b"):
                dve.wait_ge(row_in[name], 16)
            for tb in range(TB):
                o = out_acc[:, tb, :]
                chain(dve.scalar_tensor_tensor(out=o, in0=g2_row[:, :], scalar=1.0, in1=o, op0=ALU.add, op1=ALU.mult))
                if tb == 0:
                    dve.wait_ge(x1_loaded, 16)
                chain(dve.scalar_tensor_tensor(out=o, in0=x1_back[:, :] if tb == 0 else x[:, tb, :], scalar=ALPHA, in1=o,
                                               op0=ALU.mult, op1=ALU.add))
                norm_stats(out_acc, tb, var2)
            for tb in range(TB):
                normalise_rows(out_acc, tb, std2)
                gain_and_shift(out_acc[:, tb, :], out_acc[:, tb, :], ln2g, ln2b).then_inc(out_ready, 1)


_INS = ['x', 'c', 'w_ada', 'b_ada', 'w_in', 'b_f', 'sgu_ln_g', 'spatial_w', 'spatial_b', 'w_proj_a', 'w_proj_b', 'w_o',
        'ln1_g', 'ln1_b', 'router_w', 'router_b', 'w_gate', 'b_gate', 'w_up', 'b_up', 'w_down', 'b_down', 'ln2_g', 'ln2_b']


def kernel(**inputs):
    import numpy as np
    import concourse.bacc as bacc
    from concourse.bass_utils import run_bass_kernel_spmd

    nc = bacc.Bacc("TRN2", target_bir_lowering=False, num_devices=1)
    arrays, args = {}, {}
    for name in _INS:
        a = np.ascontiguousarray(inputs[name])
        arrays[f"in_{name}"] = a
        args[name] = nc.dram_tensor(f"in_{name}", a.shape, mybir.dt.from_np(a.dtype), kind="ExternalInput").ap()
    out = nc.dram_tensor("out_0", (1, SEQ, D), F32, kind="ExternalOutput").ap()
    mod_dram = nc.dram_tensor("mod_rows", (4 * KD, P), F32).ap()
    x1_dram = nc.dram_tensor("x1_rows", (P, D), F32).ap()
    layer(nc, args, mod_dram, x1_dram, out)
    r = run_bass_kernel_spmd(nc, [arrays], core_ids=[0])
    return r.results[0]["out_0"]
```
